# Optimizing a Trainium2 kernel written in Bass

```python
import math
import jax, jax.numpy as jnp
from jax import lax
import numpy as np

D_MODEL = 1024
BATCH = 1
SEQ = 1024
DEPTH = 1

POOL_WINDOWS = (2, 4, 8, 16)
POOL_GROUPS = 4
POOL_GROUP_DIM = 128
POOL_WIDTH = POOL_GROUPS * POOL_GROUP_DIM
ATTN_HEADS = 8
ATTN_HEAD_DIM = 128
ATTN_WIDTH = ATTN_HEADS * ATTN_HEAD_DIM
KV_DIM = ATTN_HEAD_DIM
IDX_HEADS = 4
IDX_DIM = 64
TOPK_MAX = 256
Q_BLOCK = 128
N_BUCKETS = 32
MAX_DISTANCE = 128
N_MEM = 256
MEM_HEADS = 4
MEM_HEAD_DIM = 128
MEM_WIDTH = MEM_HEADS * MEM_HEAD_DIM
D_FF = -(-8 * D_MODEL // (3 * 256)) * 256
EPS = 1e-6

IN_SPLITS = (POOL_WIDTH, ATTN_WIDTH, KV_DIM, KV_DIM, IDX_HEADS * IDX_DIM, IDX_DIM, IDX_HEADS, D_MODEL, D_MODEL)
IN_WIDTH = sum(IN_SPLITS)


def _rmsnorm(x, g):
    xf = x.astype(jnp.float32)
    y = xf * lax.rsqrt(jnp.mean(xf * xf, axis=-1, keepdims=True) + EPS)
    return (y * g.astype(jnp.float32)).astype(x.dtype)

def _t5_bucket(dist):
    n = jnp.maximum(dist, 0)
    max_exact = N_BUCKETS // 2
    nf = jnp.maximum(n, 1).astype(jnp.float32)
    large = max_exact + (jnp.log(nf / max_exact) / math.log(MAX_DISTANCE / max_exact)
                         * (N_BUCKETS - max_exact)).astype(jnp.int32)
    large = jnp.minimum(large, N_BUCKETS - 1)
    return jnp.where(n < max_exact, n, large)

def _pool_mixer(u, pool_w, pool_scale):
    B, S, _ = u.shape
    ug = u.reshape(B, S, POOL_GROUPS, POOL_GROUP_DIM).astype(jnp.float32)
    cs = jnp.concatenate([jnp.zeros((B, 1, POOL_GROUPS, POOL_GROUP_DIM), jnp.float32),
                          jnp.cumsum(ug, axis=1)], axis=1)
    win = jnp.array(POOL_WINDOWS, jnp.int32)
    t1 = jnp.arange(1, S + 1, dtype=jnp.int32)[:, None]
    lo = jnp.maximum(t1 - win[None, :], 0)
    cnt = jnp.minimum(t1, win[None, :]).astype(jnp.float32)
    g_idx = jnp.arange(POOL_GROUPS)[None, :]
    mean = (cs[:, 1:] - cs[:, lo, g_idx, :]) / cnt[None, :, :, None]
    pooled = (mean - ug).astype(u.dtype)
    mixed = jnp.einsum('bsgc,gcd->bsgd', pooled, pool_w)
    return mixed.reshape(B, S, POOL_WIDTH) * pool_scale

def _sparse_attention(q, k, v, q_idx, k_idx, w_idx, rel_bias_table):
    B, S = q.shape[:2]
    n_sel = min(TOPK_MAX, S // 4)
    nb = S // Q_BLOCK
    key_pos = jnp.arange(S, dtype=jnp.int32)
    idx_scale = IDX_DIM ** -0.5
    w_scale = IDX_HEADS ** -0.5
    attn_scale = ATTN_HEAD_DIM ** -0.5

    def blockify(a):
        return a.reshape((B, nb, Q_BLOCK) + a.shape[2:]).swapaxes(0, 1)

    def one_block(args):
        qb, qib, wb, start = args
        q_pos = start + jnp.arange(Q_BLOCK, dtype=jnp.int32)
        dots = jnp.einsum('bthd,bsd->bths', qib, k_idx).astype(jnp.float32) * idx_scale
        score = jnp.einsum('bths,bth->bts', jax.nn.relu(dots), wb.astype(jnp.float32) * w_scale)
        causal = key_pos[None, :] <= q_pos[:, None]
        score = jnp.where(causal[None], score, -jnp.inf)
        _, sel = lax.top_k(score, n_sel)
        valid = sel <= q_pos[None, :, None]
        kg = jax.vmap(lambda kb, ib: kb[ib])(k, sel)
        vg = jax.vmap(lambda vb, ib: vb[ib])(v, sel)
        logits = jnp.einsum('bthd,btkd->bhtk', qb, kg).astype(jnp.float32) * attn_scale
        bias = rel_bias_table[_t5_bucket(q_pos[None, :, None] - sel)]
        logits = logits + jnp.moveaxis(bias, -1, 1).astype(jnp.float32)
        logits = jnp.where(valid[:, None], logits, -jnp.inf)
        p = jax.nn.softmax(logits, axis=-1).astype(vg.dtype)
        return jnp.einsum('bhtk,btkd->bthd', p, vg)

    starts = jnp.arange(nb, dtype=jnp.int32) * Q_BLOCK
    out = lax.map(one_block, (blockify(q), blockify(q_idx), blockify(w_idx), starts))
    return out.swapaxes(0, 1).reshape(B, S, ATTN_HEADS * ATTN_HEAD_DIM)

def _mixer_sublayer(h, w_in, pool_w, pool_scale, w_proj_pool, w_proj_attn, rel_bias_table, w_out):
    B, S, _ = h.shape
    proj = h @ w_in
    offs = np.cumsum(IN_SPLITS)[:-1].tolist()
    u_pool, q, k, v, q_idx, k_idx, w_idx, g_pool, g_attn = jnp.split(proj, offs, axis=-1)
    a = _pool_mixer(u_pool, pool_w, pool_scale) @ w_proj_pool
    att = _sparse_attention(q.reshape(B, S, ATTN_HEADS, ATTN_HEAD_DIM), k, v,
                            q_idx.reshape(B, S, IDX_HEADS, IDX_DIM), k_idx, w_idx,
                            rel_bias_table)
    b = att @ w_proj_attn
    merged = jax.nn.sigmoid(g_pool) * a + jax.nn.sigmoid(g_attn) * b
    return merged @ w_out

def _memory_cross_attention(h, mem, norm_mem_kv, w_q_mem, w_kv_mem, w_o_mem):
    B, S, _ = h.shape
    q = (h @ w_q_mem).reshape(B, S, MEM_HEADS, MEM_HEAD_DIM)
    kv = _rmsnorm(mem, norm_mem_kv) @ w_kv_mem
    k, v = jnp.split(kv, 2, axis=-1)
    k = k.reshape(B, N_MEM, MEM_HEADS, MEM_HEAD_DIM)
    v = v.reshape(B, N_MEM, MEM_HEADS, MEM_HEAD_DIM)
    logits = jnp.einsum('bshd,bmhd->bhsm', q, k).astype(jnp.float32) * MEM_HEAD_DIM ** -0.5
    p = jax.nn.softmax(logits, axis=-1).astype(v.dtype)
    o = jnp.einsum('bhsm,bmhd->bshd', p, v).reshape(B, S, MEM_WIDTH)
    return o @ w_o_mem

def _swiglu(h, w_gate_up, w_down):
    g, u = jnp.split(h @ w_gate_up, 2, axis=-1)
    return (jax.nn.silu(g) * u) @ w_down

def first_inputs(seed: int = 0) -> dict:
    key = jax.random.key(seed)
    ks = jax.random.split(key, 24)
    f32 = jnp.float32

    def w(k, shape, fan_in):
        return jax.random.normal(k, shape, f32) * fan_in ** -0.5

    def gain(k, n):
        return 1.0 + 0.02 * jax.random.normal(k, (n,), f32)

    return {
        "x": jax.random.normal(ks[0], (BATCH, SEQ, D_MODEL), f32),
        "mem": jax.random.normal(ks[1], (BATCH, N_MEM, D_MODEL), f32),
        "norm_mix_pre": gain(ks[2], D_MODEL),
        "norm_mix_post": gain(ks[3], D_MODEL),
        "w_in": w(ks[4], (D_MODEL, IN_WIDTH), D_MODEL),
        "pool_w": w(ks[5], (POOL_GROUPS, POOL_GROUP_DIM, POOL_GROUP_DIM), POOL_GROUP_DIM),
        "pool_scale": gain(ks[6], POOL_WIDTH),
        "w_proj_pool": w(ks[7], (POOL_WIDTH, D_MODEL), POOL_WIDTH),
        "w_proj_attn": w(ks[8], (ATTN_WIDTH, D_MODEL), ATTN_WIDTH),
        "rel_bias_table": 0.5 * jax.random.normal(ks[9], (N_BUCKETS, ATTN_HEADS), f32),
        "w_out": w(ks[10], (D_MODEL, D_MODEL), D_MODEL),
        "norm_mem_pre": gain(ks[11], D_MODEL),
        "norm_mem_kv": gain(ks[12], D_MODEL),
        "norm_mem_post": gain(ks[13], D_MODEL),
        "w_q_mem": w(ks[14], (D_MODEL, MEM_WIDTH), D_MODEL),
        "w_kv_mem": w(ks[15], (D_MODEL, 2 * MEM_WIDTH), D_MODEL),
        "w_o_mem": w(ks[16], (MEM_WIDTH, D_MODEL), MEM_WIDTH),
        "norm_ffn_pre": gain(ks[17], D_MODEL),
        "norm_ffn_post": gain(ks[18], D_MODEL),
        "w_gate_up": w(ks[19], (D_MODEL, 2 * D_FF), D_MODEL),
        "w_down": w(ks[20], (D_FF, D_MODEL), D_FF),
    }

def first_block(x, mem, norm_mix_pre, norm_mix_post, w_in, pool_w, pool_scale, w_proj_pool,
              w_proj_attn, rel_bias_table, w_out, norm_mem_pre, norm_mem_kv, norm_mem_post,
              w_q_mem, w_kv_mem, w_o_mem, norm_ffn_pre, norm_ffn_post, w_gate_up, w_down):
    for _ in range(DEPTH):
        h = _rmsnorm(x, norm_mix_pre)
        x = x + _rmsnorm(_mixer_sublayer(h, w_in, pool_w, pool_scale, w_proj_pool,
                                         w_proj_attn, rel_bias_table, w_out), norm_mix_post)
        h = _rmsnorm(x, norm_mem_pre)
        x = x + _rmsnorm(_memory_cross_attention(h, mem, norm_mem_kv, w_q_mem, w_kv_mem, w_o_mem),
                         norm_mem_post)
        h = _rmsnorm(x, norm_ffn_pre)
        x = x + _rmsnorm(_swiglu(h, w_gate_up, w_down), norm_ffn_post)
    return x


MLA_HEADS = 4
MLA_NOPE = 128
MLA_ROPE = 64
MLA_V = 128
Q_LORA = D_MODEL // 4
KV_LORA = D_MODEL // 8
MLA_QK = MLA_NOPE + MLA_ROPE
MLA_WIDTH = MLA_HEADS * MLA_V

DIFF_HEADS = 4
DIFF_D = 64
DIFF_V = 2 * DIFF_D
DIFF_QK_WIDTH = DIFF_HEADS * 2 * DIFF_D
DIFF_WIDTH = DIFF_HEADS * DIFF_V

MIX_WIDTH = MLA_WIDTH + DIFF_WIDTH
IN_WIDTH_2 = Q_LORA + KV_LORA + MLA_ROPE + 2 * DIFF_QK_WIDTH + DIFF_WIDTH
SPLITS = (Q_LORA, Q_LORA + KV_LORA, Q_LORA + KV_LORA + MLA_ROPE,
          Q_LORA + KV_LORA + MLA_ROPE + DIFF_QK_WIDTH,
          Q_LORA + KV_LORA + MLA_ROPE + 2 * DIFF_QK_WIDTH)

D_FF_2 = 4 * D_MODEL
ROPE_THETA = 10000.0


def _rmsnorm_2(x, w):
    x32 = x.astype(jnp.float32)
    y = x32 * lax.rsqrt(jnp.mean(x32 * x32, axis=-1, keepdims=True) + EPS)
    return (y * w.astype(jnp.float32)).astype(x.dtype)

def _rotate_half(x):
    x1, x2 = jnp.split(x, 2, axis=-1)
    return jnp.concatenate([-x2, x1], axis=-1)

def _rope_tables(seq, dtype):
    inv = ROPE_THETA ** (-jnp.arange(0, MLA_ROPE, 2, dtype=jnp.float32) / MLA_ROPE)
    ang = jnp.arange(seq, dtype=jnp.float32)[:, None] * inv[None, :]
    ang = jnp.concatenate([ang, ang], axis=-1)
    return jnp.cos(ang).astype(dtype), jnp.sin(ang).astype(dtype)

def _t5_bucket_2(rel):
    half = N_BUCKETS // 2
    ret = jnp.where(rel > 0, half, 0)
    n = jnp.abs(rel)
    max_exact = half // 2
    large = max_exact + (jnp.log(jnp.maximum(n, 1).astype(jnp.float32) / max_exact)
                         / math.log(MAX_DISTANCE / max_exact)
                         * (half - max_exact)).astype(jnp.int32)
    large = jnp.minimum(large, half - 1)
    return ret + jnp.where(n < max_exact, n, large)

def _query_blocks(q):
    b, s = q.shape[:2]
    qb = q.reshape((b, s // Q_BLOCK, Q_BLOCK) + q.shape[2:])
    return jnp.moveaxis(qb, 1, 0)

def _merge_blocks(o):
    o = jnp.moveaxis(o, 0, 1)
    return o.reshape((o.shape[0], o.shape[1] * o.shape[2]) + o.shape[3:])

def _mla_attention(q, k, v):
    scale = MLA_QK ** -0.5

    def one(qblk):
        s = jnp.einsum('bqhd,bkhd->bhqk', qblk, k).astype(jnp.float32) * scale
        p = jax.nn.softmax(s, axis=-1).astype(v.dtype)
        return jnp.einsum('bhqk,bkhd->bqhd', p, v)

    return _merge_blocks(lax.map(one, _query_blocks(q)))

def _diff_attention(q, k, v, rel_bias, lam):
    seq = q.shape[1]
    scale = DIFF_D ** -0.5
    kpos = jnp.arange(seq, dtype=jnp.int32)
    starts = jnp.arange(seq // Q_BLOCK, dtype=jnp.int32) * Q_BLOCK
    table = rel_bias.astype(jnp.float32)

    def one(args):
        qblk, start = args
        qpos = start + jnp.arange(Q_BLOCK, dtype=jnp.int32)
        bucket = _t5_bucket_2(kpos[None, :] - qpos[:, None])
        bias = jnp.moveaxis(table[bucket], -1, 0)
        s = jnp.einsum('bqhmd,bkhmd->bmhqk', qblk, k).astype(jnp.float32) * scale + bias
        p = jax.nn.softmax(s, axis=-1)
        a = p[:, 0] - lam * p[:, 1]
        return jnp.einsum('bhqk,bkhd->bqhd', a.astype(v.dtype), v)

    return _merge_blocks(lax.map(one, (_query_blocks(q), starts)))

def second_inputs(seed: int = 0) -> dict:
    key = jax.random.key(seed)
    ks = jax.random.split(key, 24)
    f32 = jnp.float32

    def w(k, shape, fan_in):
        return jax.random.normal(k, shape, f32) * fan_in ** -0.5

    def gain(k, shape):
        return 1.0 + 0.02 * jax.random.normal(k, shape, f32)

    L = DEPTH
    return {
        "x": jax.random.normal(ks[0], (BATCH, SEQ, D_MODEL), f32),
        "attn_norm_w": gain(ks[1], (L, D_MODEL)),
        "w_in": w(ks[2], (L, D_MODEL, IN_WIDTH_2), D_MODEL),
        "q_a_norm_w": gain(ks[3], (L, Q_LORA)),
        "w_uq": w(ks[4], (L, Q_LORA, MLA_HEADS * MLA_QK), Q_LORA),
        "kv_a_norm_w": gain(ks[5], (L, KV_LORA)),
        "w_ukv": w(ks[6], (L, KV_LORA, MLA_HEADS * (MLA_NOPE + MLA_V)), KV_LORA),
        "mla_q_norm_w": gain(ks[7], (L, MLA_QK)),
        "mla_k_norm_w": gain(ks[8], (L, MLA_QK)),
        "diff_q_norm_w": gain(ks[9], (L, DIFF_D)),
        "diff_k_norm_w": gain(ks[10], (L, DIFF_D)),
        "lambda_q1": 0.1 * jax.random.normal(ks[11], (L, DIFF_D), f32),
        "lambda_k1": 0.1 * jax.random.normal(ks[12], (L, DIFF_D), f32),
        "lambda_q2": 0.1 * jax.random.normal(ks[13], (L, DIFF_D), f32),
        "lambda_k2": 0.1 * jax.random.normal(ks[14], (L, DIFF_D), f32),
        "diff_out_norm_w": gain(ks[15], (L, DIFF_V)),
        "w_out": w(ks[16], (L, MIX_WIDTH, D_MODEL), MIX_WIDTH),
        "mlp_norm_w": gain(ks[17], (L, D_MODEL)),
        "w_up": w(ks[18], (L, D_MODEL, D_FF_2), D_MODEL),
        "w_down": w(ks[19], (L, D_FF_2, D_MODEL), D_FF_2),
        "rel_bias": 0.5 * jax.random.normal(ks[20], (N_BUCKETS, DIFF_HEADS), f32),
    }

def second_block(x, attn_norm_w, w_in, q_a_norm_w, w_uq, kv_a_norm_w, w_ukv,
              mla_q_norm_w, mla_k_norm_w, diff_q_norm_w, diff_k_norm_w,
              lambda_q1, lambda_k1, lambda_q2, lambda_k2, diff_out_norm_w,
              w_out, mlp_norm_w, w_up, w_down, rel_bias):
    b, s, _ = x.shape
    cos, sin = _rope_tables(s, x.dtype)
    for layer in range(DEPTH):
        lam_init = 0.8 - 0.6 * math.exp(-0.3 * layer)

        h = _rmsnorm_2(x, attn_norm_w[layer])
        proj = h @ w_in[layer]
        c_q, c_kv, k_rope, dq, dk, dv = jnp.split(proj, SPLITS, axis=-1)

        q = (_rmsnorm_2(c_q, q_a_norm_w[layer]) @ w_uq[layer]).reshape(b, s, MLA_HEADS, MLA_QK)
        q_nope, q_rope = q[..., :MLA_NOPE], q[..., MLA_NOPE:]
        q_rope = q_rope * cos[:, None, :] + _rotate_half(q_rope) * sin[:, None, :]
        kv = (_rmsnorm_2(c_kv, kv_a_norm_w[layer]) @ w_ukv[layer]).reshape(b, s, MLA_HEADS, MLA_NOPE + MLA_V)
        k_nope, v_mla = kv[..., :MLA_NOPE], kv[..., MLA_NOPE:]
        k_rope = k_rope * cos + _rotate_half(k_rope) * sin
        k_rope = jnp.broadcast_to(k_rope[:, :, None, :], (b, s, MLA_HEADS, MLA_ROPE))
        q_m = _rmsnorm_2(jnp.concatenate([q_nope, q_rope], axis=-1), mla_q_norm_w[layer])
        k_m = _rmsnorm_2(jnp.concatenate([k_nope, k_rope], axis=-1), mla_k_norm_w[layer])
        o_mla = _mla_attention(q_m, k_m, v_mla).reshape(b, s, MLA_WIDTH)

        dq = _rmsnorm_2(dq.reshape(b, s, DIFF_HEADS, 2, DIFF_D), diff_q_norm_w[layer])
        dk = _rmsnorm_2(dk.reshape(b, s, DIFF_HEADS, 2, DIFF_D), diff_k_norm_w[layer])
        dv = dv.reshape(b, s, DIFF_HEADS, DIFF_V)
        lam = (jnp.exp(jnp.sum(lambda_q1[layer].astype(jnp.float32) * lambda_k1[layer].astype(jnp.float32)))
               - jnp.exp(jnp.sum(lambda_q2[layer].astype(jnp.float32) * lambda_k2[layer].astype(jnp.float32)))
               + lam_init)
        o_d = _diff_attention(dq, dk, dv, rel_bias, lam)
        o_diff = (_rmsnorm_2(o_d, diff_out_norm_w[layer]) * (1.0 - lam_init)).reshape(b, s, DIFF_WIDTH)

        x = x + jnp.concatenate([o_mla, o_diff], axis=-1) @ w_out[layer]

        h = _rmsnorm_2(x, mlp_norm_w[layer])
        x = x + jnp.square(jax.nn.relu(h @ w_up[layer])) @ w_down[layer]
    return x


def setup_inputs(seed=0):
    out = dict(first_inputs(seed))
    for name, value in second_inputs(seed + 1).items():
        if name != "x":
            out[name + "_2"] = value
    return out


def reference(
    x, mem, norm_mix_pre, norm_mix_post, w_in, pool_w, pool_scale, w_proj_pool, w_proj_attn,
    rel_bias_table, w_out, norm_mem_pre, norm_mem_kv, norm_mem_post, w_q_mem, w_kv_mem, w_o_mem,
    norm_ffn_pre, norm_ffn_post, w_gate_up, w_down, attn_norm_w_2, w_in_2, q_a_norm_w_2, w_uq_2,
    kv_a_norm_w_2, w_ukv_2, mla_q_norm_w_2, mla_k_norm_w_2, diff_q_norm_w_2, diff_k_norm_w_2,
    lambda_q1_2, lambda_k1_2, lambda_q2_2, lambda_k2_2, diff_out_norm_w_2, w_out_2,
    mlp_norm_w_2, w_up_2, w_down_2, rel_bias_2,
):
    x = first_block(
        x, mem, norm_mix_pre, norm_mix_post, w_in, pool_w, pool_scale, w_proj_pool, w_proj_attn,
        rel_bias_table, w_out, norm_mem_pre, norm_mem_kv, norm_mem_post, w_q_mem, w_kv_mem,
        w_o_mem, norm_ffn_pre, norm_ffn_post, w_gate_up, w_down,
    )
    return second_block(
        x, attn_norm_w_2, w_in_2, q_a_norm_w_2, w_uq_2, kv_a_norm_w_2, w_ukv_2, mla_q_norm_w_2,
        mla_k_norm_w_2, diff_q_norm_w_2, diff_k_norm_w_2, lambda_q1_2, lambda_k1_2, lambda_q2_2,
        lambda_k2_2, diff_out_norm_w_2, w_out_2, mlp_norm_w_2, w_up_2, w_down_2, rel_bias_2,
    )


_drawn_inputs = setup_inputs


def setup_inputs(seed=0):
    import zlib

    import numpy as np

    out = dict(_drawn_inputs(seed))
    spreads = {}
    factors = {'norm_mix_post': 3.754,
     'pool_scale': 3.488,
     'norm_mem_pre': 4.376,
     'norm_mem_kv': 2.865,
     'norm_mem_post': 3.82,
     'norm_ffn_pre': 3.913,
     'norm_ffn_post': 5.67,
     'attn_norm_w_2': 8.0,
     'q_a_norm_w_2': 8.0,
     'kv_a_norm_w_2': 8.0,
     'mla_q_norm_w_2': 8.0,
     'mla_k_norm_w_2': 8.0,
     'diff_q_norm_w_2': 8.0,
     'diff_k_norm_w_2': 8.0,
     'lambda_q1_2': 2.907,
     'lambda_k1_2': 2.718,
     'lambda_q2_2': 3.362,
     'lambda_k2_2': 2.87,
     'diff_out_norm_w_2': 8.0,
     'mlp_norm_w_2': 4.839,
     'rel_bias_2': 3.371}
    for name, (base, spread) in spreads.items():
        noise = np.random.default_rng([zlib.crc32(name.encode()), seed]).standard_normal(out[name].shape)
        drawn = base * np.exp(spread * noise) if base else spread * noise
        out[name] = __import__('jax').numpy.asarray(drawn.astype(out[name].dtype))
    for name, factor in factors.items():
        out[name] = (out[name] * factor).astype(out[name].dtype)
    return out
```

```python
from contextlib import ExitStack

import numpy as np

import concourse.bass as bass
from concourse import mybir

F32 = mybir.dt.float32
F32R = mybir.dt.float32r
BF16 = mybir.dt.bfloat16
ACT = mybir.ActivationFunctionType
ALU = mybir.AluOpType
AX = mybir.AxisListType

P = 128
D = 1024
KT = D // P
S = 1024
NT = S // P
HALF = 512
EPS = 1e-6

POOL_GROUPS = 4
HEADS = 8
IDX_HEADS, IDX_DIM = 4, 64
TOPK = 256
ROUNDS = TOPK // 8
BUCKETS = 32
MAX_DISTANCE = 128
VW = P + IDX_HEADS
M = 256
MT = M // P
MEM_HEADS = 4
FF = 2816
FF_TILES = FF // P
FF2 = 4096
FF2_TILES = FF2 // P
CHUNK = 4
MLA_HEADS = 4
DIFF_HEADS = 4
ROPE = 64
LAM_INIT = 0.2
NEG = -1e30
TAKEN = -3e38

COLS = {}
for _name, _n in (
    ("mix_pre", 8), ("mix_post", 8), ("pool_scale", 4), ("mem_pre", 8), ("mem_kv", 8), ("mem_post", 8),
    ("ffn_pre", 8), ("ffn_post", 8), ("attn_2", 8), ("q_a", 2), ("kv_a", 1), ("mla_q_nope", 1),
    ("mla_q_rope", 1), ("mla_k_nope", 1), ("mla_k_rope", 1), ("diff_q", 1), ("diff_k", 1),
    ("diff_out", 1), ("mlp_2", 8), ("lambda", 256),
):
    COLS[_name] = (sum(n for _, n in COLS.values()), _n)
N_COLS = sum(n for _, n in COLS.values())

PRE_ORDER = ("mix_pre", "mem_pre", "ffn_pre", "attn_2", "q_a", "kv_a", "mlp_2")
PRE = {}
for _name in PRE_ORDER:
    PRE[_name] = (COLS[_name][1], sum(n for n, _ in PRE.values()))

SLABS = {}
for _name, _n in (
    ("mix_in", 8),
    ("value_pool", 2),
    ("proj_pool", 4), ("gate_pool", 8), ("gate_attn", 8), ("query", 8), ("proj_attn", 8), ("mix_out", 8),
    ("mem_key", 4), ("mem_value", 4), ("mem_query", 4), ("mem_out", 4),
    ("ffn", 2 * FF_TILES + FF_TILES),
    ("in_2", 13), ("diff_value", 4), ("ukv", 1), ("uq", 2), ("out_2", 8), ("mlp_2", 64),
):
    SLABS[_name] = (sum(n for _, n in SLABS.values()), _n)
N_SLABS = sum(n for _, n in SLABS.values())


class Chain:

    def __init__(self, engine, sem):
        self.engine, self.sem, self.n = engine, sem, 0

    def __call__(self, instruction):
        self.n += 1
        instruction.then_inc(self.sem, 1)
        self.engine.wait_ge(self.sem, self.n)


def program(nc, t):
    out = t["out"]
    with ExitStack() as ctx:
        def sem(name):
            return ctx.enter_context(nc.semaphore(name))

        KB = 1024
        base = -(-nc.sbuf_base // 64) * 64
        RAW, SPLIT = base, base + 8 * KB
        XR = SPLIT + 16 * KB
        AR = XR + 32 * KB
        BR = AR + 64 * KB
        ER = BR + 64 * KB
        place = [ER]

        def at(name, offset, shape, dt=F32):
            return nc.alloc_sbuf_tensor_at(name, shape, dt, offset=offset)

        def small(name, shape, dt=F32):
            size = int(np.prod(shape[1:])) * (2 if dt == BF16 else 4)
            here = place[0]
            place[0] += -(-size // 32) * 32
            return at(name, here, shape, dt)

        raw = [at(f"w_raw{i}", RAW + 4 * KB * i, [P, 1024]) for i in range(2)]
        w_hi = [at(f"w_hi{i}", SPLIT + 8 * KB * i, [P, 1024], F32R) for i in range(2)]
        w_lo = [at(f"w_lo{i}", SPLIT + 8 * KB * i + 4 * KB, [P, 1024], F32R) for i in range(2)]

        acc = small("acc", [P, S])
        tmp_at = place[0]
        tmp = [small(f"tmp{i}", [P, S]) for i in range(2)]
        cols = small("cols", [P, N_COLS])
        ident = small("ident", [P, P])
        ident16 = small("ident16", [P, P], BF16)
        tri = small("tri", [P, P])
        ones = small("ones", [P, P])
        zero = small("zero", [P, 1])
        eps = small("eps", [P, 1])
        pool_fix = small("pool_fix", [P, POOL_GROUPS, 16])
        stat = small("stat", [P, 64])
        top8 = small("top8", [P, 2, 8])
        mstat = small("mstat", [P, 2, 4, 4])
        late_at = place[0]
        place[0] += 8 * KB
        lam_ab, minus_lam = stat[:, 0:2], stat[:, 2:3]
        value_raw = at("value_raw", late_at, [P, NT, VW])
        assert place[0] <= nc.sbuf_usable_end, place[0] - nc.sbuf_usable_end

        def col(name, k=0):
            return cols[:, COLS[name][0] + k:COLS[name][0] + k + 1]

        def pair(name, offset, shape):
            size = int(np.prod(shape[1:])) * 4
            return at(name + "_hi", offset, shape, F32R), at(name + "_lo", offset + size, shape, F32R)

        x_in = at("x_in", XR, [P, KT, S])
        h1 = pair("h1", AR, [P, KT, S])
        u = at("u", XR, [P, POOL_GROUPS, S])
        win = [at(f"win{i}", XR + 16 * KB + 4 * KB * i, [P, S]) for i in range(2)]
        pooled = pair("pooled", BR, [P, POOL_GROUPS, S])
        mixed = pair("mixed", XR, [P, POOL_GROUPS, S])
        qidx = pair("qidx", BR + 32 * KB, [P, 2, S])
        kidx = pair("kidx", BR + 48 * KB, [P, S])
        key = pair("key", BR + 56 * KB, [P, S])
        score_at = {i: sum(j + 1 for j in range(2, i)) * P for i in range(2, NT)}
        score = at("score", BR, [P, sum(j + 1 for j in range(2, NT)) * P])
        mask_at = {i: sum(j + 1 for j in range(i)) * P for i in range(NT)}
        mask = at("mask", BR + 16896, [P, sum(range(1, NT + 1)) * P], BF16)
        query = at("query", XR, [P, HEADS, S])
        value = pair("value", BR + 32 * KB, [P, NT, P])
        probs = at("probs", BR, [P, 4, S])
        probs_t = [pair(f"probs_t{i}", BR + 40 * KB + 4 * KB * i, [P, HALF]) for i in range(2)]
        q_tile = pair("q_tile", tmp_at, [P, HEADS, P])
        bias = at("bias", BR + 48 * KB, [P, HEADS, 2 * P])
        bias_2 = at("bias_2", BR + 40 * KB, [P, DIFF_HEADS, 3 * P])
        flip = at("flip", BR + 46 * KB, [P, P])
        frow = at("frow", BR + 56 * KB, [HEADS, 384])
        onehot = at("onehot", BR + 58 * KB, [BUCKETS, 384])
        table = at("table", BR + 60 * KB, [BUCKETS, HEADS])
        table_2 = at("table_2", BR + 60 * KB + 512, [BUCKETS, DIFF_HEADS])
        onehot_2 = at("onehot_2", BR + 61 * KB, [BUCKETS, HALF])
        frow_2 = at("frow_2", late_at + 6 * KB, [DIFF_HEADS, HALF])
        att = pair("att", AR, [P, HEADS, S])
        gated = [at(f"gated{i}", XR + 12 * KB * i, [P, 3, S]) for i in range(2)]
        merged = pair("merged", BR, [P, KT, S])
        y = at("y", AR, [P, KT, S])
        x = at("x", XR, [P, KT, S])

        mem_in = at("mem_in", AR + 32 * KB, [P, KT, M])
        memn = pair("memn", AR + 40 * KB, [P, KT, M])
        mem_sq = at("mem_sq", AR + 48 * KB, [P, KT, M])
        mem_rms = at("mem_rms", AR + 56 * KB, [P, M])
        kmem = pair("kmem", AR + 32 * KB, [P, MEM_HEADS, M])
        vmem = pair("vmem", late_at, [P, MT, HALF])
        normed = pair("normed", BR, [P, KT, S])
        qm = pair("qm", AR, [P, MEM_HEADS, S])
        om = pair("om", BR, [P, MEM_HEADS, S])
        mprobs = at("mprobs", BR + 32 * KB, [P, 2, 4, M])
        mpt = [pair(f"mpt{j}", BR + 40 * KB + 4 * KB * j, [P, HALF]) for j in range(MT)]
        hidden = pair("hidden", AR + 32 * KB, [P, CHUNK, S])
        c_q = at("c_q", AR, [P, 2, S])
        cq = pair("cq", AR + 8 * KB, [P, 2, S])
        c_kv = at("c_kv", AR + 24 * KB, [P, 1, S])
        ckv = pair("ckv", AR + 28 * KB, [P, 1, S])
        k_rope = at("k_rope", AR + 36 * KB, [P, S])
        q_rope = at("q_rope", AR + 40 * KB, [P, 2, S])
        q_rope_sq = at("q_rope_sq", AR + 48 * KB, [P, 2, S])
        k_rope_sq = at("k_rope_sq", AR + 56 * KB, [P, S])
        halves = at("halves", AR + 60 * KB, [P, 3, P])
        cos, sin = at("cos", late_at, [P, S]), at("sin", late_at + 4 * KB, [P, S])
        d_rms = [at(f"d_rms{i}", AR + 48 * KB + 4 * KB * i, [P, S]) for i in range(2)]
        d_out = [at(f"d_out{i}", AR + 4 * KB * i, [P, S]) for i in range(2)]
        d_value = at("d_value", BR, [P, NT, HALF])
        v_value = at("v_value", BR + 16 * KB, [P, NT, HALF])
        g_rms = [at(f"g_rms{i}", BR + 32 * KB + 4 * KB * i, [P, S]) for i in range(2)]
        g_nope = [at(f"g_nope{i}", BR + 40 * KB + 4 * KB * i, [P, S]) for i in range(2)]
        g_rope = [at(f"g_rope{i}", BR + 48 * KB + 4 * KB * i, [P, S]) for i in range(2)]
        turned = at("turned", BR + 56 * KB, [P, S])
        m_raw = [at(f"m_raw{i}", AR + 4 * KB * i, [P if i < 3 else ROPE, S]) for i in range(5)]
        m_parts = [pair(f"m_part{i}", AR + 20 * KB + 8 * KB * i, [P if i < 3 else ROPE, S]) for i in range(5)]
        m_probs2 = [at(f"m_probs{i}", BR + 16 * KB * i, [P, 4, S]) for i in range(2)]
        pt = [pair(f"pt{i}", BR + 32 * KB + 4 * KB * i, [P, HALF]) for i in range(2)]
        o_stage = at("o_stage", BR + 40 * KB, [P, 2, HALF])
        e_raw = [at(f"e_raw{i}", BR + 44 * KB + 4 * KB * i, [P, S]) for i in range(3)]
        e_bias = at("e_bias", BR + 56 * KB, [P, 3 * P])
        e_parts = [pair(f"e_part{i}", AR + 8 * KB * i, [P, S]) for i in range(3)]
        e_probs = [at("e_probs0", BR, [P, 2, 4, S]), at("e_probs1", AR + 24 * KB, [P, 2, 4, S])]
        e_stat = at("e_stat", late_at, [P, 2, 6, 2, 4])
        e_turn = at("e_turn", late_at + KB, [P, 2, 2, 4])
        o_in = at("o_in", AR, [P, KT, S])
        o_rms = [at(f"o_rms{i}", AR + 32 * KB + 4 * KB * i, [P, S]) for i in range(2)]
        o_all = pair("o_all", BR, [P, KT, S])
        ps = ctx.enter_context(nc.psum_tensor("ps", [P, 8, HALF], F32))

        def wide(slot):
            return ps[:, 2 * slot:2 * slot + 2, :].rearrange("p b n -> p (b n)")

        raw_landed = [sem(f"raw_landed{i}") for i in range(2)]
        w_rounded = sem("w_rounded")
        w_split = sem("w_split")
        w_used = sem("w_used")
        first_half = sem("first_half")
        consts_in = sem("consts_in")
        x_in_landed = [sem(f"x_in_landed{i}") for i in range(2)]
        dve_consts = sem("dve_consts")
        zero_set = sem("zero_set")
        dve_step = sem("dve_step")
        n_sq, n_added = sem("norm_squared"), sem("norm_added")
        n_post_sq, n_acc = sem("norm_post_squared"), sem("norm_post_added")
        n_sum, n_rs = sem("norm_total"), sem("norm_inverse")
        act_step = sem("act_step")
        n_tmp, n_hi, n_lo = (sem("norm_" + n) for n in ("scaled", "hi", "lo"))
        in_hi, in_free = sem("in_hi"), sem("in_free")
        value_done, value_free = sem("value_done"), sem("value_free")
        pooled_ready = sem("pooled_ready")
        pool_done, mix_free = sem("pool_done"), sem("mix_free")
        idx_done, idx_relu, idx_added = sem("idx_done"), sem("idx_relu"), sem("idx_added")
        gate_free = sem("gate_free")
        staged = [sem(f"staged{i}") for i in range(2)]
        frow_done, frow_copied, frow_out = sem("frow_done"), sem("frow_copied"), sem("frow_out")
        shifted_in, flipped, bias_done = sem("shifted_in"), sem("flipped"), sem("bias_done")
        value_split = sem("value_split")
        masks_ready = sem("masks_ready")
        qt_hi, qt_lo = sem("qt_hi"), sem("qt_lo")
        qk_done, logits_ready, nmax_ready, exp_done, probs_ready = (
            sem(n) for n in ("qk_done", "logits_ready", "nmax_ready", "exp_done", "probs_ready"))
        tr_done, pt_hi, pt_lo, pv_done, o_hi, o_lo = (
            sem(n) for n in ("tr_done", "pt_hi", "pt_lo", "pv_done", "o_hi", "o_lo"))
        gates_in = [sem(f"gates_in{i}") for i in range(2)]
        merge_free = sem("merge_free")
        x_landed = sem("x_landed")
        y_free, x_added = sem("y_free"), sem("x_added")
        mem_landed = sem("mem_landed")
        mem_squared, mem_total, mem_rs, mem_scaled, mem_hi, mem_lo = (
            sem("mem_" + n) for n in ("squared", "total", "inverse", "scaled", "hi", "lo"))
        mkv_hi, mkv_lo, mq_hi, mq_lo = (sem(n) for n in ("mem_kv_hi", "mem_kv_lo", "mem_q_hi", "mem_q_lo"))
        m_qk, m_max, m_exp, m_probs, m_tr, m_pthi, m_ptlo, m_pv, m_ohi, m_olo = (
            sem("mem_" + n) for n in ("logits", "max", "exp", "probs", "transposed", "probs_t_hi", "probs_t_lo",
                                      "weighed", "out_hi", "out_lo"))
        f_silu, f_mul, f_hi, f_lo, f_added, y_zero = (
            sem("ffn_" + n) for n in ("silu", "hidden", "hidden_hi", "hidden_lo", "added", "y_zeroed"))
        tables_in, bias_2_out = sem("tables_in"), sem("bias_2_out")
        c_free, d_free = sem("c_free"), sem("d_free")
        d_sq, d_tot, d_ln, d_rs = (sem("diff_norm_" + n) for n in ("squared", "total", "log", "inverse"))
        d_stored = [sem(f"diff_stored{i}") for i in range(2)]
        dv_act, dv_dve, v_done, v_act, v_dve = (
            sem(n) for n in ("dv_out_act", "dv_out_dve", "v_done", "v_out_act", "v_out_dve"))
        dv_stored, v_stored = sem("dv_stored"), sem("v_stored")
        rope_sq = sem("rope_squared")
        g_done, g_sq, g_tot, g_rs, g_free, g_roped = (
            sem("mla_" + n) for n in ("tile", "squared", "total", "inverse", "nope_out", "rope_out"))
        r_done, r_free = sem("rope_done"), sem("rope_free")
        g_stored = [sem(f"mla_stored{i}") for i in range(2)]
        lam_sum, lam_exp = sem("lam_sum"), sem("lam_exp")
        a_raw, a_hi, a_lo, e_raw_in, e_bias_in, e_hi, e_lo = (
            sem(n) for n in ("mla_raw_in", "mla_hi", "mla_lo", "diff_raw_in", "diff_bias_in", "diff_hi", "diff_lo"))
        a_qk, a_red, a_max, a_exp, a_inv, a_probs, a_tr, a_pthi, a_ptlo, a_pv, a_out = (
            sem("attn_" + n) for n in ("logits", "max", "minus_max", "exp", "sum_inverse", "probs", "transposed",
                                       "probs_t_hi", "probs_t_lo", "weighed", "out"))
        e_qk, e_red, e_max, e_exp, e_weighed = (
            sem("diff_" + n) for n in ("logits", "biased", "max", "exp", "weighed"))
        o_stored, o_landed = sem("o_stored"), sem("o_landed")
        s_sq, s_tot, s_rs, s_scaled, s_hi, s_lo = (
            sem("heads_" + n) for n in ("squared", "total", "inverse", "scaled", "hi", "lo"))
        u_relu, u_sq, u_hi, u_lo, u_added = (sem("mlp_" + n) for n in ("relu", "squared", "hi", "lo", "added"))
        stored = sem("stored")

        block = ctx.enter_context(nc.Block())

        @block.sync
        def _(sp):
            for s in range(2):
                sp.dma_start(raw[s][:], t["weights"][s]).then_inc(raw_landed[s], 16)
            def load_slabs(first, end):
                with sp.Fori(first // 2, end // 2) as pr:
                    for s in range(2):
                        sp.wait_ge(w_split, 2 * pr + s - 1)
                        sp.dma_start(raw[s][:], t["weights"][2 * pr + s]).then_inc(raw_landed[s], 16)

            load_slabs(2, SLABS["out_2"][0] + 2)
            sp.wait_ge(v_stored, 16 * MLA_HEADS)
            for e in range(2):
                sp.wait_ge(g_stored[e], 32 * MLA_HEADS)
            with sp.Fori(0, MLA_HEADS) as hn:
                sp.wait_ge(a_lo, 5 * hn + 5)
                for dst, src in zip(m_raw, (t["mla_nope"][hn + MLA_HEADS], t["mla_nope"][hn], t["mla_v"][hn].rearrange("p j n -> p (j n)"),
                                            t["mla_rope"][hn + MLA_HEADS], t["mla_rope"][hn])):
                    sp.dma_start(dst[:], src).then_inc(a_raw, 16)
            sp.wait_ge(dv_stored, 16 * DIFF_HEADS)
            for e in range(2):
                sp.wait_ge(d_stored[e], 16 * DIFF_HEADS)
            sp.wait_ge(bias_2_out, 16)
            with sp.Fori(0, DIFF_HEADS) as hn:
                sp.wait_ge(e_lo, 3 * hn + 3)
                for dst, src in zip(e_raw, (t["diff_qk"][hn], t["diff_qk"][hn + DIFF_HEADS], t["diff_v"][hn].rearrange("p j n -> p (j n)"))):
                    sp.dma_start(dst[:], src).then_inc(e_raw_in, 16)
                sp.wait_ge(e_red, 16 * hn + 2)
                sp.dma_start(e_bias[:], t["bias_tiles_2"][hn]).then_inc(e_bias_in, 16)
            load_slabs(SLABS["out_2"][0] + 2, N_SLABS)

        @block.gpsimd
        def _(pool):
            nc.gpsimd.memset(zero[:], 0.0).then_inc(zero_set, 1)
            pool.wait_ge(zero_set, 1)

            def split(s, n):
                nc.gpsimd.tensor_tensor(w_hi[s][:], raw[s][:], zero[:, 0:1].broadcast_to([P, 1024]),
                                        ALU.add).then_inc(w_rounded, 1)
                pool.wait_ge(w_rounded, n)
                nc.gpsimd.tensor_tensor(w_lo[s][:], raw[s][:], w_hi[s][:].bitcast(F32),
                                        ALU.subtract).then_inc(w_split, 1)

            for s in range(2):
                pool.wait_ge(raw_landed[s], 16)
                split(s, s + 1)
            with pool.Fori(1, N_SLABS // 2) as pr:
                for s in range(2):
                    pool.wait_ge(w_used, 2 * pr + s - 1)
                    pool.wait_ge(raw_landed[s], 16 * pr + 16)
                    split(s, 2 * pr + s + 1)

        @block.tensor
        def _(pe):
            def product(out, stationary, moving, start, stop):
                (sh, sl), (mh, ml) = stationary, moving
                nc.tensor.matmul(out, sh, mh, start=start, stop=False)
                nc.tensor.matmul(out, sh, ml, start=False, stop=False)
                return nc.tensor.matmul(out, sl, mh, start=False, stop=stop)

            def weight(s, b, width=P):
                return w_hi[s][:, b:b + width], w_lo[s][:, b:b + width]

            def tile(s, first, src, kt, slot, between=None):
                out = wide(slot)
                for k in range(kt):
                    for n in range(0, S, HALF):
                        last = product(out[:, n:n + HALF], weight(s, first + k * P),
                                       (src[0][:, k, n:n + HALF], src[1][:, k, n:n + HALF]), k == 0, k == kt - 1)
                    if between and k == 1:
                        between()
                return last

            def over_features(out, src, lhs, start=True, stop=True):
                for n in range(0, S, HALF):
                    last = nc.tensor.matmul(out[:, n:n + HALF], lhs, src[:, n:n + HALF], start=start, stop=stop)
                return last

            def total_added(post):
                pe.wait_ge(n_acc, 7 * (post + 1))
                over_features(wide(2), acc, ones[:]).then_inc(n_sum, 1)

            def total(name):
                tiles, before = PRE[name]
                for k in range(tiles):
                    pe.wait_ge(n_sq, before + k + 1)
                    over_features(wide(2), tmp[k % 2], ones[:], k == 0, k == tiles - 1).then_inc(
                        n_sum if k == tiles - 1 else n_added, 1)

            pe.wait_ge(dve_consts, 1)
            pe.wait_ge(consts_in, 16 * N_CONSTS)
            total("mix_pre")
            nc.tensor.matmul(ps[0:HEADS, 6, 0:384], table[:, :], onehot[:, :], start=True, stop=True)
            nc.tensor.matmul(ps[0:DIFF_HEADS, 7, :], table_2[:, :], onehot_2[:, :], start=True, stop=True).then_inc(frow_done, 1)
            pe.wait_ge(n_lo, KT)
            s0 = SLABS["mix_in"][0]
            with pe.Fori(0, 4) as it:
                for s in range(2):
                    pe.wait_ge(w_split, 2 * it + s0 + s + 1)
                    pe.wait_ge(in_free, 2 * it + s + 1)
                    tile(s, 0, h1, KT, s).then_inc(w_used, 1)
            pe.wait_ge(w_split, SLABS["value_pool"][0] + 2)
            for j in range(NT):
                out = ps[:, 4 + j // 3, (j % 3) * VW:(j % 3 + 1) * VW]
                for k in range(KT):
                    last = product(out, (h1[0][:, k, j * P:(j + 1) * P], h1[1][:, k, j * P:(j + 1) * P]),
                                   weight(k // 4, k % 4 * VW, VW), k == 0, k == KT - 1)
                last.then_inc(value_done, 1)
            pe.wait_ge(pooled_ready, POOL_GROUPS)
            for g in range(POOL_GROUPS):
                pe.wait_ge(*((in_free, 2 + 8) if g < 2 else (mix_free, g - 1)))
                b = 4 * VW + (g % 3) * P
                for n in range(0, S, HALF):
                    last = product(wide(g % 2)[:, n:n + HALF], weight(g // 3, b),
                                   (pooled[0][:, g, n:n + HALF], pooled[1][:, g, n:n + HALF]), True, True)
                last.then_inc(pool_done if g < 2 else w_used, 1)
            pe.wait_ge(value_free, 3)
            unit = 0
            for i in reversed(range(2, NT)):
                for hd in range(IDX_HEADS):
                    if unit >= 2:
                        pe.wait_ge(idx_relu, unit - 1)
                    lo, hi = IDX_DIM * (hd % 2), IDX_DIM * (hd % 2 + 1)
                    for n in range(0, (i + 1) * P, HALF):
                        m = min(HALF, (i + 1) * P - n)
                        last = product(wide(2 + unit % 2)[:, n:n + m],
                                       tuple(q[lo:hi, hd // 2, i * P:(i + 1) * P] for q in qidx),
                                       tuple(k[lo:hi, n:n + m] for k in kidx), True, True)
                    last.then_inc(idx_done, 1)
                    unit += 1
            pe.wait_ge(mix_free, POOL_GROUPS)
            s0 = SLABS["proj_pool"][0]
            with pe.Fori(0, 2) as it:
                for s in range(2):
                    pe.wait_ge(w_split, 2 * it + s0 + s + 1)
                    for half in range(2):
                        pe.wait_ge(gate_free, 4 * it + 2 * s + half + 1)
                        tile(s, half * POOL_GROUPS * P, mixed, POOL_GROUPS, half).then_inc((first_half, w_used)[half], 1)
            pe.wait_ge(shifted_in, 48)
            pe.wait_ge(idx_relu, unit)
            for n in range(4):
                last = nc.tensor.matmul(ps[:, 4 + n, :], flip[:], bias[:, 2 * n:2 * n + 2, :].rearrange("p h u -> p (h u)"),
                                        start=True, stop=True)
            last.then_inc(flipped, 1)
            pe.wait_ge(bias_done, 1)
            for n in range(3):
                last = nc.tensor.matmul(ps[:, 4 + n, :], flip[:],
                                        bias_2[:].rearrange("p h u -> p (h u)")[:, n * HALF:(n + 1) * HALF],
                                        start=True, stop=True)
            last.then_inc(flipped, 1)
            s0 = SLABS["gate_pool"][0]
            with pe.Fori(0, 12) as it:
                for s in range(2):
                    pe.wait_ge(w_split, 2 * it + s0 + s + 1)
                    pe.wait_ge(gate_free, 2 * it + KT + s + 1)
                    tile(s, 0, h1, KT, s).then_inc(w_used, 1)
            pe.wait_ge(masks_ready, 1)
            pe.wait_ge(value_split, 1)
            pe.wait_ge(bias_done, 2)
            pe.wait_ge(gate_free, 2 + 4 * KT)
            n_tr = 0
            for i in range(NT):
                pe.wait_ge(qt_lo, i + 1)
                for g in range(2):
                    for hd in range(4 * g, 4 * g + 4):
                        unit = HEADS * i + hd
                        if unit >= 2:
                            pe.wait_ge(logits_ready, unit - 1)
                        for n in range(0, (i + 1) * P, HALF):
                            m = min(HALF, (i + 1) * P - n)
                            out = wide(unit % 2)[:, n:n + m]
                            product(out, (q_tile[0][:, hd, :], q_tile[1][:, hd, :]),
                                    (key[0][:, n:n + m], key[1][:, n:n + m]), True, False)
                            last = nc.tensor.matmul(out, ident16[:], mask[:, mask_at[i] + n:mask_at[i] + n + m],
                                                    start=False, stop=True)
                        last.then_inc(qk_done, 1)
                    group = 2 * i + g
                    pe.wait_ge(probs_ready, group + 1)
                    if group >= 2:
                        pe.wait_ge(o_lo, group - 1)

                    def weigh(j, n):
                        pe.wait_ge(pt_lo, n + 1)
                        product(ps[:, 6 + group % 2, :], (value[0][:, j, :], value[1][:, j, :]),
                                (probs_t[n % 2][0][:], probs_t[n % 2][1][:]), j == 0, j == i).then_inc(pv_done, 1)

                    for j in range(i + 1):
                        if n_tr >= 2:
                            pe.wait_ge(pt_lo, n_tr - 1)
                        for hd in range(4):
                            last = nc.tensor.transpose(ps[:, 4 + n_tr % 2, hd * P:(hd + 1) * P],
                                                       probs[:, hd, j * P:(j + 1) * P], ident[:])
                        last.then_inc(tr_done, 1)
                        if j:
                            weigh(j - 1, n_tr - 1)
                        n_tr += 1
                    weigh(i, n_tr - 1)
            pe.wait_ge(o_lo, 2 * NT)
            s0 = SLABS["proj_attn"][0]
            with pe.Fori(0, 4) as it:
                for s in range(2):
                    pe.wait_ge(w_split, 2 * it + s0 + s + 1)
                    pe.wait_ge(merge_free, 2 * it + s + 1)
                    tile(s, 0, att, KT, s).then_inc(w_used, 1)
            pe.wait_ge(merge_free, 2 + KT)
            s0 = SLABS["mix_out"][0]

            def out_tiles(first, end):
                with pe.Fori(first, end) as it:
                    for s in range(2):
                        pe.wait_ge(w_split, 2 * it + s0 + s + 1)
                        pe.wait_ge(y_free, 2 * it + s + 1)
                        tile(s, 0, merged, KT, s).then_inc(w_used, 1)

            out_tiles(0, 2)
            pe.wait_ge(mem_squared, 1)
            for k in range(KT):
                last = nc.tensor.matmul(ps[:, 6, 0:M], ones[:], mem_sq[:, k, :], start=k == 0, stop=k == KT - 1)
            last.then_inc(mem_total, 1)
            out_tiles(2, 4)
            pe.wait_ge(mem_lo, 1)
            pe.wait_ge(y_free, 2 + KT)
            s0 = SLABS["mem_key"][0]
            for n in range(MEM_HEADS):
                pe.wait_ge(w_split, s0 + n + 1)
                for k in range(KT):
                    last = product(wide(0)[:, n * M:(n + 1) * M], weight(n % 2, k * P),
                                   (memn[0][:, k, :], memn[1][:, k, :]), k == 0, k == KT - 1)
                last.then_inc(w_used, 1)
                if n == 0:
                    total_added(0)
            s0 = SLABS["mem_value"][0]
            for n in range(4):
                pe.wait_ge(w_split, s0 + n + 1)
                for j in range(MT):
                    for k in (2 * n, 2 * n + 1):
                        last = product(wide(1)[:, j * HALF:(j + 1) * HALF],
                                       tuple(v[:, k, j * P:(j + 1) * P] for v in memn),
                                       weight(n % 2, k % 2 * HALF, HALF), k == 0, k == KT - 1)
                last.then_inc(w_used, 1)
            total("mem_pre")
            pe.wait_ge(mkv_lo, 2)
            pe.wait_ge(n_lo, 2 * KT)
            s0 = SLABS["mem_query"][0]
            with pe.Fori(0, 2) as it:
                for s in range(2):
                    pe.wait_ge(w_split, 2 * it + s0 + s + 1)
                    pe.wait_ge(mq_lo, 2 * it + s + 1)
                    tile(s, 0, normed, KT, s).then_inc(w_used, 1)
            pe.wait_ge(mq_lo, 2 + MEM_HEADS)

            def mem_logits(n):
                if n >= 2:
                    pe.wait_ge(m_exp, 4 * (n - 1))
                for q in range(4):
                    t0 = (4 * (n % 2) + q) * P
                    last = product(wide(n % 2)[:, q * M:(q + 1) * M], tuple(v[:, n // 2, t0:t0 + P] for v in qm),
                                   tuple(v[:, n // 2, :] for v in kmem), True, True)
                last.then_inc(m_qk, 1)

            mem_logits(0)
            for n in range(2 * MEM_HEADS):
                if n + 1 < 2 * MEM_HEADS:
                    mem_logits(n + 1)
                pe.wait_ge(m_probs, n + 1)
                for j in range(MT):
                    if n:
                        pe.wait_ge(m_ptlo, MT * (n - 1) + j + 1)
                    for q in range(4):
                        last = nc.tensor.transpose(ps[:, 4 + j, q * P:(q + 1) * P],
                                                   mprobs[:, n % 2, q, j * P:(j + 1) * P], ident[:])
                    last.then_inc(m_tr, 1)
                if n >= 2:
                    pe.wait_ge(m_olo, n - 1)
                for j in range(MT):
                    pe.wait_ge(m_ptlo, MT * n + j + 1)
                    d0 = n // 2 * P
                    product(ps[:, 6 + n % 2, :], tuple(v[:, j, d0:d0 + P] for v in vmem),
                            tuple(v[:] for v in mpt[j]), j == 0, j == MT - 1).then_inc(m_pv, 1)
            pe.wait_ge(m_olo, 2 * MEM_HEADS)
            s0 = SLABS["mem_out"][0]
            with pe.Fori(0, 2) as it:
                for s in range(2):
                    pe.wait_ge(w_split, 2 * it + s0 + s + 1)
                    for half in range(2):
                        pe.wait_ge(y_free, 4 * it + 2 * s + half + KT + 1)
                        tile(s, half * 4 * P, om, 4, half).then_inc((first_half, w_used)[half], 1)
            total_added(1)
            total("ffn_pre")
            pe.wait_ge(n_lo, 3 * KT)
            s0 = SLABS["ffn"][0]

            def ffn_chunk(c, tiles):
                for j in range(tiles):
                    pe.wait_ge(w_split, 12 * c + s0 + 2 * j + 1)
                    if j < 2:
                        pe.wait_ge(f_added, 8 * c + 2 * j + 6)
                    else:
                        pe.wait_ge(f_mul, 4 * c + j - 1)
                    tile(0, 0, normed, KT, 2 * (j % 2)).then_inc(w_used, 1)
                    pe.wait_ge(w_split, 12 * c + s0 + 2 * j + 2)
                    tile(1, 0, normed, KT, 2 * (j % 2) + 1).then_inc(w_used, 1)
                per = 8 // tiles
                for m in range(KT):
                    if m % per == 0:
                        pe.wait_ge(w_split, 12 * c + s0 + 2 * tiles + m // per + 1)
                    if m < 4:
                        pe.wait_ge(f_mul, 4 * c + (m // 2 + tiles - 1 if tiles == 4 else m // 2 + 1))
                    else:
                        pe.wait_ge(f_added, 8 * c + 8 + m - 3)
                    for k in range(tiles):
                        if m == 0:
                            pe.wait_ge(f_lo, 4 * c + 2 + k + 1)
                        for n in range(0, S, HALF):
                            last = product(wide(m % 4)[:, n:n + HALF], weight(m // per % 2, (m % per * tiles + k) * P),
                                           tuple(v[:, k, n:n + HALF] for v in hidden), k == 0, k == tiles - 1)
                    last.then_inc(w_used if m % per == per - 1 else first_half, 1)

            with pe.Fori(0, FF_TILES // CHUNK) as c:
                ffn_chunk(c, CHUNK)
            ffn_chunk(FF_TILES // CHUNK, FF_TILES % CHUNK)
            total_added(2)
            total("attn_2")
            pe.wait_ge(n_lo, PRE["attn_2"][1] + KT)
            s0 = SLABS["in_2"][0]
            for n in range(5):
                pe.wait_ge(w_split, s0 + n + 1)
                if n >= 2:
                    pe.wait_ge(c_free, n - 1)
                tile(n % 2, 0, normed, KT, n % 2).then_inc(w_used, 1)
                if n >= 3:
                    total(("q_a", "kv_a")[n - 3])
            pe.wait_ge(tables_in, 48)

            def diff_total(q, e):
                pe.wait_ge(d_sq, q + 1)
                over_features(wide(2 + e), tmp[e], halves[:, 0, :]).then_inc(d_tot, 1)

            with pe.Fori(0, DIFF_HEADS) as it:
                for e in range(2):
                    pe.wait_ge(w_split, 2 * it + s0 + 5 + e + 1)
                    pe.wait_ge(d_free, 2 * it + e + 1)
                    tile(1 - e, 0, normed, KT, 1 - e,
                         between=(lambda: diff_total(2 * it, 0)) if e else None).then_inc(w_used, 1)
                diff_total(2 * it + 1, 1)
            pe.wait_ge(d_free, 2 + 2 * DIFF_HEADS)
            s0 = SLABS["diff_value"][0]
            for n in range(4):
                pe.wait_ge(w_split, s0 + n + 1)
                for j in range(NT):
                    for k in (2 * n, 2 * n + 1):
                        last = product(ps[:, j, :], tuple(v[:, k, j * P:(j + 1) * P] for v in normed),
                                       weight((s0 + n) % 2, k % 2 * HALF, HALF), k == 0, k == KT - 1)
                last.then_inc(w_used, 1)
            s0 = SLABS["ukv"][0]
            pe.wait_ge(w_split, s0 + 1)
            for j in range(NT):
                pe.wait_ge(dv_dve if j % 2 else dv_act, j // 2 + 1)
                product(ps[:, j, :], tuple(v[:, 0, j * P:(j + 1) * P] for v in ckv),
                        weight(s0 % 2, HALF, HALF), True, True).then_inc(v_done, 1)
            pe.wait_ge(v_act, 4)
            pe.wait_ge(v_dve, 4)

            def expand(e):
                hd = e % MLA_HEADS
                if e >= 2:
                    pe.wait_ge(g_free, e - 1)
                s = SLABS["uq"][0] + 1 if e >= MLA_HEADS else s0
                parts, kt = (cq, 2) if e >= MLA_HEADS else (ckv, 1)
                tile(s % 2, hd * kt * P, parts, kt, e % 2).then_inc(w_used if hd == MLA_HEADS - 1 else g_done, 1)

            def head_total(e):
                pe.wait_ge(g_sq, e + 1)
                pe.wait_ge(rope_sq, 3 if e >= MLA_HEADS else 1)
                hd = e % MLA_HEADS
                over_features(wide(2 + e % 2), tmp[e % 2], ones[:], True, False)
                rope = q_rope_sq[:, hd // 2, :] if e >= MLA_HEADS else k_rope_sq[:]
                over_features(wide(2 + e % 2), rope, halves[:, 1 + (hd % 2 if e >= MLA_HEADS else 0), :],
                              False, True).then_inc(g_tot, 1)

            for e in range(2 * MLA_HEADS):
                if e == MLA_HEADS:
                    pe.wait_ge(w_split, SLABS["uq"][0] + 2)
                    pe.wait_ge(g_free, MLA_HEADS)
                    for p in range(2):
                        if p:
                            pe.wait_ge(r_free, 1)
                        for n in range(2):
                            tile(SLABS["uq"][0] % 2, (2 * p + n) * 2 * P, cq, 2, n).then_inc(
                                w_used if p and n else r_done, 1)
                    pe.wait_ge(r_free, 2)
                if e % MLA_HEADS == 0:
                    expand(e)
                if e % MLA_HEADS < MLA_HEADS - 1:
                    expand(e + 1)
                head_total(e)
            def weigh_values(hn, g, probs, v):
                group = 2 * hn + g
                pe.wait_ge(a_probs, group + 1)
                pe.wait_ge(a_out, group + 1)

                def add(j):
                    pe.wait_ge(a_ptlo, 8 * group + j + 3)
                    product(ps[:, 6 + g, :], tuple(e[:, j * P:(j + 1) * P] for e in v),
                            tuple(e[:] for e in pt[j % 2]), j == 0, j == NT - 1).then_inc(a_pv, 1)

                for j in range(NT):
                    pe.wait_ge(a_ptlo, 8 * group + j + 1)
                    for q in range(4):
                        last = nc.tensor.transpose(ps[:, 4 + j % 2, q * P:(q + 1) * P],
                                                   probs[:, q, j * P:(j + 1) * P], ident[:])
                    last.then_inc(a_tr, 1)
                    if j:
                        add(j - 1)
                add(NT - 1)

            pe.sem_inc(a_pv, 16)
            with pe.Fori(0, MLA_HEADS) as hn:
                q_n, k_n, v_n, q_r, k_r = m_parts
                pe.wait_ge(a_lo, 5 * hn + 10)
                for g in range(2):
                    for q in range(4):
                        pe.wait_ge(a_exp, 8 * hn + 4 * g + q + 1)
                        t0 = (4 * g + q) * P
                        for n in range(0, S, HALF):
                            out = wide(q % 2)[:, n:n + HALF]
                            product(out, tuple(e[:, t0:t0 + P] for e in q_n), tuple(e[:, n:n + HALF] for e in k_n),
                                    True, False)
                            last = product(out, tuple(e[:, t0:t0 + P] for e in q_r),
                                           tuple(e[:, n:n + HALF] for e in k_r), False, True)
                        last.then_inc(a_qk, 1)
                for g in range(2):
                    weigh_values(hn, g, m_probs2[g], v_n)
            with pe.Fori(0, DIFF_HEADS) as hn:
                q_d, k_d, v_d = e_parts
                pe.wait_ge(e_lo, 3 * hn + 6)
                for g in range(2):
                    for q in range(4):
                        t0 = (4 * g + q) * P
                        for m in range(2):
                            pe.wait_ge(e_red, 16 * hn + 8 * g + 2 * q + m + 1)
                            lo, hi = 64 * m, 64 * m + 64
                            for n in range(0, S, HALF):
                                last = product(wide(m)[:, n:n + HALF], tuple(e[lo:hi, t0:t0 + P] for e in q_d),
                                               tuple(e[lo:hi, n:n + HALF] for e in k_d), True, True)
                            last.then_inc(e_qk, 1)
                for g in range(2):
                    weigh_values(hn + MLA_HEADS, g, e_probs[g][:, 0], v_d)
            for n in range(DIFF_HEADS):
                pe.wait_ge(s_sq, n + 1)
                over_features(wide(2 + n % 2), tmp[n % 2], ones[:]).then_inc(s_tot, 1)
            pe.wait_ge(s_lo, KT)
            s0 = SLABS["out_2"][0]
            with pe.Fori(0, 4) as it:
                for s in range(2):
                    pe.wait_ge(w_split, 2 * it + s0 + s + 1)
                    pe.wait_ge(x_added, 2 * it + 3 * KT + s - 1)
                    tile(s, 0, o_all, KT, s).then_inc(w_used, 1)
            total("mlp_2")
            pe.wait_ge(n_lo, PRE["mlp_2"][1] + KT)
            s0 = SLABS["mlp_2"][0]
            with pe.Fori(0, FF2_TILES // CHUNK) as c:
                for j in range(CHUNK):
                    pe.wait_ge(w_split, 8 * c + s0 + j + 1)
                    pe.wait_ge(u_added, 8 * c + 5 + j)
                    tile(j % 2, 0, normed, KT, j).then_inc(w_used, 1)
                for m in range(KT):
                    if m % 2 == 0:
                        pe.wait_ge(w_split, 8 * c + s0 + 4 + m // 2 + 1)
                    if m < 4:
                        pe.wait_ge(u_relu, 4 * c + m + 1)
                    else:
                        pe.wait_ge(u_added, 8 * c + 8 + m - 3)
                    for k in range(CHUNK):
                        if m == 0:
                            pe.wait_ge(u_lo, 4 * c + 2 + k + 1)
                        for n in range(0, S, HALF):
                            last = product(wide(m % 4)[:, n:n + HALF], weight(m // 2 % 2, (m % 2 * CHUNK + k) * P),
                                           tuple(v[:, k, n:n + HALF] for v in hidden), k == 0, k == CHUNK - 1)
                    last.then_inc(w_used if m % 2 else first_half, 1)

        @block.scalar
        def _(act):
            step = Chain(act, act_step)

            def squares(name, src, ready):
                tiles, before = PRE[name]
                for k in range(tiles):
                    act.wait_ge(*ready(k))
                    if k >= 2:
                        act.wait_ge(n_added, before - PRE_ORDER.index(name) + k - 1)
                    nc.scalar.activation(tmp[k % 2][:], src(k), ACT.Square).then_inc(n_sq, 1)

            def post_square(post, k, src):
                if k >= 3:
                    act.wait_ge(n_acc, 7 * post + k - 2)
                nc.scalar.activation(tmp[k % 2][:] if k else acc[:], src, ACT.Square).then_inc(n_post_sq, 1)

            def inverse(r, width=D):
                act.wait_ge(n_sum, r + 1)
                step(nc.scalar.activation(acc[:], wide(2), ACT.Ln, bias=eps[:], scale=1.0 / width))
                nc.scalar.activation(acc[:], acc[:], ACT.Exp, scale=-0.5).then_inc(n_rs, 1)

            def round_hi(name, dst):
                tiles, before = PRE[name]
                for k in range(tiles):
                    act.wait_ge(n_tmp, before + k + 1)
                    nc.scalar.activation(dst[:, k, :], tmp[k % 2][:], ACT.Copy).then_inc(n_hi, 1)

            for k in range(2):
                act.dma_start(x_in[:, 4 * k:4 * k + 4, :], t["x"][:, 4 * k:4 * k + 4, :]).then_inc(x_in_landed[k], 16)
            for dst, name in ((cols, "cols"), (ident, "c_ident"), (tri, "c_tri"), (pool_fix, "c_pool_fix"),
                              (table, "rel_bias_table"), (onehot, "c_onehot"),
                              (table_2, "rel_bias_2"), (onehot_2, "c_onehot_2")):
                act.dma_start(dst[:], t[name]).then_inc(consts_in, 16)
            act.wait_ge(dve_consts, 1)
            squares("mix_pre", lambda k: x_in[:, k, :], lambda k: (x_in_landed[k // 4], 16))
            inverse(0)
            act.wait_ge(frow_done, 1)
            nc.scalar.activation(frow[:], ps[0:HEADS, 6, 0:384], ACT.Copy).then_inc(frow_copied, 1)
            nc.scalar.activation(frow_2[:], ps[0:DIFF_HEADS, 7, :], ACT.Copy).then_inc(frow_copied, 1)
            act.wait_ge(frow_copied, 2)
            act.dma_start(t["bias_rows"], frow[:]).then_inc(frow_out, 16)
            act.dma_start(t["bias_rows_2"], frow_2[:]).then_inc(frow_out, 16)
            round_hi("mix_pre", h1[0])
            for n, dst in enumerate((kidx[0][:], qidx[0][:, 0, :], qidx[0][:, 1, :], key[0][:])):
                act.wait_ge(w_used, SLABS["mix_in"][0] + 4 + n + 1)
                if n == 3:
                    act.wait_ge(frow_out, 32)
                nc.scalar.activation(dst, wide(n % 2), ACT.Copy).then_inc(in_hi, 1)
            act.wait_ge(mix_free, POOL_GROUPS)
            unit = 0
            for i in reversed(range(2, NT)):
                for hd in range(IDX_HEADS):
                    act.wait_ge(idx_done, unit + 1)
                    if unit >= 2:
                        act.wait_ge(idx_added, unit - 1)
                    n = (i + 1) * P
                    nc.scalar.activation(tmp[unit % 2][:, 0:n], wide(2 + unit % 2)[:, 0:n], ACT.Relu,
                                         scale=IDX_DIM ** -0.5 * IDX_HEADS ** -0.5).then_inc(idx_relu, 1)
                    unit += 1
            for dst, name, heads, width in ((bias, "bias_rows", HEADS, 384), (bias_2, "bias_rows_2", DIFF_HEADS, HALF)):
                rows = t[name]
                act.dma_start(dst[:], bass.AP(tensor=rows.tensor, offset=rows.offset,
                                              ap=[[1, P], [width, heads], [1, dst.shape[2]]])).then_inc(shifted_in, 16)
            act.dma_start(flip[:], t["c_flip"]).then_inc(shifted_in, 16)
            act.sem_inc(gate_free, 2)
            act.wait_ge(idx_added, unit)

            def stage(n, done, func, half, first):
                act.wait_ge(*done)
                if not first:
                    act.wait_ge(staged[half], 8 * (n - half))
                nc.scalar.activation(tmp[half][:], wide(half), func).then_inc(gate_free, 1)
                act.wait_ge(gate_free, n + 3)
                act.dma_start(t["gates"][n], tmp[half][:]).then_inc(staged[half], 16)

            s0 = SLABS["proj_pool"][0]
            for half in range(2):
                stage(half, ((first_half, w_used)[half], (1, s0 + 1)[half]), ACT.Copy, half, True)
            with act.Fori(1, 4) as it:
                for half in range(2):
                    stage(2 * it + half, ((first_half, w_used)[half], it + (1, s0 + 1)[half]), ACT.Copy, half, False)
            act.wait_ge(flipped, 1)
            nc.scalar.activation(bias[:].rearrange("p h u -> p (h u)"), ps[:, 4:8, :].rearrange("p b n -> p (b n)"),
                                 ACT.Copy).then_inc(bias_done, 1)
            act.wait_ge(flipped, 2)
            nc.scalar.activation(bias_2[:].rearrange("p h u -> p (h u)"), ps[:, 4:7, :].rearrange("p b n -> p (b n)"),
                                 ACT.Copy).then_inc(bias_done, 1)
            act.wait_ge(bias_done, 2)
            act.dma_start(t["bias_tiles_2"].rearrange("h p u -> p h u"), bias_2[:]).then_inc(bias_2_out, 16)
            act.wait_ge(bias_2_out, 16)
            s0 = SLABS["gate_pool"][0]
            with act.Fori(0, 8) as it:
                for half in range(2):
                    stage(2 * it + KT + half, (w_used, 2 * it + s0 + half + 1), ACT.Sigmoid, half, False)
            for k in range(KT):
                act.wait_ge(w_used, SLABS["query"][0] + k + 1)
                nc.scalar.activation(query[:, k, :], wide(k % 2), ACT.Copy, scale=P ** -0.5).then_inc(gate_free, 1)
            for half in range(2):
                act.wait_ge(staged[half], 16 * 12)
            n_tr = 0
            for i in range(NT):
                act.wait_ge(qk_done, HEADS * i) if i else act.wait_ge(gate_free, 2 + 4 * KT)
                act.wait_ge(masks_ready, 1)
                nc.scalar.activation(q_tile[0][:], query[:, :, i * P:(i + 1) * P], ACT.Copy).then_inc(qt_hi, 1)
                for g in range(2):
                    group = 2 * i + g
                    act.wait_ge(nmax_ready, group + 1)
                    for hd in range(4):
                        row = probs[:, hd, 0:(i + 1) * P]
                        nc.scalar.activation(row, row, ACT.Exp, bias=stat[:, 8 + hd:9 + hd],
                                             accum_out=stat[:, 12 + hd:13 + hd]).then_inc(exp_done, 1)
                    for j in range(i + 1):
                        act.wait_ge(tr_done, n_tr + 1)
                        if n_tr >= 2:
                            act.wait_ge(pv_done, n_tr - 1)
                        nc.scalar.activation(probs_t[n_tr % 2][0][:], ps[:, 4 + n_tr % 2, :], ACT.Copy).then_inc(pt_hi, 1)
                        n_tr += 1
                    act.wait_ge(pv_done, n_tr)
                    nc.scalar.activation(att[0][:, 4 * g:4 * g + 4, i * P:(i + 1) * P],
                                         ps[:, 6 + group % 2, :].rearrange("p (h q) -> p h q", h=4),
                                         ACT.Copy).then_inc(o_hi, 1)
            act.wait_ge(qk_done, HEADS * NT)
            for k in range(KT):
                if k >= 2:
                    act.wait_ge(merge_free, 2 + k - 1)
                for n in range(3):
                    act.dma_start(gated[k % 2][:, n, :], t["gates"][KT * n + k]).then_inc(gates_in[k % 2], 16)
            act.sem_inc(y_free, 2)
            act.wait_ge(merge_free, 2 + KT)
            act.dma_start(x[:], t["x"]).then_inc(x_landed, 16)
            act.dma_start(mem_in[:], t["mem"]).then_inc(mem_landed, 16)
            for k in range(KT):
                act.wait_ge(w_used, SLABS["mix_out"][0] + k + 1)
                post_square(0, k, wide(k % 2))
                nc.scalar.activation(y[:, k, :], wide(k % 2), ACT.Copy).then_inc(y_free, 1)
                if k == 1:
                    act.wait_ge(mem_landed, 16)
                    nc.scalar.activation(mem_sq[:], mem_in[:], ACT.Square).then_inc(mem_squared, 1)
                if k == 4:
                    act.wait_ge(mem_total, 1)
                    step(nc.scalar.activation(mem_rms[:], ps[:, 6, 0:M], ACT.Ln, bias=eps[:], scale=1.0 / D))
                    nc.scalar.activation(mem_rms[:], mem_rms[:], ACT.Exp, scale=-0.5).then_inc(mem_rs, 1)
                if k == 6:
                    act.wait_ge(mem_scaled, KT)
                    nc.scalar.activation(memn[0][:], mem_in[:], ACT.Copy).then_inc(mem_hi, 1)
            inverse(1)
            squares("mem_pre", lambda k: x[:, k, :], lambda k: (x_added, k + 1))
            act.wait_ge(w_used, SLABS["mem_value"][0] + 4)
            nc.scalar.activation(kmem[0][:], wide(0).rearrange("p (h m) -> p h m", h=MEM_HEADS), ACT.Copy).then_inc(mkv_hi, 1)
            nc.scalar.activation(vmem[0][:], wide(1).rearrange("p (j n) -> p j n", j=MT), ACT.Copy).then_inc(mkv_hi, 1)
            inverse(2)
            round_hi("mem_pre", normed[0])
            for n in range(MEM_HEADS):
                act.wait_ge(w_used, SLABS["mem_query"][0] + n + 1)
                nc.scalar.activation(qm[0][:, n, :], wide(n % 2), ACT.Copy, scale=P ** -0.5).then_inc(mq_hi, 1)
            for n in range(2 * MEM_HEADS):
                act.wait_ge(m_max, n + 1)
                if n >= 2:
                    act.wait_ge(m_tr, MT * (n - 1))
                for q in range(4):
                    nc.scalar.activation(mprobs[:, n % 2, q, :], wide(n % 2)[:, q * M:(q + 1) * M], ACT.Exp,
                                         bias=mstat[:, n % 2, 1, q:q + 1],
                                         accum_out=mstat[:, n % 2, 2, q:q + 1]).then_inc(m_exp, 1)
                for j in range(MT):
                    act.wait_ge(m_tr, MT * n + j + 1)
                    if n:
                        act.wait_ge(m_pv, MT * (n - 1) + j + 1)
                    nc.scalar.activation(mpt[j][0][:], ps[:, 4 + j, :], ACT.Copy).then_inc(m_pthi, 1)
                act.wait_ge(m_pv, MT * (n + 1))
                t0 = n % 2 * HALF
                nc.scalar.activation(om[0][:, n // 2, t0:t0 + HALF], ps[:, 6 + n % 2, :], ACT.Copy).then_inc(m_ohi, 1)
            act.wait_ge(m_olo, 2 * MEM_HEADS)
            for k in range(KT):
                act.wait_ge(*((w_used, SLABS["mem_out"][0] + k // 2 + 1) if k % 2 else (first_half, 4 + k // 2 + 1)))
                post_square(1, k, wide(k % 2))
                nc.scalar.activation(y[:, k, :], wide(k % 2), ACT.Copy).then_inc(y_free, 1)
            inverse(3)
            squares("ffn_pre", lambda k: x[:, k, :], lambda k: (x_added, KT + k + 1))
            inverse(4)
            round_hi("ffn_pre", normed[0])
            s0 = SLABS["ffn"][0]

            def ffn_hidden(c, tiles):
                for j in range(tiles):
                    act.wait_ge(w_used, 12 * c + s0 + 2 * j + 1)
                    act.wait_ge(f_lo, 4 * c + j + 1)
                    nc.scalar.activation(tmp[j % 2][:], wide(2 * (j % 2)), ACT.Silu).then_inc(f_silu, 1)
                    act.wait_ge(f_mul, 4 * c + j + 1)
                    nc.scalar.activation(hidden[0][:, j, :], tmp[j % 2][:], ACT.Copy).then_inc(f_hi, 1)

            with act.Fori(0, FF_TILES // CHUNK) as c:
                ffn_hidden(c, CHUNK)
            ffn_hidden(FF_TILES // CHUNK, FF_TILES % CHUNK)
            for k in range(KT):
                act.wait_ge(f_added, 8 + 8 * (FF_TILES // CHUNK) + k + 1)
                post_square(2, k, y[:, k, :])
            inverse(5)
            squares("attn_2", lambda k: x[:, k, :], lambda k: (x_added, 2 * KT + k + 1))
            for dst, name in ((cos, "c_cos"), (sin, "c_sin"), (halves, "c_halves")):
                act.dma_start(dst[:], t[name]).then_inc(tables_in, 16)
            inverse(6)
            round_hi("attn_2", normed[0])
            act.wait_ge(lam_sum, 1)
            nc.scalar.activation(lam_ab, lam_ab, ACT.Exp).then_inc(lam_exp, 1)
            s0 = SLABS["in_2"][0]
            for n, dst in enumerate((c_q[:, 0, :], c_q[:, 1, :], c_kv[:, 0, :])):
                act.wait_ge(w_used, s0 + n + 1)
                nc.scalar.activation(dst, wide(n % 2), ACT.Copy).then_inc(c_free, 1)
            squares("q_a", lambda k: c_q[:, k, :], lambda k: (c_free, k + 1))
            inverse(7, 2 * P)
            round_hi("q_a", cq[0])
            act.wait_ge(n_lo, PRE["kv_a"][1])
            squares("kv_a", lambda k: c_kv[:, k, :], lambda k: (c_free, 3))
            inverse(8, P)
            round_hi("kv_a", ckv[0])
            act.wait_ge(d_free, 2)
            nc.scalar.activation(k_rope_sq[:], k_rope[:], ACT.Square).then_inc(rope_sq, 1)
            act.wait_ge(n_lo, PRE["kv_a"][1] + 1)
            with act.Fori(0, DIFF_HEADS) as it:
                for e in range(2):
                    act.wait_ge(w_used, 2 * it + s0 + 5 + e + 1)
                    nc.scalar.activation(tmp[e][:], wide(1 - e), ACT.Square).then_inc(d_sq, 1)
                    act.wait_ge(d_tot, 2 * it + e + 1)
                    act.wait_ge(d_free, 2 * it + e + 1)
                    nc.scalar.activation(d_rms[e][:], wide(2 + e), ACT.Ln, bias=eps[:], scale=1.0 / 64).then_inc(d_ln, 1)
                    act.wait_ge(d_ln, 2 * it + e + 1)
                    nc.scalar.activation(d_rms[e][:], d_rms[e][:], ACT.Exp, scale=-0.5).then_inc(d_rs, 1)
                    act.wait_ge(d_free, 2 * it + e + 3)
                    act.dma_start(t["diff_qk"][2 * it + e], d_out[e][:]).then_inc(d_stored[e], 16)
            act.wait_ge(w_used, SLABS["diff_value"][0] + 4)
            for j in range(0, NT, 2):
                nc.scalar.activation(d_value[:, j, :], ps[:, j, :], ACT.Copy).then_inc(dv_act, 1)
            act.wait_ge(dv_act, 4)
            act.wait_ge(dv_dve, 4)
            for hd in range(DIFF_HEADS):
                act.dma_start(t["diff_v"][hd], d_value[:, :, hd * P:(hd + 1) * P]).then_inc(dv_stored, 16)
            for j in range(0, NT, 2):
                act.wait_ge(v_done, j + 1)
                nc.scalar.activation(v_value[:, j, :], ps[:, j, :], ACT.Copy).then_inc(v_act, 1)
            act.wait_ge(v_act, 4)
            act.wait_ge(v_dve, 4)
            for hd in range(MLA_HEADS):
                act.dma_start(t["mla_v"][hd], v_value[:, :, hd * P:(hd + 1) * P]).then_inc(v_stored, 16)
            for e in range(2 * MLA_HEADS):
                hd, is_q = e % MLA_HEADS, e >= MLA_HEADS
                if e == MLA_HEADS:
                    for p in range(2):
                        act.wait_ge(r_free, p + 1)
                        nc.scalar.activation(q_rope_sq[:, p, :], q_rope[:, p, :], ACT.Square).then_inc(rope_sq, 1)
                act.wait_ge(*((w_used, (SLABS["uq"][0] + 2) if is_q else SLABS["ukv"][0] + 1) if hd == MLA_HEADS - 1
                              else (g_done, (MLA_HEADS - 1) * is_q + hd + 1)))
                nc.scalar.activation(tmp[e % 2][:], wide(e % 2), ACT.Square).then_inc(g_sq, 1)
                act.wait_ge(g_tot, e + 1)
                if e >= 2:
                    act.wait_ge(g_roped, e - 1)
                step(nc.scalar.activation(g_rms[e % 2][:], wide(2 + e % 2), ACT.Ln, bias=eps[:],
                                     scale=1.0 / (P + ROPE)))
                nc.scalar.activation(g_rms[e % 2][:], g_rms[e % 2][:], ACT.Exp, scale=-0.5).then_inc(g_rs, 1)
                act.wait_ge(g_roped, e + 1)
                r0 = ROPE * (hd % 2) if is_q else 0
                act.dma_start(t["mla_nope"][e], g_nope[e % 2][:]).then_inc(g_stored[e % 2], 16)
                act.dma_start(t["mla_rope"][e], g_rope[e % 2][r0:r0 + ROPE, :]).then_inc(g_stored[e % 2], 16)
            def weighed(hn, g, dst):
                group = 2 * hn + g
                for j in range(NT):
                    act.wait_ge(a_tr, 8 * group + j + 1)
                    act.wait_ge(a_pv, 8 * group + j + 15)
                    nc.scalar.activation(pt[j % 2][0][:], ps[:, 4 + j % 2, :], ACT.Copy).then_inc(a_pthi, 1)
                act.wait_ge(a_pv, 8 * group + 24)
                nc.scalar.activation(o_stage[:, g, :], ps[:, 6 + g, :], ACT.Copy).then_inc(a_out, 1)
                act.wait_ge(a_out, group + 3)
                act.dma_start(dst[:, g * HALF:(g + 1) * HALF], o_stage[:, g, :]).then_inc(o_stored, 16)

            act.sem_inc(a_exp, 2)
            act.sem_inc(a_out, 2)
            with act.Fori(0, MLA_HEADS) as hn:
                act.wait_ge(a_raw, 80 * hn + 80)
                act.wait_ge(a_pv, 16 * hn + 16)
                for (hi, _), src in zip(m_parts, m_raw):
                    nc.scalar.activation(hi[:], src[:], ACT.Copy).then_inc(a_hi, 1)
                for g in range(2):
                    for q in range(4):
                        act.wait_ge(a_max, 8 * hn + 4 * g + q + 1)
                        nc.scalar.activation(m_probs2[g][:, q, :], wide(q % 2), ACT.Exp, bias=mstat[:, g, 1, q:q + 1],
                                             scale=(P + ROPE) ** -0.5,
                                             accum_out=mstat[:, g, 2, q:q + 1]).then_inc(a_exp, 1)
                for g in range(2):
                    weighed(hn, g, t["heads_out"][hn])
                act.wait_ge(o_stored, 32 * hn + 32)
            with act.Fori(0, DIFF_HEADS) as hn:
                act.wait_ge(e_raw_in, 48 * hn + 48)
                act.wait_ge(a_pv, 16 * hn + 16 * MLA_HEADS + 16)
                for (hi, _), src in zip(e_parts, e_raw):
                    nc.scalar.activation(hi[:], src[:], ACT.Copy).then_inc(e_hi, 1)
                for g in range(2):
                    act.wait_ge(e_max, 2 * hn + g + 1)
                    for q in range(4):
                        for m in range(2):
                            row = e_probs[g][:, m, q, :]
                            nc.scalar.activation(row, row, ACT.Exp, bias=e_stat[:, g, 3, m, q:q + 1],
                                                 accum_out=e_stat[:, g, 4, m, q:q + 1]).then_inc(e_exp, 1)
                for g in range(2):
                    weighed(hn + MLA_HEADS, g, t["heads_out"][hn + MLA_HEADS])
                act.wait_ge(o_stored, 32 * hn + 32 * MLA_HEADS + 32)
            act.wait_ge(a_pv, 16 * KT + 16)
            for k in range(KT):
                act.dma_start(o_in[:, k, :], t["heads_out"][k]).then_inc(o_landed, 16)
            act.wait_ge(o_landed, 16 * KT)
            for k in range(MLA_HEADS):
                nc.scalar.activation(o_all[0][:, k, :], o_in[:, k, :], ACT.Copy).then_inc(s_hi, 1)
            for n in range(DIFF_HEADS):
                if n >= 2:
                    act.wait_ge(s_tot, n - 1)
                nc.scalar.activation(tmp[n % 2][:], o_in[:, MLA_HEADS + n, :], ACT.Square).then_inc(s_sq, 1)
                act.wait_ge(s_tot, n + 1)
                if n >= 2:
                    act.wait_ge(s_scaled, n - 1)
                step(nc.scalar.activation(o_rms[n % 2][:], wide(2 + n % 2), ACT.Ln, bias=eps[:], scale=1.0 / P))
                nc.scalar.activation(o_rms[n % 2][:], o_rms[n % 2][:], ACT.Exp, scale=-0.5).then_inc(s_rs, 1)
            for n in range(DIFF_HEADS):
                act.wait_ge(s_scaled, n + 1)
                nc.scalar.activation(o_all[0][:, MLA_HEADS + n, :], o_in[:, MLA_HEADS + n, :], ACT.Copy).then_inc(s_hi, 1)
            squares("mlp_2", lambda k: x[:, k, :], lambda k: (x_added, 3 * KT + k + 1))
            inverse(9)
            round_hi("mlp_2", normed[0])
            s0 = SLABS["mlp_2"][0]
            with act.Fori(0, FF2_TILES // CHUNK) as c:
                for j in range(CHUNK):
                    act.wait_ge(w_used, 8 * c + s0 + j + 1)
                    act.wait_ge(u_lo, 4 * c + j + 1)
                    nc.scalar.activation(tmp[j % 2][:], wide(j), ACT.Relu).then_inc(u_relu, 1)
                    act.wait_ge(u_sq, 4 * c + j + 1)
                    nc.scalar.activation(hidden[0][:, j, :], tmp[j % 2][:], ACT.Copy).then_inc(u_hi, 1)
            for m in range(KT):
                act.wait_ge(u_added, 8 * (FF2_TILES // CHUNK) + m + 1)
                act.dma_start(out[:, m, :], x[:, m, :]).then_inc(stored, 16)
            act.wait_ge(stored, 16 * KT)
        @block.vector
        def _(dve):
            step = Chain(dve, dve_step)
            tt, ts, stt = nc.vector.tensor_tensor, nc.vector.tensor_scalar, nc.vector.scalar_tensor_tensor

            def add_square(post, k):
                dve.wait_ge(n_post_sq, KT * post + k + 1)
                if k >= 2:
                    dve.wait_ge(n_acc, 7 * post + k - 1)
                tt(acc[:], acc[:], tmp[k % 2][:], ALU.add).then_inc(n_acc, 1)

            def scaled(r, name, src, dst):
                tiles, before = PRE[name]

                def rest(k):
                    dve.wait_ge(n_hi, before + k + 1)
                    tt(dst[1][:, k, :], tmp[k % 2][:], dst[0][:, k, :].bitcast(F32), ALU.subtract).then_inc(n_lo, 1)

                dve.wait_ge(n_rs, r + 1)
                for k in range(tiles):
                    if k >= 2:
                        dve.wait_ge(n_lo, before + k - 1)
                    stt(tmp[k % 2][:], src[:, k, :], col(name, k), acc[:], ALU.mult, ALU.mult).then_inc(n_tmp, 1)
                    if k:
                        rest(k - 1)
                rest(tiles - 1)

            def residual(r, gain):
                dve.wait_ge(n_rs, r + 1)
                for k in range(KT):
                    step(stt(y[:, k, :], y[:, k, :], col(gain, k), acc[:], ALU.mult, ALU.mult))
                    tt(x[:, k, :], x[:, k, :], y[:, k, :], ALU.add).then_inc(x_added, 1)

            nc.vector.memset(eps[:], EPS)
            step(nc.vector.memset(ones[:], 1.0))
            dve.wait_ge(consts_in, 16 * N_CONSTS)
            nc.vector.tensor_copy(ident16[:], ident[:]).then_inc(dve_consts, 1)
            dve.wait_ge(dve_consts, 1)
            scaled(0, "mix_pre", x_in, h1)
            dve.sem_inc(in_free, 2)

            def pool_window(g):
                cur = u[:, g, :]
                for e in range(g + 1):
                    n, nxt = 1 << e, win[e % 2]
                    nc.vector.tensor_copy(nxt[:, 0:n], cur[:, 0:n])
                    step(tt(nxt[:, n:S], cur[:, n:S], cur[:, 0:S - n], ALU.add))
                    cur = nxt[:]
                step(tt(cur[:, 0:16], cur[:, 0:16], pool_fix[:, g, :], ALU.mult))
                step(stt(tmp[0][:], cur, 1.0 / (2 << g), u[:, g, :], ALU.mult, ALU.subtract))
                step(nc.vector.tensor_copy(pooled[0][:, g, :], tmp[0][:]))
                tt(pooled[1][:, g, :], tmp[0][:], pooled[0][:, g, :].bitcast(F32), ALU.subtract).then_inc(pooled_ready, 1)

            for k in range(4):
                dve.wait_ge(w_used, SLABS["mix_in"][0] + k + 1)
                nc.vector.tensor_copy(u[:, k, :], wide(k % 2)).then_inc(in_free, 1)
            for n, (hi, lo) in enumerate(((kidx[0][:], kidx[1][:]), (qidx[0][:, 0, :], qidx[1][:, 0, :]),
                                          (qidx[0][:, 1, :], qidx[1][:, 1, :]), (key[0][:], key[1][:]))):
                dve.wait_ge(in_hi, n + 1)
                tt(lo, wide(n % 2), hi.bitcast(F32), ALU.subtract).then_inc(in_free, 1)
                dve.wait_ge(in_free, 2 + 4 + n + 1)
                pool_window(n)
            for b in range(3):
                m = min(3, NT - 3 * b)
                dve.wait_ge(value_done, 3 * b + m)
                nc.vector.tensor_copy(value_raw[:, 3 * b:3 * b + m, :], ps[:, 4 + b, 0:m * VW].rearrange(
                    "p (j n) -> p j n", j=m)).then_inc(value_free, 1)
            for g in range(POOL_GROUPS):
                dve.wait_ge(*((pool_done, g + 1) if g < 2 else (w_used, SLABS["value_pool"][0] + g - 1)))
                step(ts(tmp[g % 2][:], wide(g % 2), col("pool_scale", g), None, ALU.mult))
                step(nc.vector.tensor_copy(mixed[0][:, g, :], tmp[g % 2][:]))
                tt(mixed[1][:, g, :], tmp[g % 2][:], mixed[0][:, g, :].bitcast(F32), ALU.subtract).then_inc(mix_free, 1)
            unit = 0
            for i in reversed(range(2, NT)):
                sc = score[:, score_at[i]:score_at[i] + (i + 1) * P]
                for hd in range(IDX_HEADS):
                    dve.wait_ge(idx_relu, unit + 1)
                    part, w = tmp[unit % 2][:, 0:(i + 1) * P], value_raw[:, i, P + hd:P + hd + 1]
                    if hd == 0:
                        ins = ts(sc, part, w, None, ALU.mult)
                    else:
                        dve.wait_ge(idx_added, unit)
                        ins = stt(sc, part, w, sc, ALU.mult, ALU.add)
                    ins.then_inc(idx_added, 1)
                    unit += 1
                dve.wait_ge(idx_added, unit)
                step(tt(sc[:, i * P:(i + 1) * P], sc[:, i * P:(i + 1) * P], tri[:], ALU.add))
            for both in ((7, 2), (6, 3), (5, 4)):
                scs = [score[:, score_at[i]:score_at[i] + (i + 1) * P] for i in both]
                for _ in range(ROUNDS):
                    found = step.n
                    for e, sc in enumerate(scs):
                        if step.n > 2:
                            dve.wait_ge(dve_step, step.n - 1)
                        step.n += 1
                        nc.vector.max(top8[:, e, :], sc).then_inc(dve_step, 1)
                    for e, sc in enumerate(scs):
                        dve.wait_ge(dve_step, found + e + 1)
                        step.n += 1
                        nc.vector.match_replace(sc, top8[:, e, :], sc, TAKEN).then_inc(dve_step, 1)
            dve.wait_ge(dve_step, step.n)
            for i in range(2, NT):
                ts(mask[:, mask_at[i]:mask_at[i] + (i + 1) * P], score[:, score_at[i]:score_at[i] + (i + 1) * P],
                   TAKEN, NEG, ALU.not_equal, ALU.mult)
            nc.vector.memset(mask[:, mask_at[1]:mask_at[1] + P], 0.0)
            nc.vector.tensor_copy(mask[:, mask_at[1] + P:mask_at[1] + 2 * P], tri[:])
            nc.vector.tensor_copy(mask[:, 0:P], tri[:]).then_inc(masks_ready, 1)
            dve.wait_ge(idx_done, unit)
            step(nc.vector.tensor_copy(value[0][:], value_raw[:, :, 0:P]))
            tt(value[1][:], value_raw[:, :, 0:P], value[0][:].bitcast(F32), ALU.subtract).then_inc(value_split, 1)
            dve.wait_ge(bias_done, 1)
            dve.wait_ge(masks_ready, 1)
            n_tr = 0
            for i in range(NT):
                n = (i + 1) * P
                late = max(0, i - 1) * P
                dve.wait_ge(qt_hi, i + 1)
                tt(q_tile[1][:], query[:, :, i * P:(i + 1) * P], q_tile[0][:].bitcast(F32),
                   ALU.subtract).then_inc(qt_lo, 1)
                for g in range(2):
                    group = 2 * i + g
                    if group:
                        dve.wait_ge(tr_done, n_tr)
                    for hd in range(4 * g, 4 * g + 4):
                        unit = HEADS * i + hd
                        h = hd - 4 * g
                        dve.wait_ge(qk_done, unit + 1)
                        if late:
                            nc.vector.tensor_tensor_reduce(
                                probs[:, h, 0:late], wide(unit % 2)[:, 0:late], bias[:, hd, 0:1].broadcast_to([P, late]),
                                1.0, TAKEN, ALU.add, ALU.max, stat[:, 4 + h:5 + h])
                        nc.vector.tensor_tensor_reduce(
                            probs[:, h, late:n], wide(unit % 2)[:, late:n], bias[:, hd, 2 * P - (n - late):2 * P],
                            1.0, TAKEN, ALU.add, ALU.max, stat[:, h:1 + h]).then_inc(logits_ready, 1)
                    dve.wait_ge(logits_ready, HEADS * i + 4 * g + 4)
                    if late:
                        step(tt(stat[:, 0:4], stat[:, 0:4], stat[:, 4:8], ALU.max))
                    ts(stat[:, 8:12], stat[:, 0:4], -1.0, None, ALU.mult).then_inc(nmax_ready, 1)
                    dve.wait_ge(exp_done, 4 * (group + 1))
                    step(nc.vector.reciprocal(stat[:, 16:20], stat[:, 12:16]))
                    for h in range(4):
                        ins = ts(probs[:, h, 0:n], probs[:, h, 0:n], stat[:, 16 + h:17 + h], None, ALU.mult)
                    ins.then_inc(probs_ready, 1)
                    for j in range(i + 1):
                        dve.wait_ge(pt_hi, n_tr + 1)
                        tt(probs_t[n_tr % 2][1][:], ps[:, 4 + n_tr % 2, :], probs_t[n_tr % 2][0][:].bitcast(F32),
                           ALU.subtract).then_inc(pt_lo, 1)
                        n_tr += 1
                    dve.wait_ge(o_hi, group + 1)
                    tt(att[1][:, 4 * g:4 * g + 4, i * P:(i + 1) * P],
                       ps[:, 6 + group % 2, :].rearrange("p (h q) -> p h q", h=4),
                       att[0][:, 4 * g:4 * g + 4, i * P:(i + 1) * P].bitcast(F32), ALU.subtract).then_inc(o_lo, 1)
            dve.sem_inc(merge_free, 2)
            for k in range(KT):
                pool_part, pool_gate, attn_gate = (gated[k % 2][:, n, :] for n in range(3))
                dve.wait_ge(gates_in[k % 2], 48 * (k // 2 + 1))
                tt(pool_part, pool_part, pool_gate, ALU.mult)
                dve.wait_ge(w_used, SLABS["proj_attn"][0] + k + 1)
                step(tt(attn_gate, wide(k % 2), attn_gate, ALU.mult))
                step(tt(pool_part, pool_part, attn_gate, ALU.add))
                step(nc.vector.tensor_copy(merged[0][:, k, :], pool_part))
                tt(merged[1][:, k, :], pool_part, merged[0][:, k, :].bitcast(F32), ALU.subtract).then_inc(merge_free, 1)
            for k in range(1, KT):
                add_square(0, k)
                if k == 4:
                    dve.wait_ge(mem_rs, 1)
                    for e in range(KT):
                        stt(mem_in[:, e, :], mem_in[:, e, :], col("mem_kv", e), mem_rms[:], ALU.mult,
                            ALU.mult).then_inc(mem_scaled, 1)
            dve.wait_ge(mem_hi, 1)
            tt(memn[1][:], mem_in[:], memn[0][:].bitcast(F32), ALU.subtract).then_inc(mem_lo, 1)
            dve.wait_ge(x_landed, 16)
            dve.wait_ge(y_free, 2 + KT)
            residual(1, "mix_post")
            dve.wait_ge(mkv_hi, 1)
            tt(kmem[1][:], wide(0).rearrange("p (h m) -> p h m", h=MEM_HEADS), kmem[0][:].bitcast(F32),
               ALU.subtract).then_inc(mkv_lo, 1)
            dve.wait_ge(mkv_hi, 2)
            tt(vmem[1][:], wide(1).rearrange("p (j n) -> p j n", j=MT), vmem[0][:].bitcast(F32),
               ALU.subtract).then_inc(mkv_lo, 1)
            scaled(2, "mem_pre", x, normed)
            dve.sem_inc(mq_lo, 2)
            for n in range(MEM_HEADS):
                dve.wait_ge(mq_hi, n + 1)
                stt(qm[1][:, n, :], wide(n % 2), P ** -0.5, qm[0][:, n, :].bitcast(F32), ALU.mult,
                    ALU.subtract).then_inc(mq_lo, 1)
            for n in range(2 * MEM_HEADS):
                biggest, minus, total, inv = (mstat[:, n % 2, e, :] for e in range(4))
                dve.wait_ge(m_qk, n + 1)
                step(nc.vector.tensor_reduce(biggest, wide(n % 2).rearrange("p (q m) -> p q m", q=4), AX.X, ALU.max))
                ts(minus, biggest, -1.0, None, ALU.mult).then_inc(m_max, 1)
                dve.wait_ge(m_exp, 4 * (n + 1))
                step(nc.vector.reciprocal(inv, total))
                tt(mprobs[:, n % 2], mprobs[:, n % 2], inv.unsqueeze(2).broadcast_to([P, 4, M]),
                   ALU.mult).then_inc(m_probs, 1)
                for j in range(MT):
                    dve.wait_ge(m_pthi, MT * n + j + 1)
                    tt(mpt[j][1][:], ps[:, 4 + j, :], mpt[j][0][:].bitcast(F32), ALU.subtract).then_inc(m_ptlo, 1)
                dve.wait_ge(m_ohi, n + 1)
                t0 = n % 2 * HALF
                tt(om[1][:, n // 2, t0:t0 + HALF], ps[:, 6 + n % 2, :], om[0][:, n // 2, t0:t0 + HALF].bitcast(F32),
                   ALU.subtract).then_inc(m_olo, 1)
            for k in range(1, KT):
                add_square(1, k)
            dve.wait_ge(y_free, 2 + 2 * KT)
            residual(3, "mem_post")
            scaled(4, "ffn_pre", x, normed)
            dve.sem_inc(f_lo, 2)
            nc.vector.memset(y[:], 0.0).then_inc(y_zero, 1)
            dve.wait_ge(y_zero, 1)
            dve.sem_inc(f_added, 8)
            s0 = SLABS["ffn"][0]

            def ffn_hidden(c, tiles, down_before):
                for j in range(tiles):
                    part = tmp[j % 2]
                    dve.wait_ge(w_used, 12 * c + s0 + 2 * j + 2)
                    dve.wait_ge(f_silu, 4 * c + j + 1)
                    tt(part[:], part[:], wide(2 * (j % 2) + 1), ALU.mult).then_inc(f_mul, 1)
                    dve.wait_ge(f_hi, 4 * c + j + 1)
                    tt(hidden[1][:, j, :], part[:], hidden[0][:, j, :].bitcast(F32), ALU.subtract).then_inc(f_lo, 1)
                per = 8 // tiles
                for m in range(KT):
                    if m % per == per - 1:
                        dve.wait_ge(w_used, 12 * c + s0 + 2 * tiles + m // per + 1)
                    else:
                        dve.wait_ge(first_half, down_before + m - m // per + 1)
                    tt(y[:, m, :], y[:, m, :], wide(m % 4), ALU.add).then_inc(f_added, 1)

            with dve.Fori(0, FF_TILES // CHUNK) as c:
                ffn_hidden(c, CHUNK, 4 * c + 8)
            ffn_hidden(FF_TILES // CHUNK, FF_TILES % CHUNK, 4 * (FF_TILES // CHUNK) + 8)
            for k in range(1, KT):
                add_square(2, k)
            residual(5, "ffn_post")
            lam = cols[:, COLS["lambda"][0]:COLS["lambda"][0] + 256].rearrange("p (v n) -> p v n", v=4)
            ts(col("diff_q"), col("diff_q"), 64 ** -0.5, None, ALU.mult)
            ts(col("diff_out"), col("diff_out"), 1.0 - LAM_INIT, None, ALU.mult)
            tt(lam[:, 0, :], lam[:, 0, :], lam[:, 1, :], ALU.mult)
            step(tt(lam[:, 2, :], lam[:, 2, :], lam[:, 3, :], ALU.mult))
            nc.vector.tensor_reduce(lam_ab[:, 0:1], lam[:, 0, :], AX.X, ALU.add)
            nc.vector.tensor_reduce(lam_ab[:, 1:2], lam[:, 2, :], AX.X, ALU.add).then_inc(lam_sum, 1)
            scaled(6, "attn_2", x, normed)
            dve.wait_ge(lam_exp, 1)
            step(tt(minus_lam, lam_ab[:, 1:2], lam_ab[:, 0:1], ALU.subtract))
            step(ts(minus_lam, minus_lam, -LAM_INIT, None, ALU.add))
            s0 = SLABS["in_2"][0]
            dve.wait_ge(tables_in, 48)
            dve.wait_ge(w_used, s0 + 4)
            tt(k_rope[:], wide(1), cos[:], ALU.mult).then_inc(d_free, 1)
            scaled(7, "q_a", c_q, cq)
            dve.wait_ge(w_used, s0 + 5)
            dve.wait_ge(n_lo, PRE["kv_a"][1])
            dve.wait_ge(n_sq, PRE["kv_a"][1] + 1)
            step(tt(tmp[1][:], wide(0), sin[:], ALU.mult))
            tt(k_rope[:], k_rope[:], tmp[1][:], ALU.add).then_inc(d_free, 1)
            scaled(8, "kv_a", c_kv, ckv)
            for part, gain in enumerate(("diff_q", "diff_k")):
                with dve.Fori(2 * part, 2 * part + 2) as it:
                    for e in range(2):
                        dve.wait_ge(d_rs, 2 * it + e + 1)
                        stt(d_out[e][:], wide(1 - e), col(gain), d_rms[e][:], ALU.mult, ALU.mult).then_inc(d_free, 1)
                    for e in range(2):
                        dve.wait_ge(d_stored[e], 16 * it + 16)
            dve.wait_ge(w_used, SLABS["diff_value"][0] + 4)
            for j in range(1, NT, 2):
                nc.vector.tensor_copy(d_value[:, j, :], ps[:, j, :]).then_inc(dv_dve, 1)
            for j in range(1, NT, 2):
                dve.wait_ge(v_done, j + 1)
                nc.vector.tensor_copy(v_value[:, j, :], ps[:, j, :]).then_inc(v_dve, 1)
            for e in range(2 * MLA_HEADS):
                hd, is_q = e % MLA_HEADS, e >= MLA_HEADS
                if e == MLA_HEADS:
                    for p in range(2):
                        dve.wait_ge(r_done, 2 * p + 1)
                        tt(q_rope[:, p, :], wide(0), cos[:], ALU.mult)
                        dve.wait_ge(*((w_used, SLABS["uq"][0] + 1) if p else (r_done, 2)))
                        step(tt(turned[:], wide(1), sin[:], ALU.mult))
                        tt(q_rope[:, p, :], q_rope[:, p, :], turned[:], ALU.add).then_inc(r_free, 1)
                        dve.wait_ge(r_free, p + 1)
                dve.wait_ge(g_rs, e + 1)
                if e >= 2:
                    dve.wait_ge(g_stored[e % 2], 32 * (e // 2))
                which = "mla_q" if is_q else "mla_k"
                stt(g_nope[e % 2][:], wide(e % 2), col(which + "_nope"), g_rms[e % 2][:], ALU.mult,
                    ALU.mult).then_inc(g_free, 1)
                r0 = ROPE * (hd % 2) if is_q else 0
                rope = q_rope[r0:r0 + ROPE, hd // 2, :] if is_q else k_rope[0:ROPE, :]
                stt(g_rope[e % 2][r0:r0 + ROPE, :], rope, col(which + "_rope")[r0:r0 + ROPE, :],
                    g_rms[e % 2][r0:r0 + ROPE, :], ALU.mult, ALU.mult).then_inc(g_roped, 1)
            def weighed(hn, g):
                group = 2 * hn + g
                for j in range(NT):
                    dve.wait_ge(a_pthi, 8 * group + j + 1)
                    tt(pt[j % 2][1][:], ps[:, 4 + j % 2, :], pt[j % 2][0][:].bitcast(F32), ALU.subtract).then_inc(a_ptlo, 1)

            dve.sem_inc(a_ptlo, 2)
            dve.sem_inc(a_lo, 5)
            with dve.Fori(0, MLA_HEADS) as hn:
                for n, ((hi, lo), src) in enumerate(zip(m_parts, m_raw)):
                    dve.wait_ge(a_hi, 5 * hn + n + 1)
                    tt(lo[:], src[:], hi[:].bitcast(F32), ALU.subtract).then_inc(a_lo, 1)
                for g in range(2):
                    biggest, minus, total, inv = (mstat[:, g, e, :] for e in range(4))
                    for q in range(4):
                        dve.wait_ge(a_qk, 8 * hn + 4 * g + q + 1)
                        nc.vector.tensor_reduce(biggest[:, q:q + 1], wide(q % 2), AX.X, ALU.max).then_inc(a_red, 1)
                        dve.wait_ge(a_red, 8 * hn + 4 * g + q + 1)
                        ts(minus[:, q:q + 1], biggest[:, q:q + 1], -(P + ROPE) ** -0.5, None, ALU.mult).then_inc(a_max, 1)
                    dve.wait_ge(a_exp, 8 * hn + 4 * g + 6)
                    nc.vector.reciprocal(inv, total).then_inc(a_inv, 1)
                    dve.wait_ge(a_inv, 2 * hn + g + 1)
                    for q in range(4):
                        ins = ts(m_probs2[g][:, q, :], m_probs2[g][:, q, :], inv[:, q:q + 1], None, ALU.mult)
                    ins.then_inc(a_probs, 1)
                for g in range(2):
                    weighed(hn, g)
            dve.wait_ge(a_pv, 16 * MLA_HEADS + 16)
            nc.vector.memset(e_stat[:], TAKEN).then_inc(e_red, 2)
            dve.wait_ge(e_red, 2)
            dve.sem_inc(e_lo, 3)
            with dve.Fori(0, DIFF_HEADS) as hn:
                for n, ((hi, lo), src) in enumerate(zip(e_parts, e_raw)):
                    dve.wait_ge(e_hi, 3 * hn + n + 1)
                    tt(lo[:], src[:], hi[:].bitcast(F32), ALU.subtract).then_inc(e_lo, 1)
                dve.wait_ge(e_bias_in, 16 * hn + 16)
                for g in range(2):
                    past, near, future, minus, total, inv = (e_stat[:, g, e] for e in range(6))
                    for q in range(4):
                        i = 4 * g + q
                        a0, a1 = max(0, i - 1) * P, min(NT, i + 2) * P
                        b0 = P if i == 0 else 0
                        for m in range(2):
                            dve.wait_ge(e_qk, 16 * hn + 8 * g + 2 * q + m + 1)
                            ts(e_turn[:, g, m, q:q + 1], zero[:], 0.0, None, ALU.add)
                            row = e_probs[g][:, m, q, :]

                            def biased(lo, hi, bias, biggest):
                                return nc.vector.tensor_tensor_reduce(
                                    row[:, lo:hi], wide(m)[:, lo:hi], bias, 1.0, TAKEN, ALU.add, ALU.max,
                                    biggest[:, m, q:q + 1])

                            if a0:
                                biased(0, a0, e_bias[:, 0:1].broadcast_to([P, a0]), past)
                            if a1 < S:
                                biased(a1, S, e_bias[:, 3 * P - 1:3 * P].broadcast_to([P, S - a1]), future)
                            biased(a0, a1, e_bias[:, b0:b0 + a1 - a0], near).then_inc(e_red, 1)
                    dve.wait_ge(e_red, 16 * hn + 8 * g + 10)
                    tt(near, near, past, ALU.max).then_inc(a_red, 1)
                    dve.wait_ge(a_red, 6 * hn + 3 * g + 8 * MLA_HEADS + 1)
                    tt(near, near, future, ALU.max).then_inc(a_red, 1)
                    dve.wait_ge(a_red, 6 * hn + 3 * g + 8 * MLA_HEADS + 2)
                    ts(minus, near, -1.0, None, ALU.mult).then_inc(e_max, 1)
                    dve.wait_ge(e_exp, 16 * hn + 8 * g + 8)
                    nc.vector.reciprocal(inv, total).then_inc(a_inv, 1)
                    dve.wait_ge(a_inv, 2 * hn + g + 2 * MLA_HEADS + 1)
                    ts(inv[:, 1, :], inv[:, 1, :], minus_lam, None, ALU.mult).then_inc(a_red, 1)
                    dve.wait_ge(a_red, 6 * hn + 3 * g + 8 * MLA_HEADS + 3)
                    for q in range(4):
                        ts(e_probs[g][:, 1, q, :], e_probs[g][:, 1, q, :], inv[:, 1, q:q + 1], None,
                           ALU.mult).then_inc(e_weighed, 1)
                    for q in range(4):
                        dve.wait_ge(e_weighed, 8 * hn + 4 * g + q + 1)
                        ins = stt(e_probs[g][:, 0, q, :], e_probs[g][:, 0, q, :], inv[:, 0, q:q + 1],
                                  e_probs[g][:, 1, q, :], ALU.mult, ALU.add)
                    ins.then_inc(a_probs, 1)
                for g in range(2):
                    weighed(hn + MLA_HEADS, g)
            for k in range(MLA_HEADS):
                dve.wait_ge(s_hi, k + 1)
                tt(o_all[1][:, k, :], o_in[:, k, :], o_all[0][:, k, :].bitcast(F32), ALU.subtract).then_inc(s_lo, 1)
            for n in range(DIFF_HEADS):
                dve.wait_ge(s_rs, n + 1)
                k = MLA_HEADS + n
                stt(o_in[:, k, :], o_in[:, k, :], col("diff_out"), o_rms[n % 2][:], ALU.mult, ALU.mult).then_inc(s_scaled, 1)
            for n in range(DIFF_HEADS):
                k = MLA_HEADS + n
                dve.wait_ge(s_hi, k + 1)
                tt(o_all[1][:, k, :], o_in[:, k, :], o_all[0][:, k, :].bitcast(F32), ALU.subtract).then_inc(s_lo, 1)
            for k in range(KT):
                dve.wait_ge(w_used, SLABS["out_2"][0] + k + 1)
                tt(x[:, k, :], x[:, k, :], wide(k % 2), ALU.add).then_inc(x_added, 1)
            scaled(9, "mlp_2", x, normed)
            dve.sem_inc(u_lo, 2)
            dve.sem_inc(u_added, 8)
            s0 = SLABS["mlp_2"][0]
            down0 = 4 + 4 + 4 * (FF_TILES // CHUNK) + 6
            with dve.Fori(0, FF2_TILES // CHUNK) as c:
                for j in range(CHUNK):
                    part = tmp[j % 2]
                    dve.wait_ge(u_relu, 4 * c + j + 1)
                    tt(part[:], part[:], part[:], ALU.mult).then_inc(u_sq, 1)
                    dve.wait_ge(u_hi, 4 * c + j + 1)
                    tt(hidden[1][:, j, :], part[:], hidden[0][:, j, :].bitcast(F32), ALU.subtract).then_inc(u_lo, 1)
                for m in range(KT):
                    if m % 2:
                        dve.wait_ge(w_used, 8 * c + s0 + 4 + m // 2 + 1)
                    else:
                        dve.wait_ge(first_half, 4 * c + down0 + m // 2 + 1)
                    tt(x[:, m, :], x[:, m, :], wide(m % 4), ALU.add).then_inc(u_added, 1)


def slabs_of(w, kt):
    n = w.shape[1] // P
    w = w.reshape(kt, P, n, P).transpose(2, 0, 1, 3).reshape(n * kt // 8, 8, P, P)
    return w.transpose(0, 2, 1, 3).reshape(-1, P, 1024)


def moving_slabs(w):
    return w.reshape(4, 2, P, 512).transpose(0, 2, 1, 3).reshape(4, P, 1024)


def pack_weights(a):
    out = np.zeros((N_SLABS, P, 1024), np.float32)

    def put(name, slabs):
        first, n = SLABS[name]
        assert slabs.shape[0] == n, (name, slabs.shape)
        out[first:first + n] = slabs

    w = a["w_in"]
    pool_w, q_w, k_w, v_w, qi_w, ki_w, wi_w, gp_w, ga_w = np.split(
        w, np.cumsum((512, 1024, 128, 128, 256, 64, 4, 1024)), axis=1)
    put("mix_in", slabs_of(np.concatenate([pool_w, ki_w, ki_w, qi_w, k_w], axis=1), KT))
    vw = np.concatenate([v_w, wi_w], axis=1).reshape(2, 4, P, VW).transpose(0, 2, 1, 3).reshape(2, P, 4 * VW)
    first = SLABS["value_pool"][0]
    out[first:first + 2, :, 0:4 * VW] = vw
    for g in range(POOL_GROUPS):
        b = 4 * VW + g % 3 * P
        out[first + g // 3, :, b:b + P] = a["pool_w"][g]
    put("proj_pool", slabs_of(a["w_proj_pool"], 4))
    put("gate_pool", slabs_of(gp_w, KT))
    put("gate_attn", slabs_of(ga_w, KT))
    put("query", slabs_of(q_w, KT))
    put("proj_attn", slabs_of(a["w_proj_attn"], KT))
    put("mix_out", slabs_of(a["w_out"], KT))
    w = a["w_kv_mem"]
    put("mem_key", slabs_of(w[:, :MEM_HEADS * P], KT))
    put("mem_value", moving_slabs(w[:, MEM_HEADS * P:]))
    put("mem_query", slabs_of(a["w_q_mem"], KT))
    put("mem_out", slabs_of(a["w_o_mem"], 4))
    gate, up = slabs_of(a["w_gate_up"][:, :FF], KT), slabs_of(a["w_gate_up"][:, FF:], KT)
    parts = []
    for c in range(0, FF_TILES, CHUNK):
        n = min(CHUNK, FF_TILES - c)
        parts.append(np.stack([gate[c:c + n], up[c:c + n]], axis=1).reshape(2 * n, P, 1024))
        parts.append(slabs_of(a["w_down"][c * P:(c + n) * P], n))
    put("ffn", np.concatenate(parts))
    w = a["w_in_2"][0]
    cq, ckv, kr, dq, dk, dv = np.split(w, np.cumsum((256, 128, 64, 512, 512)), axis=1)
    kr2 = np.roll(kr, 32, axis=1)
    put("in_2", slabs_of(np.concatenate([cq, ckv, kr, kr, kr2, kr2, dq, dk], axis=1), KT))
    put("diff_value", moving_slabs(dv))
    w = a["w_ukv_2"][0].reshape(P, MLA_HEADS, 2, P)
    put("ukv", np.concatenate([w[:, :, 0].reshape(P, 512), w[:, :, 1].reshape(P, 512)], axis=1)[None])
    w = a["w_uq_2"][0].reshape(2 * P, MLA_HEADS, P + ROPE)
    rope = w[:, :, P:]
    turned = np.roll(rope, 32, axis=2)
    order = [v[:, 2 * p:2 * p + 2].reshape(2 * P, P) for p in range(2) for v in (rope, turned)]
    put("uq", slabs_of(np.concatenate(order + [w[:, :, :P].reshape(2 * P, 512)], axis=1), 2))
    put("out_2", slabs_of(a["w_out_2"][0], KT))
    up = slabs_of(a["w_up_2"][0], KT)
    parts = []
    for c in range(0, FF2_TILES, CHUNK):
        parts += [up[c:c + CHUNK], slabs_of(a["w_down_2"][0][c * P:(c + CHUNK) * P], CHUNK)]
    put("mlp_2", np.concatenate(parts))
    return out


def pack_cols(a):
    out = np.zeros((P, N_COLS), np.float32)

    def put(name, v):
        first, n = COLS[name]
        out[:, first:first + n] = v.reshape(n, P).T

    for name, key in (("mix_pre", "norm_mix_pre"), ("mix_post", "norm_mix_post"), ("pool_scale", "pool_scale"),
                      ("mem_pre", "norm_mem_pre"), ("mem_kv", "norm_mem_kv"), ("mem_post", "norm_mem_post"),
                      ("ffn_pre", "norm_ffn_pre"), ("ffn_post", "norm_ffn_post"), ("attn_2", "attn_norm_w_2"),
                      ("q_a", "q_a_norm_w_2"), ("kv_a", "kv_a_norm_w_2"), ("diff_out", "diff_out_norm_w_2"),
                      ("mlp_2", "mlp_norm_w_2")):
        put(name, a[key])
    for name, key in (("mla_q", "mla_q_norm_w_2"), ("mla_k", "mla_k_norm_w_2")):
        put(name + "_nope", a[key][0, :P])
        put(name + "_rope", np.tile(a[key][0, P:], 2))
    put("diff_q", np.tile(a["diff_q_norm_w_2"][0], 2))
    put("diff_k", np.tile(a["diff_k_norm_w_2"][0], 2))
    first = COLS["lambda"][0]
    for n, key in enumerate(("lambda_q1_2", "lambda_k1_2", "lambda_q2_2", "lambda_k2_2")):
        out[:, first + 64 * n:first + 64 * n + 64] = a[key]
    return out


def features_first(v):
    return np.ascontiguousarray(v.T.reshape(-1, P, v.shape[0]).transpose(1, 0, 2))


def bucket_causal(dist):
    n = np.maximum(dist, 0)
    large = 16 + (np.log(np.maximum(n, 1).astype(np.float32) / np.float32(16)) / np.float32(np.log(8.0))
                  * np.float32(16)).astype(np.int32)
    return np.where(n < 16, n, np.minimum(large, 31))


def bucket_both_ways(rel):
    n = np.abs(rel)
    large = 8 + (np.log(np.maximum(n, 1).astype(np.float32) / np.float32(8)) / np.float32(np.log(16.0))
                 * np.float32(8)).astype(np.int32)
    return np.where(rel > 0, 16, 0) + np.where(n < 8, n, np.minimum(large, 15))


def constants():
    c = {"c_ident": np.eye(P, dtype=np.float32)}
    c["c_flip"] = c["c_ident"][::-1].copy()
    c["c_tri"] = np.where(np.arange(P)[None, :] > np.arange(P)[:, None], np.float32(NEG), np.float32(0))
    fix = np.ones((POOL_GROUPS, 16), np.float32)
    for g in range(POOL_GROUPS):
        n = np.arange(1, 17)
        fix[g] = (2 << g) / np.minimum(n, 2 << g)
    c["c_pool_fix"] = np.broadcast_to(fix, (P, POOL_GROUPS, 16)).copy()
    dist = 255 - np.arange(384)
    c["c_onehot"] = (bucket_causal(dist)[None, :] == np.arange(BUCKETS)[:, None]).astype(np.float32)
    rel = np.arange(512) - 255
    c["c_onehot_2"] = (bucket_both_ways(rel)[None, :] == np.arange(BUCKETS)[:, None]).astype(np.float32)
    inv = (10000.0 ** (-np.arange(0, ROPE, 2) / ROPE)).astype(np.float32)
    ang = (np.arange(S, dtype=np.float32)[None, :] * inv[:, None]).astype(np.float64)
    c["c_cos"] = np.tile(np.cos(ang), (4, 1)).astype(np.float32)
    c["c_sin"] = np.concatenate([-np.sin(ang), np.sin(ang)] * 2).astype(np.float32)
    halves = np.zeros((P, 3, P), np.float32)
    halves[:64, 0, :64] = halves[64:, 0, 64:] = 1
    halves[:64, 1] = halves[64:, 2] = 1
    c["c_halves"] = halves
    return c


N_CONSTS = 8
SCRATCH = {"bias_rows": (HEADS, 384), "gates": (3 * KT, P, S), "bias_rows_2": (DIFF_HEADS, 512),
           "bias_tiles_2": (DIFF_HEADS, P, 3 * P),
           "diff_qk": (2 * DIFF_HEADS, P, S), "diff_v": (DIFF_HEADS, P, NT, P),
           "mla_nope": (2 * MLA_HEADS, P, S), "mla_rope": (2 * MLA_HEADS, ROPE, S), "mla_v": (MLA_HEADS, P, NT, P),
           "heads_out": (KT, P, S)}


def arrays_of(inputs):
    a = {k: np.asarray(v) for k, v in inputs.items()}
    out = {"weights": pack_weights(a), "cols": pack_cols(a), "x": features_first(a["x"][0]),
           "mem": features_first(a["mem"][0]), "rel_bias_table": a["rel_bias_table"],
           "rel_bias_2": a["rel_bias_2"]}
    return {**out, **constants()}


def kernel(**inputs):
    from concourse import bacc
    from concourse.bass_utils import run_bass_kernel_spmd

    nc = bacc.Bacc("TRN2", target_bir_lowering=False, num_devices=1)
    arrays = arrays_of(inputs)
    t = {name: nc.dram_tensor(f"{name}_dram", a.shape, mybir.dt.from_np(a.dtype), kind="ExternalInput").ap()
         for name, a in arrays.items()}
    t["out"] = nc.dram_tensor("out_dram", (P, KT, S), F32, kind="ExternalOutput").ap()
    for name, shape in SCRATCH.items():
        t[name] = nc.dram_tensor(f"{name}_scratch", shape, F32, kind="Internal").ap()
    program(nc, t)
    r = run_bass_kernel_spmd(nc, [{f"{name}_dram": a for name, a in arrays.items()}], core_ids=[0])
    got = r.results[0]["out_dram"]
    return np.ascontiguousarray(got.transpose(2, 1, 0).reshape(1, S, D))
```

```python
from contextlib import ExitStack

import numpy as np

import concourse.bass as bass
from concourse import mybir

F32 = mybir.dt.float32
F32R = mybir.dt.float32r
BF16 = mybir.dt.bfloat16
ACT = mybir.ActivationFunctionType
ALU = mybir.AluOpType
AX = mybir.AxisListType

P = 128
D = 1024
KT = D // P
S = 1024
NT = S // P
HALF = 512
EPS = 1e-6

POOL_GROUPS = 4
HEADS = 8
IDX_HEADS, IDX_DIM = 4, 64
TOPK = 256
ROUNDS = TOPK // 8
BUCKETS = 32
MAX_DISTANCE = 128
VW = P + IDX_HEADS
M = 256
MT = M // P
MEM_HEADS = 4
FF = 2816
FF_TILES = FF // P
FF2 = 4096
FF2_TILES = FF2 // P
CHUNK = 4
MLA_HEADS = 4
DIFF_HEADS = 4
ROPE = 64
LAM_INIT = 0.2
NEG = -1e30
TAKEN = -3e38

GROUPS = (MLA_HEADS + DIFF_HEADS) * NT // 4

COLS = {}
for _name, _n in (
    ("mix_pre", 8), ("mix_post", 8), ("pool_scale", 4), ("mem_pre", 8), ("mem_kv", 8), ("mem_post", 8),
    ("ffn_pre", 8), ("ffn_post", 8), ("attn_2", 8), ("q_a", 2), ("kv_a", 1), ("mla_q_nope", 1),
    ("mla_q_rope", 1), ("mla_k_nope", 1), ("mla_k_rope", 1), ("diff_q", 1), ("diff_k", 1),
    ("diff_out", 1), ("mlp_2", 8), ("lambda", 256),
):
    COLS[_name] = (sum(n for _, n in COLS.values()), _n)
N_COLS = sum(n for _, n in COLS.values())

PRE_ORDER = ("mix_pre", "mem_pre", "ffn_pre", "attn_2", "q_a", "kv_a", "mlp_2")
PRE = {}
for _name in PRE_ORDER:
    PRE[_name] = (COLS[_name][1], sum(n for n, _ in PRE.values()))

SLABS = {}
for _name, _n in (
    ("mix_in", 8),
    ("value_pool", 2),
    ("proj_pool", 4), ("gate_pool", 8), ("gate_attn", 8), ("query", 8), ("proj_attn", 8), ("mix_out", 8),
    ("mem_key", 4), ("mem_value", 4), ("mem_query", 4), ("mem_out", 4),
    ("ffn", 2 * FF_TILES + FF_TILES),
    ("in_2", 13), ("diff_value", 4), ("uq_rope", 1), ("ukv", 1), ("uq_nope", 1), ("out_2", 8), ("mlp_2", 64),
):
    SLABS[_name] = (sum(n for _, n in SLABS.values()), _n)
N_SLABS = sum(n for _, n in SLABS.values())


class Chain:

    def __init__(self, engine, sem):
        self.engine, self.sem, self.n = engine, sem, 0

    def __call__(self, instruction):
        self.n += 1
        instruction.then_inc(self.sem, 1)
        self.engine.wait_ge(self.sem, self.n)


def program(nc, t):
    out = t["out"]
    with ExitStack() as ctx:
        def sem(name):
            return ctx.enter_context(nc.semaphore(name))

        KB = 1024
        base = -(-nc.sbuf_base // 64) * 64
        RAW, SPLIT = base, base + 8 * KB
        XR = SPLIT + 16 * KB
        AR = XR + 32 * KB
        BR = AR + 64 * KB
        ER = BR + 64 * KB
        place = [ER]

        def at(name, offset, shape, dt=F32):
            return nc.alloc_sbuf_tensor_at(name, shape, dt, offset=offset)

        def small(name, shape, dt=F32):
            size = int(np.prod(shape[1:])) * (2 if dt == BF16 else 4)
            here = place[0]
            place[0] += -(-size // 32) * 32
            return at(name, here, shape, dt)

        raw = [at(f"w_raw{i}", RAW + 4 * KB * i, [P, 1024]) for i in range(2)]
        w_hi = [at(f"w_hi{i}", SPLIT + 8 * KB * i, [P, 1024], F32R) for i in range(2)]
        w_lo = [at(f"w_lo{i}", SPLIT + 8 * KB * i + 4 * KB, [P, 1024], F32R) for i in range(2)]

        acc_at = place[0]
        acc = small("acc", [P, S])
        tmp_at = place[0]
        tmp = [small(f"tmp{i}", [P, S]) for i in range(2)]
        cols = small("cols", [P, N_COLS])
        ident = small("ident", [P, P])
        ident16 = small("ident16", [P, P], BF16)
        tri = small("tri", [P, P])
        ones = small("ones", [P, P])
        zero = small("zero", [P, 1])
        eps = small("eps", [P, 1])
        pool_fix = small("pool_fix", [P, POOL_GROUPS, 16])
        stat = small("stat", [P, 64])
        top8 = small("top8", [P, 2, 8])
        mstat = small("mstat", [P, 2, 4, 4])
        late_at = place[0]
        place[0] += 8 * KB
        lam_ab, minus_lam = stat[:, 0:2], stat[:, 2:3]
        value_raw = at("value_raw", late_at, [P, NT, VW])
        assert place[0] <= nc.sbuf_usable_end, place[0] - nc.sbuf_usable_end

        def col(name, k=0):
            return cols[:, COLS[name][0] + k:COLS[name][0] + k + 1]

        def pair(name, offset, shape):
            size = int(np.prod(shape[1:])) * 4
            return at(name + "_hi", offset, shape, F32R), at(name + "_lo", offset + size, shape, F32R)

        x_in = at("x_in", XR, [P, KT, S])
        h1 = pair("h1", AR, [P, KT, S])
        u = at("u", XR, [P, POOL_GROUPS, S])
        win = [at(f"win{i}", XR + 16 * KB + 4 * KB * i, [P, S]) for i in range(2)]
        pooled = pair("pooled", BR, [P, POOL_GROUPS, S])
        mixed = pair("mixed", XR, [P, POOL_GROUPS, S])
        qidx = pair("qidx", BR + 32 * KB, [P, 2, S])
        kidx = pair("kidx", BR + 48 * KB, [P, S])
        key = pair("key", BR + 56 * KB, [P, S])
        score_at = {i: sum(j + 1 for j in range(2, i)) * P for i in range(2, NT)}
        score = at("score", BR, [P, sum(j + 1 for j in range(2, NT)) * P])
        mask_at = {i: sum(j + 1 for j in range(i)) * P for i in range(NT)}
        mask = at("mask", BR + 16896, [P, sum(range(1, NT + 1)) * P], BF16)
        query = at("query", XR, [P, HEADS, S])
        value = pair("value", BR + 32 * KB, [P, NT, P])
        mix_rows = [[at(f"mix_rows0_{q}", BR + 4 * KB * q, [P, S]) for q in range(4)],
                    [at(f"mix_rows1_{q}", o, [P, S]) for q, o in enumerate((late_at, late_at + 4 * KB, BR + 26 * KB, acc_at))]]
        probs_t = [pair(f"probs_t{i}", BR + 40 * KB + 4 * KB * i, [P, HALF]) for i in range(2)]
        q_tile = [pair(f"q_tile{i}", tmp_at + 4 * KB * i, [P, 4, P]) for i in range(2)]
        bias = at("bias", BR + 48 * KB, [P, HEADS, 2 * P])
        bias_2 = at("bias_2", BR + 40 * KB, [P, DIFF_HEADS, 3 * P])
        flip = at("flip", BR + 46 * KB, [P, P])
        frow = at("frow", BR + 56 * KB, [HEADS, 384])
        onehot = at("onehot", BR + 58 * KB, [BUCKETS, 384])
        table = at("table", BR + 60 * KB, [BUCKETS, HEADS])
        table_2 = at("table_2", BR + 60 * KB + 512, [BUCKETS, DIFF_HEADS])
        onehot_2 = at("onehot_2", BR + 61 * KB, [BUCKETS, HALF])
        frow_2 = at("frow_2", late_at + 6 * KB, [DIFF_HEADS, HALF])
        att = pair("att", AR, [P, HEADS, S])
        gated = [at(f"gated{i}", XR + 12 * KB * i, [P, 3, S]) for i in range(2)]
        merged = pair("merged", BR, [P, KT, S])
        y = at("y", AR, [P, KT, S])
        x = at("x", XR, [P, KT, S])

        mem_in = at("mem_in", AR + 32 * KB, [P, KT, M])
        memn = pair("memn", AR + 40 * KB, [P, KT, M])
        mem_sq = at("mem_sq", AR + 48 * KB, [P, KT, M])
        mem_rms = at("mem_rms", AR + 56 * KB, [P, M])
        kmem = pair("kmem", AR + 32 * KB, [P, MEM_HEADS, M])
        vmem = pair("vmem", late_at, [P, MT, HALF])
        normed = pair("normed", BR, [P, KT, S])
        qm = pair("qm", AR, [P, MEM_HEADS, S])
        om = pair("om", BR, [P, MEM_HEADS, S])
        mprobs = at("mprobs", BR + 32 * KB, [P, 2, 4, M])
        mpt = [pair(f"mpt{j}", BR + 40 * KB + 4 * KB * j, [P, HALF]) for j in range(MT)]
        hidden = pair("hidden", AR + 32 * KB, [P, CHUNK, S])
        c_q = at("c_q", AR, [P, 2, S])
        cq = pair("cq", AR + 8 * KB, [P, 2, S])
        c_kv = at("c_kv", AR + 24 * KB, [P, 1, S])
        ckv = pair("ckv", AR + 28 * KB, [P, 1, S])
        k_rope = at("k_rope", AR + 36 * KB, [P, S])
        q_rope = at("q_rope", AR + 40 * KB, [P, 2, S])
        q_rope_sq = at("q_rope_sq", AR + 48 * KB, [P, 2, S])
        k_rope_sq = at("k_rope_sq", AR + 56 * KB, [P, S])
        halves = at("halves", AR + 60 * KB, [P, 3, P])
        cos, sin = at("cos", late_at, [P, S]), at("sin", late_at + 4 * KB, [P, S])
        d_rms = [at(f"d_rms{i}", AR + 48 * KB + 4 * KB * i, [P, S]) for i in range(2)]
        d_out = [at(f"d_out{i}", AR + 4 * KB * i, [P, S]) for i in range(2)]
        d_value = at("d_value", BR, [P, NT, HALF])
        v_value = at("v_value", BR + 16 * KB, [P, NT, HALF])
        g_rms = [at(f"g_rms{i}", AR + 4 * KB * i, [P, S]) for i in range(2)]
        g_nope = [at(f"g_nope{i}", BR + 56 * KB + 4 * KB * i, [P, S]) for i in range(2)]
        g_rope = [at(f"g_rope{i}", late_at + 4 * KB * i, [P, S]) for i in range(2)]
        turned = at("turned", acc_at, [P, S])
        head_raw = [at(f"head_raw{i}", BR + 36 * KB + 4 * KB * i, [P, S]) for i in range(5)]
        head_parts = [[at(f"head_part{e}_{i}", (BR, AR)[e] + 4 * KB * i, [P, S], F32R) for i in range(9)]
                      for e in range(2)]
        pt = [pair(f"pt{i}", AR + 36 * KB + 4 * KB * i, [P, HALF]) for i in range(2)]
        rows_at = [AR + 44 * KB + 4 * KB * i for i in range(5)] + [BR + 56 * KB, BR + 60 * KB, acc_at]
        prob_rows = [[at(f"rows{g}_{q}", rows_at[4 * g + q], [P, S]) for q in range(4)] for g in range(2)]
        second = [at(f"second{i}", tmp_at + 4 * KB * i, [P, S]) for i in range(2)]
        o_stage = at("o_stage", late_at, [P, HALF])
        diagonal = at("diagonal", late_at + 2 * KB, [P, 4, P])
        e_bias = at("e_bias", late_at + 4 * KB, [P, 2, 3 * P])
        e_stat = at("e_stat", late_at + 7 * KB, [P, 8, 6, 2])
        o_in = at("o_in", BR, [P, KT, S])
        o_rms = [at(f"o_rms{i}", BR + 40 * KB + 4 * KB * i, [P, S]) for i in range(2)]
        o_all = pair("o_all", AR, [P, KT, S])
        ps = ctx.enter_context(nc.psum_tensor("ps", [P, 8, HALF], F32))

        def wide(slot):
            return ps[:, 2 * slot:2 * slot + 2, :].rearrange("p b n -> p (b n)")

        def mix_stat(unit, kind):
            c = 6 * (unit % 8) + kind
            return stat[:, c:c + 1]

        def tiles_before(group):
            return sum(g // 2 + 1 for g in range(group))

        def tiles_of(group, n):
            tiles = group // 2 + 1
            return range(-(-n * tiles // 4), -(-(n + 1) * tiles // 4))

        raw_landed = [sem(f"raw_landed{i}") for i in range(2)]
        w_rounded = sem("w_rounded")
        w_split = sem("w_split")
        w_used = sem("w_used")
        first_half = sem("first_half")
        consts_in = sem("consts_in")
        x_in_landed = [sem(f"x_in_landed{i}") for i in range(4)]
        dve_consts = sem("dve_consts")
        zero_set = sem("zero_set")
        dve_step = sem("dve_step")
        n_sq, n_added = sem("norm_squared"), sem("norm_added")
        n_post_sq, n_acc = sem("norm_post_squared"), sem("norm_post_added")
        n_sum, n_rs = sem("norm_total"), sem("norm_inverse")
        act_step = sem("act_step")
        n_tmp, n_hi, n_lo = (sem("norm_" + n) for n in ("scaled", "hi", "lo"))
        in_hi, in_free = sem("in_hi"), sem("in_free")
        value_done, value_free = sem("value_done"), sem("value_free")
        pooled_ready = sem("pooled_ready")
        pool_done, mix_free = sem("pool_done"), sem("mix_free")
        idx_done, idx_relu, idx_added = sem("idx_done"), sem("idx_relu"), sem("idx_added")
        gate_free = sem("gate_free")
        staged = [sem(f"staged{i}") for i in range(2)]
        frow_done, frow_copied, frow_out = sem("frow_done"), sem("frow_copied"), sem("frow_out")
        shifted_in, flipped, bias_done = sem("shifted_in"), sem("flipped"), sem("bias_done")
        value_split = sem("value_split")
        masks_ready = sem("masks_ready")
        qt_hi, qt_lo, inv_ready = sem("qt_hi"), sem("qt_lo"), sem("inv_ready")
        qk_done, logits_ready, nmax_ready, exp_done, probs_ready = (
            sem(n) for n in ("qk_done", "logits_ready", "nmax_ready", "exp_done", "probs_ready"))
        tr_done, pt_hi, pt_lo, pv_done, o_hi, o_lo = (
            sem(n) for n in ("tr_done", "pt_hi", "pt_lo", "pv_done", "o_hi", "o_lo"))
        gates_in = [sem(f"gates_in{i}") for i in range(2)]
        merge_free = sem("merge_free")
        x_landed = sem("x_landed")
        y_free, x_added = sem("y_free"), sem("x_added")
        mem_landed = sem("mem_landed")
        mem_squared, mem_total, mem_rs, mem_scaled, mem_hi, mem_lo = (
            sem("mem_" + n) for n in ("squared", "total", "inverse", "scaled", "hi", "lo"))
        mkv_hi, mkv_lo, mq_hi, mq_lo = (sem(n) for n in ("mem_kv_hi", "mem_kv_lo", "mem_q_hi", "mem_q_lo"))
        m_qk, m_max, m_exp, m_probs, m_tr, m_pthi, m_ptlo, m_pv, m_ohi, m_olo = (
            sem("mem_" + n) for n in ("logits", "max", "exp", "probs", "transposed", "probs_t_hi", "probs_t_lo",
                                      "weighed", "out_hi", "out_lo"))
        f_silu, f_mul, f_hi, f_lo, f_added, y_zero = (
            sem("ffn_" + n) for n in ("silu", "hidden", "hidden_hi", "hidden_lo", "added", "y_zeroed"))
        tables_in, bias_2_out = sem("tables_in"), sem("bias_2_out")
        c_free, d_free = sem("c_free"), sem("d_free")
        d_sq, d_tot, d_ln, d_rs = (sem("diff_norm_" + n) for n in ("squared", "total", "log", "inverse"))
        d_stored = [sem(f"diff_stored{i}") for i in range(2)]
        dv_act, dv_dve, v_done, v_act, v_dve = (
            sem(n) for n in ("dv_out_act", "dv_out_dve", "v_done", "v_out_act", "v_out_dve"))
        dv_stored, v_stored = sem("dv_stored"), sem("v_stored")
        rope_sq = sem("rope_squared")
        g_done, g_sq, g_tot, g_rs, g_free, g_roped = (
            sem("mla_" + n) for n in ("tile", "squared", "total", "inverse", "nope_out", "rope_out"))
        r_done, r_free = sem("rope_done"), sem("rope_free")
        g_stored = [sem(f"mla_stored{i}") for i in range(2)]
        lam_sum, lam_exp = sem("lam_sum"), sem("lam_exp")
        heads_in, bias_2_in, head_split = sem("heads_in"), [sem(f"bias_2_in{i}") for i in range(2)], sem("head_split")
        a_qk, a_max, a_exp, a_probs, a_tr, a_pthi, a_ptlo, a_pv, a_out, e_red, a_diag, a_spread, a_copied = (
            sem("attn_" + n) for n in ("logits", "max", "exp", "probs", "transposed", "probs_t_hi", "probs_t_lo",
                                       "weighed", "out", "biased", "diagonal", "spread", "copied"))
        o_stored, o_landed, o_last = sem("o_stored"), sem("o_landed"), sem("o_last")
        s_sq, s_tot, s_rs, s_scaled, s_hi, s_lo = (
            sem("heads_" + n) for n in ("squared", "total", "inverse", "scaled", "hi", "lo"))
        u_relu, u_sq, u_hi, u_lo, u_added = (sem("mlp_" + n) for n in ("relu", "squared", "hi", "lo", "added"))
        stored = sem("stored")

        block = ctx.enter_context(nc.Block())

        @block.sync
        def _(sp):
            for s in range(2):
                sp.dma_start(raw[s][:], t["weights"][s]).then_inc(raw_landed[s], 16)
            def load_slabs(first, end):
                with sp.Fori(first // 2, end // 2) as pr:
                    for s in range(2):
                        sp.wait_ge(w_split, 2 * pr + s - 1)
                        sp.dma_start(raw[s][:], t["weights"][2 * pr + s]).then_inc(raw_landed[s], 16)

            load_slabs(2, SLABS["out_2"][0] + 2)
            sp.wait_ge(v_stored, 16 * MLA_HEADS)
            sp.wait_ge(dv_stored, 16 * DIFF_HEADS)
            for hd in range(2 * MLA_HEADS):
                if hd < MLA_HEADS:
                    sp.wait_ge(g_stored[hd % 2], 32 * (MLA_HEADS // 2 + hd // 2 + 1))
                if hd == MLA_HEADS:
                    sp.wait_ge(bias_2_out, 16)
                    for e in range(2):
                        sp.wait_ge(d_stored[e], 16 * DIFF_HEADS)
                d = hd - MLA_HEADS
                if d < 0:
                    srcs = ((t["mla_nope"][hd + MLA_HEADS],), (t["mla_nope"][hd],), (t["mla_v"][hd].rearrange("p j n -> p (j n)"),),
                            (t["mla_rope"][hd + MLA_HEADS],) * 2, (t["mla_rope"][hd],) * 2)
                else:
                    q, k = t["diff_qk"][d], t["diff_qk"][d + DIFF_HEADS]
                    srcs = ((q[0:64],) * 2, (q[64:P],) * 2, (t["diff_v"][d].rearrange("p j n -> p (j n)"),),
                            (k[0:64],) * 2, (k[64:P],) * 2)
                for n, src in enumerate(srcs):
                    if hd:
                        sp.wait_ge(head_split, 10 * (hd - 1) + 6 + n)
                    for e, part in enumerate(src):
                        rows_of = slice(0, P) if len(src) == 1 else slice(64 * e, 64 * e + 64)
                        sp.dma_start(head_raw[n][rows_of, :], part).then_inc(heads_in, 16)
                if d >= 2:
                    sp.wait_ge(e_red, 16 * (d - 1))
                if d >= 0:
                    sp.dma_start(e_bias[:, d % 2, :], t["bias_tiles_2"][d]).then_inc(bias_2_in[d % 2], 16)
            load_slabs(SLABS["out_2"][0] + 2, N_SLABS)

        @block.gpsimd
        def _(pool):
            nc.gpsimd.memset(zero[:], 0.0).then_inc(zero_set, 1)
            pool.wait_ge(zero_set, 1)

            def split(s, n):
                nc.gpsimd.tensor_tensor(w_hi[s][:], raw[s][:], zero[:, 0:1].broadcast_to([P, 1024]),
                                        ALU.add).then_inc(w_rounded, 1)
                pool.wait_ge(w_rounded, n)
                nc.gpsimd.tensor_tensor(w_lo[s][:], raw[s][:], w_hi[s][:].bitcast(F32),
                                        ALU.subtract).then_inc(w_split, 1)

            for s in range(2):
                pool.wait_ge(raw_landed[s], 16)
                split(s, s + 1)
            def split_slabs(first, end):
                with pool.Fori(first // 2, end // 2) as pr:
                    for s in range(2):
                        pool.wait_ge(w_used, 2 * pr + s - 1)
                        pool.wait_ge(raw_landed[s], 16 * pr + 16)
                        split(s, 2 * pr + s + 1)

            split_slabs(2, SLABS["proj_attn"][0] + 2)
            for unit in range(HEADS * NT):
                group, q = unit // 4, unit % 4
                n = (group // 2 + 1) * P
                row = mix_rows[group % 2][q][:, 0:n]
                pool.wait_ge(inv_ready, unit + 1)
                nc.gpsimd.tensor_tensor(row, row, mix_stat(unit, 5).broadcast_to([P, n]), ALU.mult).then_inc(probs_ready, 1)
            split_slabs(SLABS["proj_attn"][0] + 2, SLABS["out_2"][0] + 2)
            landed = 0
            for hd in range(2 * MLA_HEADS):
                p = head_parts[hd % 2]
                top, bottom, both = slice(0, 64), slice(64, P), slice(0, P)
                if hd < MLA_HEADS:
                    landed += 16 * 7
                    hi = (p[0], p[2], p[4], p[6], p[7])
                    lo = ((p[1], both), (p[3], both), (p[5], both), (p[6], bottom), (p[8], top))
                else:
                    landed += 16 * 9
                    hi = (p[0], p[1], p[4], p[2], p[3])
                    lo = ((p[0], bottom), (p[1], top), (p[5], both), (p[8], top), (p[8], bottom))
                pool.wait_ge(heads_in, landed)
                if hd == 1:
                    pool.wait_ge(g_roped, 2 * MLA_HEADS)
                if hd >= 2:
                    pool.wait_ge(a_pv, 16 * (hd - 1))
                if hd:
                    pool.wait_ge(head_split, 10 * hd)
                for dst, src in zip(hi, head_raw):
                    nc.gpsimd.tensor_tensor(dst[:], src[:], zero[:, 0:1].broadcast_to([P, S]), ALU.add).then_inc(head_split, 1)
                for n, (dst, lanes) in enumerate(lo):
                    pool.wait_ge(head_split, 10 * hd + n + 5)
                    nc.gpsimd.tensor_tensor(dst[lanes, :], head_raw[n][lanes, :], hi[n][lanes, :].bitcast(F32),
                                            ALU.subtract).then_inc(head_split, 1)
            pool.wait_ge(head_split, 20 * MLA_HEADS)
            split_slabs(SLABS["out_2"][0] + 2, N_SLABS)

        @block.tensor
        def _(pe):
            def product(out, stationary, moving, start, stop):
                (sh, sl), (mh, ml) = stationary, moving
                nc.tensor.matmul(out, sh, mh, start=start, stop=False)
                nc.tensor.matmul(out, sh, ml, start=False, stop=False)
                return nc.tensor.matmul(out, sl, mh, start=False, stop=stop)

            def weight(s, b, width=P):
                return w_hi[s][:, b:b + width], w_lo[s][:, b:b + width]

            def tile(s, first, src, kt, slot, between=None):
                out = wide(slot)
                for k in range(kt):
                    for n in range(0, S, HALF):
                        last = product(out[:, n:n + HALF], weight(s, first + k * P),
                                       (src[0][:, k, n:n + HALF], src[1][:, k, n:n + HALF]), k == 0, k == kt - 1)
                    if between and k == 1:
                        between()
                return last

            def first_tiles(slabs, name, src):
                tiles, before = PRE[name]
                for s in range(2):
                    pe.wait_ge(w_split, SLABS[slabs][0] + s + 1)
                for k in range(tiles):
                    pe.wait_ge(n_lo, before + k + 1)
                    for s in range(2):
                        for n in range(0, S, HALF):
                            last = product(wide(s)[:, n:n + HALF], weight(s, k * P),
                                           (src[0][:, k, n:n + HALF], src[1][:, k, n:n + HALF]), k == 0, k == tiles - 1)
                        if k == tiles - 1:
                            last.then_inc(w_used, 1)

            def over_features(out, src, lhs, start=True, stop=True):
                for n in range(0, S, HALF):
                    last = nc.tensor.matmul(out[:, n:n + HALF], lhs, src[:, n:n + HALF], start=start, stop=stop)
                return last

            def total_added(post):
                pe.wait_ge(n_acc, 7 * (post + 1))
                over_features(wide(2), acc, ones[:]).then_inc(n_sum, 1)

            def total(name):
                tiles, before = PRE[name]
                for k in range(tiles):
                    pe.wait_ge(n_sq, before + k + 1)
                    over_features(wide(2), tmp[k % 2], ones[:], k == 0, k == tiles - 1).then_inc(
                        n_sum if k == tiles - 1 else n_added, 1)

            pe.wait_ge(dve_consts, 1)
            pe.wait_ge(consts_in, 16 * N_CONSTS)
            total("mix_pre")
            nc.tensor.matmul(ps[0:HEADS, 6, 0:384], table[:, :], onehot[:, :], start=True, stop=True)
            nc.tensor.matmul(ps[0:DIFF_HEADS, 7, :], table_2[:, :], onehot_2[:, :], start=True, stop=True).then_inc(frow_done, 1)
            first_tiles("mix_in", "mix_pre", h1)
            s0 = SLABS["mix_in"][0]
            with pe.Fori(1, 4) as it:
                for s in range(2):
                    pe.wait_ge(w_split, 2 * it + s0 + s + 1)
                    pe.wait_ge(in_free, 2 * it + s + 1)
                    tile(s, 0, h1, KT, s).then_inc(w_used, 1)
            pe.wait_ge(w_split, SLABS["value_pool"][0] + 2)
            for j in range(NT):
                out = ps[:, 4 + j // 3, (j % 3) * VW:(j % 3 + 1) * VW]
                for k in range(KT):
                    last = product(out, (h1[0][:, k, j * P:(j + 1) * P], h1[1][:, k, j * P:(j + 1) * P]),
                                   weight(k // 4, k % 4 * VW, VW), k == 0, k == KT - 1)
                last.then_inc(value_done, 1)
            pe.wait_ge(pooled_ready, POOL_GROUPS)
            for g in range(POOL_GROUPS):
                pe.wait_ge(*((in_free, 2 + 8) if g < 2 else (mix_free, g - 1)))
                b = 4 * VW + (g % 3) * P
                for n in range(0, S, HALF):
                    last = product(wide(g % 2)[:, n:n + HALF], weight(g // 3, b),
                                   (pooled[0][:, g, n:n + HALF], pooled[1][:, g, n:n + HALF]), True, True)
                last.then_inc(pool_done if g < 2 else w_used, 1)
            pe.wait_ge(value_free, 3)
            unit = 0
            for i in reversed(range(2, NT)):
                for hd in range(IDX_HEADS):
                    if unit >= 2:
                        pe.wait_ge(idx_relu, unit - 1)
                    lo, hi = IDX_DIM * (hd % 2), IDX_DIM * (hd % 2 + 1)
                    for n in range(0, (i + 1) * P, HALF):
                        m = min(HALF, (i + 1) * P - n)
                        last = product(wide(2 + unit % 2)[:, n:n + m],
                                       tuple(q[lo:hi, hd // 2, i * P:(i + 1) * P] for q in qidx),
                                       tuple(k[lo:hi, n:n + m] for k in kidx), True, True)
                    last.then_inc(idx_done, 1)
                    unit += 1
            pe.wait_ge(mix_free, POOL_GROUPS)
            s0 = SLABS["proj_pool"][0]
            with pe.Fori(0, 2) as it:
                for s in range(2):
                    pe.wait_ge(w_split, 2 * it + s0 + s + 1)
                    for half in range(2):
                        pe.wait_ge(gate_free, 4 * it + 2 * s + half + 1)
                        tile(s, half * POOL_GROUPS * P, mixed, POOL_GROUPS, half).then_inc((first_half, w_used)[half], 1)
            pe.wait_ge(shifted_in, 48)
            pe.wait_ge(idx_relu, unit)
            for n in range(4):
                last = nc.tensor.matmul(ps[:, 4 + n, :], flip[:], bias[:, 2 * n:2 * n + 2, :].rearrange("p h u -> p (h u)"),
                                        start=True, stop=True)
            last.then_inc(flipped, 1)
            pe.wait_ge(bias_done, 1)
            for n in range(3):
                last = nc.tensor.matmul(ps[:, 4 + n, :], flip[:],
                                        bias_2[:].rearrange("p h u -> p (h u)")[:, n * HALF:(n + 1) * HALF],
                                        start=True, stop=True)
            last.then_inc(flipped, 1)
            s0 = SLABS["gate_pool"][0]
            with pe.Fori(0, 12) as it:
                for s in range(2):
                    pe.wait_ge(w_split, 2 * it + s0 + s + 1)
                    pe.wait_ge(gate_free, 2 * it + KT + s + 1)
                    tile(s, 0, h1, KT, s).then_inc(w_used, 1)
            pe.wait_ge(masks_ready, 1)
            pe.wait_ge(value_split, 1)
            pe.wait_ge(bias_done, 2)
            pe.wait_ge(gate_free, 2 + 4 * KT)
            def mix_logits(unit):
                group, q = unit // 4, unit % 4
                i = group // 2
                if q == 0:
                    pe.wait_ge(qt_lo, group + 1)
                if unit >= 2:
                    pe.wait_ge(logits_ready, unit - 1)
                for n in range(0, (i + 1) * P, HALF):
                    m = min(HALF, (i + 1) * P - n)
                    out = wide(unit % 2)[:, n:n + m]
                    product(out, tuple(e[:, q, :] for e in q_tile[group % 2]), tuple(e[:, n:n + m] for e in key), True, False)
                    last = nc.tensor.matmul(out, ident16[:], mask[:, mask_at[i] + n:mask_at[i] + n + m],
                                            start=False, stop=True)
                last.then_inc(qk_done, 1)

            def mix_transposes(group, j):
                n_tr = tiles_before(group) + j
                if j == 0:
                    pe.wait_ge(probs_ready, 4 * group + 4)
                if n_tr >= 2:
                    pe.wait_ge(pt_lo, n_tr - 1)
                for q in range(4):
                    last = nc.tensor.transpose(ps[:, 4 + n_tr % 2, q * P:(q + 1) * P],
                                               mix_rows[group % 2][q][:, j * P:(j + 1) * P], ident[:])
                last.then_inc(tr_done, 1)

            def mix_values(group, j):
                n_tr = tiles_before(group) + j
                if j == 0 and group >= 2:
                    pe.wait_ge(o_lo, group - 1)
                pe.wait_ge(pt_lo, n_tr + 1)
                product(ps[:, 6 + group % 2, :], (value[0][:, j, :], value[1][:, j, :]),
                        tuple(e[:] for e in probs_t[n_tr % 2]), j == 0, j == group // 2).then_inc(pv_done, 1)

            for q in range(4):
                mix_logits(q)
            pending = ()
            for group in range(2 * NT):
                for n in range(4):
                    if group + 1 < 2 * NT:
                        mix_logits(4 * (group + 1) + n)
                    for g, j in pending:
                        mix_values(g, j)
                    pending = [(group, j) for j in tiles_of(group, n)]
                    for g, j in pending:
                        mix_transposes(g, j)
            for g, j in pending:
                mix_values(g, j)
            pe.wait_ge(o_lo, 2 * NT)
            s0 = SLABS["proj_attn"][0]
            with pe.Fori(0, 4) as it:
                for s in range(2):
                    pe.wait_ge(w_split, 2 * it + s0 + s + 1)
                    pe.wait_ge(merge_free, 2 * it + s + 1)
                    tile(s, 0, att, KT, s).then_inc(w_used, 1)
            pe.wait_ge(merge_free, 2 + KT)
            s0 = SLABS["mix_out"][0]

            def out_tiles(first, end):
                with pe.Fori(first, end) as it:
                    for s in range(2):
                        pe.wait_ge(w_split, 2 * it + s0 + s + 1)
                        pe.wait_ge(y_free, 2 * it + s + 1)
                        tile(s, 0, merged, KT, s).then_inc(w_used, 1)

            out_tiles(0, 2)
            pe.wait_ge(mem_squared, 1)
            for k in range(KT):
                last = nc.tensor.matmul(ps[:, 6, 0:M], ones[:], mem_sq[:, k, :], start=k == 0, stop=k == KT - 1)
            last.then_inc(mem_total, 1)
            out_tiles(2, 4)
            pe.wait_ge(mem_lo, 1)
            pe.wait_ge(y_free, 2 + KT)
            s0 = SLABS["mem_key"][0]
            for n in range(MEM_HEADS):
                pe.wait_ge(w_split, s0 + n + 1)
                for k in range(KT):
                    last = product(wide(0)[:, n * M:(n + 1) * M], weight(n % 2, k * P),
                                   (memn[0][:, k, :], memn[1][:, k, :]), k == 0, k == KT - 1)
                last.then_inc(w_used, 1)
                if n == 0:
                    total_added(0)
            s0 = SLABS["mem_value"][0]
            for n in range(4):
                pe.wait_ge(w_split, s0 + n + 1)
                for j in range(MT):
                    for k in (2 * n, 2 * n + 1):
                        last = product(wide(1)[:, j * HALF:(j + 1) * HALF],
                                       tuple(v[:, k, j * P:(j + 1) * P] for v in memn),
                                       weight(n % 2, k % 2 * HALF, HALF), k == 0, k == KT - 1)
                last.then_inc(w_used, 1)
            total("mem_pre")
            pe.wait_ge(mkv_lo, 2)
            first_tiles("mem_query", "mem_pre", normed)
            for n in range(2, MEM_HEADS):
                pe.wait_ge(w_split, SLABS["mem_query"][0] + n + 1)
                pe.wait_ge(mq_lo, n + 1)
                tile(n % 2, 0, normed, KT, n % 2).then_inc(w_used, 1)
            pe.wait_ge(mq_lo, 2 + MEM_HEADS)

            def mem_logits(n):
                if n >= 2:
                    pe.wait_ge(m_exp, 4 * (n - 1))
                for q in range(4):
                    t0 = (4 * (n % 2) + q) * P
                    last = product(wide(n % 2)[:, q * M:(q + 1) * M], tuple(v[:, n // 2, t0:t0 + P] for v in qm),
                                   tuple(v[:, n // 2, :] for v in kmem), True, True)
                last.then_inc(m_qk, 1)

            def mem_values(n):
                if n >= 2:
                    pe.wait_ge(m_olo, n - 1)
                for j in range(MT):
                    pe.wait_ge(m_ptlo, MT * n + j + 1)
                    d0 = n // 2 * P
                    product(ps[:, 6 + n % 2, :], tuple(v[:, j, d0:d0 + P] for v in vmem),
                            tuple(v[:] for v in mpt[j]), j == 0, j == MT - 1).then_inc(m_pv, 1)

            mem_logits(0)
            for n in range(2 * MEM_HEADS):
                if n + 1 < 2 * MEM_HEADS:
                    mem_logits(n + 1)
                if n:
                    mem_values(n - 1)
                pe.wait_ge(m_probs, n + 1)
                for j in range(MT):
                    if n:
                        pe.wait_ge(m_ptlo, MT * (n - 1) + j + 1)
                    for q in range(4):
                        last = nc.tensor.transpose(ps[:, 4 + j, q * P:(q + 1) * P],
                                                   mprobs[:, n % 2, q, j * P:(j + 1) * P], ident[:])
                    last.then_inc(m_tr, 1)
            mem_values(2 * MEM_HEADS - 1)
            pe.wait_ge(m_olo, 2 * MEM_HEADS)
            s0 = SLABS["mem_out"][0]
            with pe.Fori(0, 2) as it:
                for s in range(2):
                    pe.wait_ge(w_split, 2 * it + s0 + s + 1)
                    for half in range(2):
                        pe.wait_ge(y_free, 4 * it + 2 * s + half + KT + 1)
                        tile(s, half * 4 * P, om, 4, half).then_inc((first_half, w_used)[half], 1)
            total_added(1)
            total("ffn_pre")
            s0 = SLABS["ffn"][0]

            def ffn_chunk(c, tiles, first=0):
                for j in range(first, tiles):
                    pe.wait_ge(w_split, 12 * c + s0 + 2 * j + 1)
                    if j < 2:
                        pe.wait_ge(f_added, 8 * c + 2 * j + 6)
                    else:
                        pe.wait_ge(f_mul, 4 * c + j - 1)
                    tile(0, 0, normed, KT, 2 * (j % 2)).then_inc(w_used, 1)
                    pe.wait_ge(w_split, 12 * c + s0 + 2 * j + 2)
                    tile(1, 0, normed, KT, 2 * (j % 2) + 1).then_inc(w_used, 1)
                per = 8 // tiles
                for m in range(KT):
                    if m % per == 0:
                        pe.wait_ge(w_split, 12 * c + s0 + 2 * tiles + m // per + 1)
                    if m < 4:
                        pe.wait_ge(f_mul, 4 * c + (m // 2 + tiles - 1 if tiles == 4 else m // 2 + 1))
                    else:
                        pe.wait_ge(f_added, 8 * c + 8 + m - 3)
                    for k in range(tiles):
                        if m == 0:
                            pe.wait_ge(f_lo, 4 * c + 2 + k + 1)
                        for n in range(0, S, HALF):
                            last = product(wide(m % 4)[:, n:n + HALF], weight(m // per % 2, (m % per * tiles + k) * P),
                                           tuple(v[:, k, n:n + HALF] for v in hidden), k == 0, k == tiles - 1)
                    last.then_inc(w_used if m % per == per - 1 else first_half, 1)

            pe.wait_ge(y_free, 2 + 2 * KT)
            first_tiles("ffn", "ffn_pre", normed)
            ffn_chunk(0, CHUNK, 1)
            with pe.Fori(1, FF_TILES // CHUNK) as c:
                ffn_chunk(c, CHUNK)
            ffn_chunk(FF_TILES // CHUNK, FF_TILES % CHUNK)
            total_added(2)
            total("attn_2")
            first_tiles("in_2", "attn_2", normed)
            s0 = SLABS["in_2"][0]
            for n in range(2, 5):
                pe.wait_ge(w_split, s0 + n + 1)
                pe.wait_ge(c_free, n - 1)
                tile(n % 2, 0, normed, KT, n % 2).then_inc(w_used, 1)
                if n >= 3:
                    total(("q_a", "kv_a")[n - 3])
            pe.wait_ge(tables_in, 48)

            def diff_total(q, e):
                pe.wait_ge(d_sq, q + 1)
                over_features(wide(2 + e), tmp[e], halves[:, 0, :]).then_inc(d_tot, 1)

            with pe.Fori(0, DIFF_HEADS) as it:
                for e in range(2):
                    pe.wait_ge(w_split, 2 * it + s0 + 5 + e + 1)
                    pe.wait_ge(d_free, 2 * it + e + 1)
                    tile(1 - e, 0, normed, KT, 1 - e,
                         between=(lambda: diff_total(2 * it, 0)) if e else None).then_inc(w_used, 1)
                diff_total(2 * it + 1, 1)
            pe.wait_ge(d_free, 2 + 2 * DIFF_HEADS)
            s0 = SLABS["diff_value"][0]
            for n in range(4):
                pe.wait_ge(w_split, s0 + n + 1)
                for j in range(NT):
                    for k in (2 * n, 2 * n + 1):
                        last = product(ps[:, j, :], tuple(v[:, k, j * P:(j + 1) * P] for v in normed),
                                       weight((s0 + n) % 2, k % 2 * HALF, HALF), k == 0, k == KT - 1)
                last.then_inc(w_used, 1)
            s0 = SLABS["uq_rope"][0]
            pe.wait_ge(w_split, s0 + 1)
            for p in range(2):
                pe.wait_ge(dv_act, 2 * p + 2)
                pe.wait_ge(dv_dve, 2 * p + 2)
                for n in range(2):
                    tile(s0 % 2, (2 * p + n) * 2 * P, cq, 2, 2 * p + n).then_inc(w_used if p and n else r_done, 1)
            s0 = SLABS["ukv"][0]
            pe.wait_ge(w_split, s0 + 1)
            for j in range(NT):
                pe.wait_ge(r_free, j // 4 + 1)
                product(ps[:, j, :], tuple(v[:, 0, j * P:(j + 1) * P] for v in ckv),
                        weight(s0 % 2, HALF, HALF), True, True).then_inc(v_done, 1)
            pe.wait_ge(v_act, 4)
            pe.wait_ge(v_dve, 4)

            def expand(e):
                hd = e % MLA_HEADS
                if e >= 2:
                    pe.wait_ge(g_free, e - 1)
                s = SLABS["uq_nope" if e >= MLA_HEADS else "ukv"][0]
                if e == MLA_HEADS:
                    pe.wait_ge(w_split, s + 1)
                parts, kt = (cq, 2) if e >= MLA_HEADS else (ckv, 1)
                tile(s % 2, hd * kt * P, parts, kt, e % 2).then_inc(w_used if hd == MLA_HEADS - 1 else g_done, 1)

            def head_total(e):
                pe.wait_ge(g_sq, e + 1)
                if e == 0:
                    pe.wait_ge(rope_sq, 3)
                hd = e % MLA_HEADS
                over_features(wide(2 + e % 2), tmp[e % 2], ones[:], True, False)
                rope = q_rope_sq[:, hd // 2, :] if e >= MLA_HEADS else k_rope_sq[:]
                over_features(wide(2 + e % 2), rope, halves[:, 1 + (hd % 2 if e >= MLA_HEADS else 0), :],
                              False, True).then_inc(g_tot, 1)

            expand(0)
            for e in range(2 * MLA_HEADS):
                head_total(e)
                if e + 1 < 2 * MLA_HEADS:
                    expand(e + 1)
            def logits(unit):
                hd, t0 = unit // NT, unit % NT * P
                p, d = head_parts[hd % 2], unit - NT * MLA_HEADS
                if unit % NT == 0:
                    pe.wait_ge(head_split, 10 * (hd + 1))
                if d < 0:
                    if unit >= 2:
                        pe.wait_ge(a_exp, unit - 1)
                    for n in range(0, S, HALF):
                        out, keys = wide(unit % 2)[:, n:n + HALF], slice(n, n + HALF)
                        product(out, (p[0][:, t0:t0 + P], p[1][:, t0:t0 + P]), (p[2][:, keys], p[3][:, keys]), True, False)
                        nc.tensor.matmul(out, p[6][:, t0:t0 + P], p[7][:, keys], start=False, stop=False)
                        last = nc.tensor.matmul(out, p[6][0:64, t0:t0 + P], p[8][0:64, keys], start=False, stop=True)
                    last.then_inc(a_qk, 1)
                    return
                for m in range(2):
                    if d:
                        pe.wait_ge(e_red, 2 * d + m - 1)
                    else:
                        pe.wait_ge(a_exp, NT * MLA_HEADS - 1 + m)
                    lanes = slice(64 * m, 64 * m + 64)
                    for n in range(0, S, HALF):
                        out, keys = wide(m)[:, n:n + HALF], slice(n, n + HALF)
                        nc.tensor.matmul(out, p[m][:, t0:t0 + P], p[2 + m][:, keys], start=True, stop=False)
                        last = nc.tensor.matmul(out, p[m][lanes, t0:t0 + P], p[8][lanes, keys], start=False, stop=True)
                    last.then_inc(a_qk, 1)

            def transposes(group, j):
                if j == 0:
                    pe.wait_ge(*((a_exp, 4 * group + 4) if group < 2 * MLA_HEADS else (a_probs, 4 * (group - 2 * MLA_HEADS) + 4)))
                if 8 * group + j >= 2:
                    pe.wait_ge(a_ptlo, 8 * group + j - 1)
                for q in range(4):
                    last = nc.tensor.transpose(ps[:, 4 + j % 2, q * P:(q + 1) * P],
                                               prob_rows[group % 2][q][:, j * P:(j + 1) * P], ident[:])
                last.then_inc(a_tr, 1)

            def add_values(group, j):
                v = head_parts[group // 2 % 2][4:6]
                if j == 0 and group:
                    pe.wait_ge(a_out, group)
                pe.wait_ge(a_ptlo, 8 * group + j + 1)
                product(ps[:, 6 + group % 2, :], tuple(e[:, j * P:(j + 1) * P] for e in v),
                        tuple(e[:] for e in pt[j % 2]), j == 0, j == NT - 1).then_inc(a_pv, 1)

            def finish(group):
                add_values(group, NT - 2)
                add_values(group, NT - 1)
                pe.wait_ge(a_diag, group + 1)
                nc.tensor.matmul(ps[:, 7 - group % 2, :], ones[:], diagonal[:].rearrange("p q n -> p (q n)"),
                                 start=True, stop=True).then_inc(a_spread, 1)

            pe.wait_ge(g_free, 2 * MLA_HEADS)
            for q in range(4):
                logits(q)
            for group in range(GROUPS):
                for n in range(4):
                    if group + 1 < GROUPS:
                        logits(4 * (group + 1) + n)
                    if n:
                        add_values(group, 2 * n - 2)
                        add_values(group, 2 * n - 1)
                    elif group:
                        finish(group - 1)
                    transposes(group, 2 * n)
                    transposes(group, 2 * n + 1)
            finish(GROUPS - 1)
            def head_square_total(n):
                pe.wait_ge(s_sq, n + 1)
                if n >= 2:
                    pe.wait_ge(s_rs, n - 1)
                over_features(wide(2 + n % 2), tmp[n % 2], ones[:]).then_inc(s_tot, 1)

            s0 = SLABS["out_2"][0]
            pe.wait_ge(a_out, GROUPS)
            for s in range(2):
                pe.wait_ge(w_split, s0 + s + 1)
            for k in range(KT):
                pe.wait_ge(s_lo, k + 1)
                for s in range(2):
                    for n in range(0, S, HALF):
                        last = product(wide(s)[:, n:n + HALF], weight(s, k * P),
                                       tuple(e[:, k, n:n + HALF] for e in o_all), k == 0, k == KT - 1)
                    if k == KT - 1:
                        last.then_inc(w_used, 1)
                if k in (0, 1, 2, 4):
                    head_square_total((0, 1, 2, 4).index(k))
            with pe.Fori(1, 4) as it:
                for s in range(2):
                    pe.wait_ge(w_split, 2 * it + s0 + s + 1)
                    pe.wait_ge(x_added, 2 * it + 3 * KT + s - 1)
                    tile(s, 0, o_all, KT, s).then_inc(w_used, 1)
            total("mlp_2")
            first_tiles("mlp_2", "mlp_2", normed)
            s0 = SLABS["mlp_2"][0]

            def mlp_chunk(c, first=0):
                for j in range(first, CHUNK):
                    pe.wait_ge(w_split, 8 * c + s0 + j + 1)
                    pe.wait_ge(u_added, 8 * c + 5 + j)
                    tile(j % 2, 0, normed, KT, j).then_inc(w_used, 1)
                for m in range(KT):
                    if m % 2 == 0:
                        pe.wait_ge(w_split, 8 * c + s0 + 4 + m // 2 + 1)
                    if m < 4:
                        pe.wait_ge(u_relu, 4 * c + m + 1)
                    else:
                        pe.wait_ge(u_added, 8 * c + 8 + m - 3)
                    for k in range(CHUNK):
                        if m == 0:
                            pe.wait_ge(u_lo, 4 * c + 2 + k + 1)
                        for n in range(0, S, HALF):
                            last = product(wide(m % 4)[:, n:n + HALF], weight(m // 2 % 2, (m % 2 * CHUNK + k) * P),
                                           tuple(v[:, k, n:n + HALF] for v in hidden), k == 0, k == CHUNK - 1)
                    last.then_inc(w_used if m % 2 else first_half, 1)

            mlp_chunk(0, 2)
            with pe.Fori(1, FF2_TILES // CHUNK) as c:
                mlp_chunk(c)

        @block.scalar
        def _(act):
            step = Chain(act, act_step)

            def squares(name, src, ready):
                tiles, before = PRE[name]
                for k in range(tiles):
                    act.wait_ge(*ready(k))
                    if k >= 2:
                        act.wait_ge(n_added, before - PRE_ORDER.index(name) + k - 1)
                    nc.scalar.activation(tmp[k % 2][:], src(k), ACT.Square).then_inc(n_sq, 1)

            def post_square(post, k, src):
                if k >= 3:
                    act.wait_ge(n_acc, 7 * post + k - 2)
                nc.scalar.activation(tmp[k % 2][:] if k else acc[:], src, ACT.Square).then_inc(n_post_sq, 1)

            def inverse(r, width=D):
                act.wait_ge(n_sum, r + 1)
                step(nc.scalar.activation(acc[:], wide(2), ACT.Ln, bias=eps[:], scale=1.0 / width))
                nc.scalar.activation(acc[:], acc[:], ACT.Exp, scale=-0.5).then_inc(n_rs, 1)

            def round_hi(name, dst):
                tiles, before = PRE[name]
                for k in range(tiles):
                    act.wait_ge(n_tmp, before + k + 1)
                    nc.scalar.activation(dst[:, k, :], tmp[k % 2][:], ACT.Copy).then_inc(n_hi, 1)

            for k in range(4):
                act.dma_start(x_in[:, 2 * k:2 * k + 2, :], t["x"][:, 2 * k:2 * k + 2, :]).then_inc(x_in_landed[k], 16)
            for dst, name in ((cols, "cols"), (ident, "c_ident"), (tri, "c_tri"), (pool_fix, "c_pool_fix"),
                              (table, "rel_bias_table"), (onehot, "c_onehot"),
                              (table_2, "rel_bias_2"), (onehot_2, "c_onehot_2")):
                act.dma_start(dst[:], t[name]).then_inc(consts_in, 16)
            act.wait_ge(dve_consts, 1)
            squares("mix_pre", lambda k: x_in[:, k, :], lambda k: (x_in_landed[k // 2], 16))
            inverse(0)
            act.wait_ge(frow_done, 1)
            nc.scalar.activation(frow[:], ps[0:HEADS, 6, 0:384], ACT.Copy).then_inc(frow_copied, 1)
            nc.scalar.activation(frow_2[:], ps[0:DIFF_HEADS, 7, :], ACT.Copy).then_inc(frow_copied, 1)
            act.wait_ge(frow_copied, 2)
            act.dma_start(t["bias_rows"], frow[:]).then_inc(frow_out, 16)
            act.dma_start(t["bias_rows_2"], frow_2[:]).then_inc(frow_out, 16)
            round_hi("mix_pre", h1[0])
            for n, dst in enumerate((kidx[0][:], qidx[0][:, 0, :], qidx[0][:, 1, :], key[0][:])):
                act.wait_ge(w_used, SLABS["mix_in"][0] + 4 + n + 1)
                if n == 3:
                    act.wait_ge(frow_out, 32)
                nc.scalar.activation(dst, wide(n % 2), ACT.Copy).then_inc(in_hi, 1)
            act.wait_ge(mix_free, POOL_GROUPS)
            unit = 0
            for i in reversed(range(2, NT)):
                for hd in range(IDX_HEADS):
                    act.wait_ge(idx_done, unit + 1)
                    if unit >= 2:
                        act.wait_ge(idx_added, unit - 1)
                    n = (i + 1) * P
                    nc.scalar.activation(tmp[unit % 2][:, 0:n], wide(2 + unit % 2)[:, 0:n], ACT.Relu,
                                         scale=IDX_DIM ** -0.5 * IDX_HEADS ** -0.5).then_inc(idx_relu, 1)
                    unit += 1
            for dst, name, heads, width in ((bias, "bias_rows", HEADS, 384), (bias_2, "bias_rows_2", DIFF_HEADS, HALF)):
                rows = t[name]
                act.dma_start(dst[:], bass.AP(tensor=rows.tensor, offset=rows.offset,
                                              ap=[[1, P], [width, heads], [1, dst.shape[2]]])).then_inc(shifted_in, 16)
            act.dma_start(flip[:], t["c_flip"]).then_inc(shifted_in, 16)
            act.sem_inc(gate_free, 2)
            act.wait_ge(idx_added, unit)

            def stage(n, done, func, half, first):
                act.wait_ge(*done)
                if not first:
                    act.wait_ge(staged[half], 8 * (n - half))
                nc.scalar.activation(tmp[half][:], wide(half), func).then_inc(gate_free, 1)
                act.wait_ge(gate_free, n + 3)
                act.dma_start(t["gates"][n], tmp[half][:]).then_inc(staged[half], 16)

            s0 = SLABS["proj_pool"][0]
            for half in range(2):
                stage(half, ((first_half, w_used)[half], (1, s0 + 1)[half]), ACT.Copy, half, True)
            with act.Fori(1, 4) as it:
                for half in range(2):
                    stage(2 * it + half, ((first_half, w_used)[half], it + (1, s0 + 1)[half]), ACT.Copy, half, False)
            act.wait_ge(flipped, 1)
            nc.scalar.activation(bias[:].rearrange("p h u -> p (h u)"), ps[:, 4:8, :].rearrange("p b n -> p (b n)"),
                                 ACT.Copy).then_inc(bias_done, 1)
            act.wait_ge(flipped, 2)
            nc.scalar.activation(bias_2[:].rearrange("p h u -> p (h u)"), ps[:, 4:7, :].rearrange("p b n -> p (b n)"),
                                 ACT.Copy).then_inc(bias_done, 1)
            act.wait_ge(bias_done, 2)
            act.dma_start(t["bias_tiles_2"].rearrange("h p u -> p h u"), bias_2[:]).then_inc(bias_2_out, 16)
            act.wait_ge(bias_2_out, 16)
            s0 = SLABS["gate_pool"][0]
            with act.Fori(0, 8) as it:
                for half in range(2):
                    stage(2 * it + KT + half, (w_used, 2 * it + s0 + half + 1), ACT.Sigmoid, half, False)
            for k in range(KT):
                act.wait_ge(w_used, SLABS["query"][0] + k + 1)
                nc.scalar.activation(query[:, k, :], wide(k % 2), ACT.Copy, scale=P ** -0.5).then_inc(gate_free, 1)
            for half in range(2):
                act.wait_ge(staged[half], 16 * 12)
            def round_query(group):
                if group >= 2:
                    act.wait_ge(qk_done, 4 * (group - 1))
                i, g = group // 2, group % 2
                nc.scalar.activation(q_tile[g][0][:], query[:, 4 * g:4 * g + 4, i * P:(i + 1) * P], ACT.Copy).then_inc(qt_hi, 1)

            def mix_exps(unit):
                group, q = unit // 4, unit % 4
                row = mix_rows[group % 2][q][:, 0:(group // 2 + 1) * P]
                act.wait_ge(nmax_ready, unit + 1)
                nc.scalar.activation(row, row, ACT.Exp, bias=mix_stat(unit, 3),
                                     accum_out=mix_stat(unit, 4)).then_inc(exp_done, 1)

            def mix_out_hi(group):
                i, g = group // 2, group % 2
                act.wait_ge(pv_done, tiles_before(group + 1))
                nc.scalar.activation(att[0][:, 4 * g:4 * g + 4, i * P:(i + 1) * P],
                                     ps[:, 6 + g, :].rearrange("p (h q) -> p h q", h=4), ACT.Copy).then_inc(o_hi, 1)

            act.wait_ge(masks_ready, 1)
            act.wait_ge(gate_free, 2 + 4 * KT)
            for group in range(2):
                round_query(group)
            for q in range(4):
                mix_exps(q)
            for group in range(2 * NT):
                for n in range(4):
                    if n == 0 and group:
                        mix_out_hi(group - 1)
                    for j in tiles_of(group, n):
                        n_tr = tiles_before(group) + j
                        act.wait_ge(tr_done, n_tr + 1)
                        if n_tr >= 2:
                            act.wait_ge(pv_done, n_tr - 1)
                        nc.scalar.activation(probs_t[n_tr % 2][0][:], ps[:, 4 + n_tr % 2, :], ACT.Copy).then_inc(pt_hi, 1)
                    if group + 1 < 2 * NT:
                        mix_exps(4 * (group + 1) + n)
                    if n == 1 and group + 2 < 2 * NT:
                        round_query(group + 2)
            mix_out_hi(2 * NT - 1)
            act.wait_ge(qk_done, HEADS * NT)
            for k in range(KT):
                if k >= 2:
                    act.wait_ge(merge_free, 2 + k - 1)
                for n in range(3):
                    act.dma_start(gated[k % 2][:, n, :], t["gates"][KT * n + k]).then_inc(gates_in[k % 2], 16)
            act.sem_inc(y_free, 2)
            act.wait_ge(merge_free, 2 + KT)
            act.dma_start(x[:], t["x"]).then_inc(x_landed, 16)
            act.dma_start(mem_in[:], t["mem"]).then_inc(mem_landed, 16)
            for k in range(KT):
                act.wait_ge(w_used, SLABS["mix_out"][0] + k + 1)
                post_square(0, k, wide(k % 2))
                nc.scalar.activation(y[:, k, :], wide(k % 2), ACT.Copy).then_inc(y_free, 1)
                if k == 1:
                    act.wait_ge(mem_landed, 16)
                    nc.scalar.activation(mem_sq[:], mem_in[:], ACT.Square).then_inc(mem_squared, 1)
                if k == 4:
                    act.wait_ge(mem_total, 1)
                    step(nc.scalar.activation(mem_rms[:], ps[:, 6, 0:M], ACT.Ln, bias=eps[:], scale=1.0 / D))
                    nc.scalar.activation(mem_rms[:], mem_rms[:], ACT.Exp, scale=-0.5).then_inc(mem_rs, 1)
                if k == 6:
                    act.wait_ge(mem_scaled, KT)
                    nc.scalar.activation(memn[0][:], mem_in[:], ACT.Copy).then_inc(mem_hi, 1)
            inverse(1)
            squares("mem_pre", lambda k: x[:, k, :], lambda k: (x_added, k + 1))
            act.wait_ge(w_used, SLABS["mem_value"][0] + 4)
            nc.scalar.activation(kmem[0][:], wide(0).rearrange("p (h m) -> p h m", h=MEM_HEADS), ACT.Copy).then_inc(mkv_hi, 1)
            nc.scalar.activation(vmem[0][:], wide(1).rearrange("p (j n) -> p j n", j=MT), ACT.Copy).then_inc(mkv_hi, 1)
            inverse(2)
            round_hi("mem_pre", normed[0])
            for n in range(MEM_HEADS):
                act.wait_ge(w_used, SLABS["mem_query"][0] + n + 1)
                nc.scalar.activation(qm[0][:, n, :], wide(n % 2), ACT.Copy, scale=P ** -0.5).then_inc(mq_hi, 1)
            def mem_exps(n):
                act.wait_ge(m_max, n + 1)
                if n >= 2:
                    act.wait_ge(m_tr, MT * (n - 1))
                for q in range(4):
                    nc.scalar.activation(mprobs[:, n % 2, q, :], wide(n % 2)[:, q * M:(q + 1) * M], ACT.Exp,
                                         bias=mstat[:, n % 2, 1, q:q + 1],
                                         accum_out=mstat[:, n % 2, 2, q:q + 1]).then_inc(m_exp, 1)

            def mem_out_hi(n):
                act.wait_ge(m_pv, MT * (n + 1))
                t0 = n % 2 * HALF
                nc.scalar.activation(om[0][:, n // 2, t0:t0 + HALF], ps[:, 6 + n % 2, :], ACT.Copy).then_inc(m_ohi, 1)

            mem_exps(0)
            for n in range(2 * MEM_HEADS):
                if n:
                    mem_out_hi(n - 1)
                for j in range(MT):
                    act.wait_ge(m_tr, MT * n + j + 1)
                    if n:
                        act.wait_ge(m_pv, MT * (n - 1) + j + 1)
                    nc.scalar.activation(mpt[j][0][:], ps[:, 4 + j, :], ACT.Copy).then_inc(m_pthi, 1)
                if n + 1 < 2 * MEM_HEADS:
                    mem_exps(n + 1)
            mem_out_hi(2 * MEM_HEADS - 1)
            act.wait_ge(m_olo, 2 * MEM_HEADS)
            for k in range(KT):
                act.wait_ge(*((w_used, SLABS["mem_out"][0] + k // 2 + 1) if k % 2 else (first_half, 4 + k // 2 + 1)))
                post_square(1, k, wide(k % 2))
                nc.scalar.activation(y[:, k, :], wide(k % 2), ACT.Copy).then_inc(y_free, 1)
            inverse(3)
            squares("ffn_pre", lambda k: x[:, k, :], lambda k: (x_added, KT + k + 1))
            inverse(4)
            round_hi("ffn_pre", normed[0])
            s0 = SLABS["ffn"][0]

            def ffn_hidden(c, tiles):
                for j in range(tiles):
                    act.wait_ge(w_used, 12 * c + s0 + 2 * j + 1)
                    act.wait_ge(f_lo, 4 * c + j + 1)
                    nc.scalar.activation(tmp[j % 2][:], wide(2 * (j % 2)), ACT.Silu).then_inc(f_silu, 1)
                    act.wait_ge(f_mul, 4 * c + j + 1)
                    nc.scalar.activation(hidden[0][:, j, :], tmp[j % 2][:], ACT.Copy).then_inc(f_hi, 1)

            with act.Fori(0, FF_TILES // CHUNK) as c:
                ffn_hidden(c, CHUNK)
            ffn_hidden(FF_TILES // CHUNK, FF_TILES % CHUNK)
            for k in range(KT):
                act.wait_ge(f_added, 8 + 8 * (FF_TILES // CHUNK) + k + 1)
                post_square(2, k, y[:, k, :])
            inverse(5)
            squares("attn_2", lambda k: x[:, k, :], lambda k: (x_added, 2 * KT + k + 1))
            for dst, name in ((cos, "c_cos"), (sin, "c_sin"), (halves, "c_halves")):
                act.dma_start(dst[:], t[name]).then_inc(tables_in, 16)
            inverse(6)
            round_hi("attn_2", normed[0])
            act.wait_ge(lam_sum, 1)
            nc.scalar.activation(lam_ab, lam_ab, ACT.Exp).then_inc(lam_exp, 1)
            s0 = SLABS["in_2"][0]
            for n, dst in enumerate((c_q[:, 0, :], c_q[:, 1, :], c_kv[:, 0, :])):
                act.wait_ge(w_used, s0 + n + 1)
                nc.scalar.activation(dst, wide(n % 2), ACT.Copy).then_inc(c_free, 1)
            squares("q_a", lambda k: c_q[:, k, :], lambda k: (c_free, k + 1))
            inverse(7, 2 * P)
            round_hi("q_a", cq[0])
            act.wait_ge(n_lo, PRE["kv_a"][1])
            squares("kv_a", lambda k: c_kv[:, k, :], lambda k: (c_free, 3))
            inverse(8, P)
            round_hi("kv_a", ckv[0])
            act.wait_ge(d_free, 2)
            nc.scalar.activation(k_rope_sq[:], k_rope[:], ACT.Square).then_inc(rope_sq, 1)
            act.wait_ge(n_lo, PRE["kv_a"][1] + 1)
            with act.Fori(0, DIFF_HEADS) as it:
                for e in range(2):
                    act.wait_ge(w_used, 2 * it + s0 + 5 + e + 1)
                    nc.scalar.activation(tmp[e][:], wide(1 - e), ACT.Square).then_inc(d_sq, 1)
                    act.wait_ge(d_tot, 2 * it + e + 1)
                    act.wait_ge(d_free, 2 * it + e + 1)
                    nc.scalar.activation(d_rms[e][:], wide(2 + e), ACT.Ln, bias=eps[:], scale=1.0 / 64).then_inc(d_ln, 1)
                    act.wait_ge(d_ln, 2 * it + e + 1)
                    nc.scalar.activation(d_rms[e][:], d_rms[e][:], ACT.Exp, scale=-0.5).then_inc(d_rs, 1)
                    act.wait_ge(d_free, 2 * it + e + 3)
                    act.dma_start(t["diff_qk"][2 * it + e], d_out[e][:]).then_inc(d_stored[e], 16)
            act.wait_ge(w_used, SLABS["diff_value"][0] + 4)
            for j in range(0, NT, 2):
                nc.scalar.activation(d_value[:, j, :], ps[:, j, :], ACT.Copy).then_inc(dv_act, 1)
            act.wait_ge(dv_act, 4)
            act.wait_ge(dv_dve, 4)
            for hd in range(DIFF_HEADS):
                act.dma_start(t["diff_v"][hd], d_value[:, :, hd * P:(hd + 1) * P]).then_inc(dv_stored, 16)
            for j in range(0, NT, 2):
                act.wait_ge(v_done, j + 1)
                nc.scalar.activation(v_value[:, j, :], ps[:, j, :], ACT.Copy).then_inc(v_act, 1)
            act.wait_ge(v_act, 4)
            act.wait_ge(v_dve, 4)
            for hd in range(MLA_HEADS):
                act.dma_start(t["mla_v"][hd], v_value[:, :, hd * P:(hd + 1) * P]).then_inc(v_stored, 16)
            for p in range(2):
                act.wait_ge(r_free, p + 1)
                nc.scalar.activation(q_rope_sq[:, p, :], q_rope[:, p, :], ACT.Square).then_inc(rope_sq, 1)
            for e in range(2):
                act.wait_ge(d_stored[e], 16 * DIFF_HEADS)

            def head_square(e):
                hd, is_q = e % MLA_HEADS, e >= MLA_HEADS
                act.wait_ge(*((w_used, SLABS["uq_nope" if is_q else "ukv"][0] + 1) if hd == MLA_HEADS - 1
                              else (g_done, (MLA_HEADS - 1) * is_q + hd + 1)))
                nc.scalar.activation(tmp[e % 2][:], wide(e % 2), ACT.Square).then_inc(g_sq, 1)

            def store_parts(e):
                r0 = ROPE * (e % 2) if e >= MLA_HEADS else 0
                act.wait_ge(g_roped, e + 1)
                act.dma_start(t["mla_nope"][e], g_nope[e % 2][:]).then_inc(g_stored[e % 2], 16)
                act.dma_start(t["mla_rope"][e], g_rope[e % 2][r0:r0 + ROPE, :]).then_inc(g_stored[e % 2], 16)

            head_square(0)
            for e in range(2 * MLA_HEADS):
                act.wait_ge(g_tot, e + 1)
                if e >= 2:
                    act.wait_ge(g_roped, e - 1)
                step(nc.scalar.activation(g_rms[e % 2][:], wide(2 + e % 2), ACT.Ln, bias=eps[:],
                                          scale=1.0 / (P + ROPE)))
                nc.scalar.activation(g_rms[e % 2][:], g_rms[e % 2][:], ACT.Exp, scale=-0.5).then_inc(g_rs, 1)
                if e + 1 < 2 * MLA_HEADS:
                    head_square(e + 1)
                store_parts(e)
            def exps(unit):
                g, q, d = unit // 4 % 2, unit % 4, unit - NT * MLA_HEADS
                act.wait_ge(a_max, unit + 1)
                if d < 0:
                    if unit >= 8:
                        act.wait_ge(a_tr, 2 * (unit - unit % 4) - 8)
                    nc.scalar.activation(prob_rows[g][q][:], wide(unit % 2), ACT.Exp, bias=mstat[:, g, 1, q:q + 1],
                                         scale=(P + ROPE) ** -0.5, accum_out=mstat[:, g, 2, q:q + 1]).then_inc(a_exp, 1)
                    return
                for m, row in enumerate((prob_rows[g][q], second[unit % 2])):
                    nc.scalar.activation(row[:], row[:], ACT.Exp, bias=e_stat[:, unit % 8, 3, m:m + 1],
                                         accum_out=e_stat[:, unit % 8, 4, m:m + 1]).then_inc(a_exp, 1)

            def round_probs(group, j):
                act.wait_ge(a_tr, 8 * group + j + 1)
                if 8 * group + j >= 2:
                    act.wait_ge(a_pv, 8 * group + j - 1)
                nc.scalar.activation(pt[j % 2][0][:], ps[:, 4 + j % 2, :], ACT.Copy).then_inc(a_pthi, 1)

            def copy_head(group):
                act.wait_ge(a_pv, 8 * group + 8)
                if group:
                    act.wait_ge(o_stored, 16 * group)
                nc.scalar.activation(o_stage[:], ps[:, 6 + group % 2, :], ACT.Copy).then_inc(a_copied, 1)

            def store_head(group):
                g = group % 2
                act.wait_ge(a_out, group + 1)
                act.dma_start(t["heads_out"][group // 2][:, g * HALF:(g + 1) * HALF], o_stage[:]).then_inc(o_stored, 16)

            for q in range(4):
                exps(q)
            for e in range(2):
                act.wait_ge(g_stored[e], 32 * MLA_HEADS)
            for group in range(GROUPS):
                for n in range(4):
                    if n == 0 and group:
                        copy_head(group - 1)
                    round_probs(group, 2 * n)
                    round_probs(group, 2 * n + 1)
                    if group + 1 < GROUPS:
                        exps(4 * (group + 1) + n)
                    if n == 1 and group:
                        store_head(group - 1)
                    if n == 3 and group == GROUPS - 2:
                        act.wait_ge(a_pv, 8 * (GROUPS - 2))
                        act.wait_ge(o_stored, 16 * (GROUPS - 2))
                        for k in range(KT - 1):
                            act.dma_start(o_in[:, k, :], t["heads_out"][k]).then_inc(o_landed, 16)
            copy_head(GROUPS - 1)
            store_head(GROUPS - 1)
            act.wait_ge(o_stored, 16 * GROUPS)
            act.dma_start(o_in[:, KT - 1, :], t["heads_out"][KT - 1]).then_inc(o_last, 16)

            def out_hi(k):
                if k >= MLA_HEADS:
                    act.wait_ge(s_scaled, k - MLA_HEADS + 1)
                nc.scalar.activation(o_all[0][:, k, :], o_in[:, k, :], ACT.Copy).then_inc(s_hi, 1)

            def out_square(n):
                if n >= 2:
                    act.wait_ge(s_tot, n - 1)
                if n == DIFF_HEADS - 1:
                    act.wait_ge(o_last, 16)
                nc.scalar.activation(tmp[n % 2][:], o_in[:, MLA_HEADS + n, :], ACT.Square).then_inc(s_sq, 1)

            def out_inverse(n):
                act.wait_ge(s_tot, n + 1)
                if n >= 2:
                    act.wait_ge(s_scaled, n - 1)
                step(nc.scalar.activation(o_rms[n % 2][:], wide(2 + n % 2), ACT.Ln, bias=eps[:], scale=1.0 / P))
                nc.scalar.activation(o_rms[n % 2][:], o_rms[n % 2][:], ACT.Exp, scale=-0.5).then_inc(s_rs, 1)

            act.wait_ge(o_landed, 16 * (KT - 1))
            act.wait_ge(a_probs, 4 * NT)
            act.wait_ge(a_pv, 8 * GROUPS)
            out_hi(0)
            out_square(0)
            out_hi(1)
            out_square(1)
            out_hi(2)
            out_inverse(0)
            out_hi(3)
            out_square(2)
            out_inverse(1)
            out_hi(4)
            out_square(3)
            out_inverse(2)
            out_hi(5)
            out_inverse(3)
            out_hi(6)
            out_hi(7)
            squares("mlp_2", lambda k: x[:, k, :], lambda k: (x_added, 3 * KT + k + 1))
            inverse(9)
            round_hi("mlp_2", normed[0])
            s0 = SLABS["mlp_2"][0]
            with act.Fori(0, FF2_TILES // CHUNK) as c:
                for j in range(CHUNK):
                    act.wait_ge(w_used, 8 * c + s0 + j + 1)
                    act.wait_ge(u_lo, 4 * c + j + 1)
                    nc.scalar.activation(tmp[j % 2][:], wide(j), ACT.Relu).then_inc(u_relu, 1)
                    act.wait_ge(u_sq, 4 * c + j + 1)
                    nc.scalar.activation(hidden[0][:, j, :], tmp[j % 2][:], ACT.Copy).then_inc(u_hi, 1)
            for m in range(KT):
                act.wait_ge(u_added, 8 * (FF2_TILES // CHUNK) + m + 1)
                act.dma_start(out[:, m, :], x[:, m, :]).then_inc(stored, 16)
            act.wait_ge(stored, 16 * KT)
        @block.vector
        def _(dve):
            step = Chain(dve, dve_step)
            tt, ts, stt = nc.vector.tensor_tensor, nc.vector.tensor_scalar, nc.vector.scalar_tensor_tensor

            def add_square(post, k):
                dve.wait_ge(n_post_sq, KT * post + k + 1)
                if k >= 2:
                    dve.wait_ge(n_acc, 7 * post + k - 1)
                tt(acc[:], acc[:], tmp[k % 2][:], ALU.add).then_inc(n_acc, 1)

            def scaled(r, name, src, dst):
                tiles, before = PRE[name]

                def rest(k):
                    dve.wait_ge(n_hi, before + k + 1)
                    tt(dst[1][:, k, :], tmp[k % 2][:], dst[0][:, k, :].bitcast(F32), ALU.subtract).then_inc(n_lo, 1)

                dve.wait_ge(n_rs, r + 1)
                for k in range(tiles):
                    if k >= 2:
                        dve.wait_ge(n_lo, before + k - 1)
                    stt(tmp[k % 2][:], src[:, k, :], col(name, k), acc[:], ALU.mult, ALU.mult).then_inc(n_tmp, 1)
                    if k:
                        rest(k - 1)
                rest(tiles - 1)

            def residual(r, gain):
                dve.wait_ge(n_rs, r + 1)
                for k in range(KT):
                    step(stt(y[:, k, :], y[:, k, :], col(gain, k), acc[:], ALU.mult, ALU.mult))
                    tt(x[:, k, :], x[:, k, :], y[:, k, :], ALU.add).then_inc(x_added, 1)

            nc.vector.memset(eps[:], EPS)
            step(nc.vector.memset(ones[:], 1.0))
            dve.wait_ge(consts_in, 16 * N_CONSTS)
            nc.vector.tensor_copy(ident16[:], ident[:]).then_inc(dve_consts, 1)
            dve.wait_ge(dve_consts, 1)
            scaled(0, "mix_pre", x_in, h1)
            dve.sem_inc(in_free, 2)

            def pool_window(g):
                cur = u[:, g, :]
                for e in range(g + 1):
                    n, nxt = 1 << e, win[e % 2]
                    nc.vector.tensor_copy(nxt[:, 0:n], cur[:, 0:n])
                    step(tt(nxt[:, n:S], cur[:, n:S], cur[:, 0:S - n], ALU.add))
                    cur = nxt[:]
                step(tt(cur[:, 0:16], cur[:, 0:16], pool_fix[:, g, :], ALU.mult))
                step(stt(tmp[0][:], cur, 1.0 / (2 << g), u[:, g, :], ALU.mult, ALU.subtract))
                step(nc.vector.tensor_copy(pooled[0][:, g, :], tmp[0][:]))
                tt(pooled[1][:, g, :], tmp[0][:], pooled[0][:, g, :].bitcast(F32), ALU.subtract).then_inc(pooled_ready, 1)

            for k in range(4):
                dve.wait_ge(w_used, SLABS["mix_in"][0] + k + 1)
                nc.vector.tensor_copy(u[:, k, :], wide(k % 2)).then_inc(in_free, 1)
            for n, (hi, lo) in enumerate(((kidx[0][:], kidx[1][:]), (qidx[0][:, 0, :], qidx[1][:, 0, :]),
                                          (qidx[0][:, 1, :], qidx[1][:, 1, :]), (key[0][:], key[1][:]))):
                dve.wait_ge(in_hi, n + 1)
                tt(lo, wide(n % 2), hi.bitcast(F32), ALU.subtract).then_inc(in_free, 1)
                dve.wait_ge(in_free, 2 + 4 + n + 1)
                pool_window(n)
            for b in range(3):
                m = min(3, NT - 3 * b)
                dve.wait_ge(value_done, 3 * b + m)
                nc.vector.tensor_copy(value_raw[:, 3 * b:3 * b + m, :], ps[:, 4 + b, 0:m * VW].rearrange(
                    "p (j n) -> p j n", j=m)).then_inc(value_free, 1)
            for g in range(POOL_GROUPS):
                dve.wait_ge(*((pool_done, g + 1) if g < 2 else (w_used, SLABS["value_pool"][0] + g - 1)))
                step(ts(tmp[g % 2][:], wide(g % 2), col("pool_scale", g), None, ALU.mult))
                step(nc.vector.tensor_copy(mixed[0][:, g, :], tmp[g % 2][:]))
                tt(mixed[1][:, g, :], tmp[g % 2][:], mixed[0][:, g, :].bitcast(F32), ALU.subtract).then_inc(mix_free, 1)
            unit = 0
            for i in reversed(range(2, NT)):
                sc = score[:, score_at[i]:score_at[i] + (i + 1) * P]
                for hd in range(IDX_HEADS):
                    dve.wait_ge(idx_relu, unit + 1)
                    part, w = tmp[unit % 2][:, 0:(i + 1) * P], value_raw[:, i, P + hd:P + hd + 1]
                    if hd == 0:
                        ins = ts(sc, part, w, None, ALU.mult)
                    else:
                        dve.wait_ge(idx_added, unit)
                        ins = stt(sc, part, w, sc, ALU.mult, ALU.add)
                    ins.then_inc(idx_added, 1)
                    unit += 1
                dve.wait_ge(idx_added, unit)
                step(tt(sc[:, i * P:(i + 1) * P], sc[:, i * P:(i + 1) * P], tri[:], ALU.add))
            for both in ((7, 2), (6, 3), (5, 4)):
                scs = [score[:, score_at[i]:score_at[i] + (i + 1) * P] for i in both]
                for _ in range(ROUNDS):
                    found = step.n
                    for e, sc in enumerate(scs):
                        if step.n > 2:
                            dve.wait_ge(dve_step, step.n - 1)
                        step.n += 1
                        nc.vector.max(top8[:, e, :], sc).then_inc(dve_step, 1)
                    for e, sc in enumerate(scs):
                        dve.wait_ge(dve_step, found + e + 1)
                        step.n += 1
                        nc.vector.match_replace(sc, top8[:, e, :], sc, TAKEN).then_inc(dve_step, 1)
            dve.wait_ge(dve_step, step.n)
            for i in range(2, NT):
                ts(mask[:, mask_at[i]:mask_at[i] + (i + 1) * P], score[:, score_at[i]:score_at[i] + (i + 1) * P],
                   TAKEN, NEG, ALU.not_equal, ALU.mult)
            nc.vector.memset(mask[:, mask_at[1]:mask_at[1] + P], 0.0)
            nc.vector.tensor_copy(mask[:, mask_at[1] + P:mask_at[1] + 2 * P], tri[:])
            nc.vector.tensor_copy(mask[:, 0:P], tri[:]).then_inc(masks_ready, 1)
            dve.wait_ge(idx_done, unit)
            step(nc.vector.tensor_copy(value[0][:], value_raw[:, :, 0:P]))
            tt(value[1][:], value_raw[:, :, 0:P], value[0][:].bitcast(F32), ALU.subtract).then_inc(value_split, 1)
            dve.wait_ge(bias_done, 1)
            dve.wait_ge(masks_ready, 1)
            def rest_query(group):
                i, g = group // 2, group % 2
                dve.wait_ge(qt_hi, group + 1)
                tt(q_tile[g][1][:], query[:, 4 * g:4 * g + 4, i * P:(i + 1) * P], q_tile[g][0][:].bitcast(F32),
                   ALU.subtract).then_inc(qt_lo, 1)

            def mix_maxima(unit):
                group, q = unit // 4, unit % 4
                i, hd = group // 2, 4 * (group % 2) + q
                row, n = mix_rows[group % 2][q], (i + 1) * P
                late = max(0, i - 1) * P
                if q == 0 and group >= 2:
                    dve.wait_ge(tr_done, tiles_before(group - 1))
                dve.wait_ge(qk_done, unit + 1)
                if late:
                    nc.vector.tensor_tensor_reduce(row[:, 0:late], wide(unit % 2)[:, 0:late],
                                                   bias[:, hd, 0:1].broadcast_to([P, late]), 1.0, TAKEN, ALU.add,
                                                   ALU.max, mix_stat(unit, 1))
                nc.vector.tensor_tensor_reduce(row[:, late:n], wide(unit % 2)[:, late:n],
                                               bias[:, hd, 2 * P - (n - late):2 * P], 1.0, TAKEN, ALU.add, ALU.max,
                                               mix_stat(unit, 0)).then_inc(logits_ready, 1)
                dve.wait_ge(logits_ready, unit + 1)
                if late:
                    step(tt(mix_stat(unit, 0), mix_stat(unit, 0), mix_stat(unit, 1), ALU.max))
                ts(mix_stat(unit, 3), mix_stat(unit, 0), -1.0, None, ALU.mult).then_inc(nmax_ready, 1)

            def mix_inverse(unit):
                dve.wait_ge(exp_done, unit + 1)
                nc.vector.reciprocal(mix_stat(unit, 5), mix_stat(unit, 4)).then_inc(inv_ready, 1)

            def mix_out_lo(group):
                i, g = group // 2, group % 2
                dve.wait_ge(o_hi, group + 1)
                tt(att[1][:, 4 * g:4 * g + 4, i * P:(i + 1) * P], ps[:, 6 + g, :].rearrange("p (h q) -> p h q", h=4),
                   att[0][:, 4 * g:4 * g + 4, i * P:(i + 1) * P].bitcast(F32), ALU.subtract).then_inc(o_lo, 1)

            dve.wait_ge(value_split, 1)
            for group in range(2):
                rest_query(group)
            for q in range(4):
                mix_maxima(q)
                mix_inverse(q)
            for group in range(2 * NT):
                for n in range(4):
                    unit = 4 * (group + 1) + n
                    more = group + 1 < 2 * NT
                    if more:
                        mix_maxima(unit)
                    if n == 0 and group:
                        mix_out_lo(group - 1)
                    for j in tiles_of(group, n):
                        n_tr = tiles_before(group) + j
                        dve.wait_ge(pt_hi, n_tr + 1)
                        tt(probs_t[n_tr % 2][1][:], ps[:, 4 + n_tr % 2, :], probs_t[n_tr % 2][0][:].bitcast(F32),
                           ALU.subtract).then_inc(pt_lo, 1)
                    if more and n:
                        mix_inverse(unit - 1)
                    if more and n == 3:
                        mix_inverse(unit)
                    if n == 1 and group + 2 < 2 * NT:
                        rest_query(group + 2)
            mix_out_lo(2 * NT - 1)
            dve.sem_inc(merge_free, 2)
            for k in range(KT):
                pool_part, pool_gate, attn_gate = (gated[k % 2][:, n, :] for n in range(3))
                dve.wait_ge(gates_in[k % 2], 48 * (k // 2 + 1))
                tt(pool_part, pool_part, pool_gate, ALU.mult)
                dve.wait_ge(w_used, SLABS["proj_attn"][0] + k + 1)
                step(tt(attn_gate, wide(k % 2), attn_gate, ALU.mult))
                step(tt(pool_part, pool_part, attn_gate, ALU.add))
                step(nc.vector.tensor_copy(merged[0][:, k, :], pool_part))
                tt(merged[1][:, k, :], pool_part, merged[0][:, k, :].bitcast(F32), ALU.subtract).then_inc(merge_free, 1)
            for k in range(1, KT):
                add_square(0, k)
                if k == 4:
                    dve.wait_ge(mem_rs, 1)
                    for e in range(KT):
                        stt(mem_in[:, e, :], mem_in[:, e, :], col("mem_kv", e), mem_rms[:], ALU.mult,
                            ALU.mult).then_inc(mem_scaled, 1)
            dve.wait_ge(mem_hi, 1)
            tt(memn[1][:], mem_in[:], memn[0][:].bitcast(F32), ALU.subtract).then_inc(mem_lo, 1)
            dve.wait_ge(x_landed, 16)
            dve.wait_ge(y_free, 2 + KT)
            residual(1, "mix_post")
            dve.wait_ge(mkv_hi, 1)
            tt(kmem[1][:], wide(0).rearrange("p (h m) -> p h m", h=MEM_HEADS), kmem[0][:].bitcast(F32),
               ALU.subtract).then_inc(mkv_lo, 1)
            dve.wait_ge(mkv_hi, 2)
            tt(vmem[1][:], wide(1).rearrange("p (j n) -> p j n", j=MT), vmem[0][:].bitcast(F32),
               ALU.subtract).then_inc(mkv_lo, 1)
            scaled(2, "mem_pre", x, normed)
            dve.sem_inc(mq_lo, 2)
            for n in range(MEM_HEADS):
                dve.wait_ge(mq_hi, n + 1)
                stt(qm[1][:, n, :], wide(n % 2), P ** -0.5, qm[0][:, n, :].bitcast(F32), ALU.mult,
                    ALU.subtract).then_inc(mq_lo, 1)
            def mem_maxima(n):
                biggest, minus = (mstat[:, n % 2, e, :] for e in range(2))
                dve.wait_ge(m_qk, n + 1)
                step(nc.vector.tensor_reduce(biggest, wide(n % 2).rearrange("p (q m) -> p q m", q=4), AX.X, ALU.max))
                ts(minus, biggest, -1.0, None, ALU.mult).then_inc(m_max, 1)

            def mem_normalise(n):
                total, inv = (mstat[:, n % 2, e, :] for e in range(2, 4))
                dve.wait_ge(m_exp, 4 * (n + 1))
                step(nc.vector.reciprocal(inv, total))
                tt(mprobs[:, n % 2], mprobs[:, n % 2], inv.unsqueeze(2).broadcast_to([P, 4, M]),
                   ALU.mult).then_inc(m_probs, 1)

            def mem_out_lo(n):
                dve.wait_ge(m_ohi, n + 1)
                t0 = n % 2 * HALF
                tt(om[1][:, n // 2, t0:t0 + HALF], ps[:, 6 + n % 2, :], om[0][:, n // 2, t0:t0 + HALF].bitcast(F32),
                   ALU.subtract).then_inc(m_olo, 1)

            mem_maxima(0)
            mem_normalise(0)
            for n in range(2 * MEM_HEADS):
                if n + 1 < 2 * MEM_HEADS:
                    mem_maxima(n + 1)
                if n:
                    mem_out_lo(n - 1)
                for j in range(MT):
                    dve.wait_ge(m_pthi, MT * n + j + 1)
                    tt(mpt[j][1][:], ps[:, 4 + j, :], mpt[j][0][:].bitcast(F32), ALU.subtract).then_inc(m_ptlo, 1)
                if n + 1 < 2 * MEM_HEADS:
                    mem_normalise(n + 1)
            mem_out_lo(2 * MEM_HEADS - 1)
            for k in range(1, KT):
                add_square(1, k)
            dve.wait_ge(y_free, 2 + 2 * KT)
            residual(3, "mem_post")
            scaled(4, "ffn_pre", x, normed)
            dve.sem_inc(f_lo, 2)
            nc.vector.memset(y[:], 0.0).then_inc(y_zero, 1)
            dve.wait_ge(y_zero, 1)
            dve.sem_inc(f_added, 8)
            s0 = SLABS["ffn"][0]

            def ffn_hidden(c, tiles, down_before):
                for j in range(tiles):
                    part = tmp[j % 2]
                    dve.wait_ge(w_used, 12 * c + s0 + 2 * j + 2)
                    dve.wait_ge(f_silu, 4 * c + j + 1)
                    tt(part[:], part[:], wide(2 * (j % 2) + 1), ALU.mult).then_inc(f_mul, 1)
                    dve.wait_ge(f_hi, 4 * c + j + 1)
                    tt(hidden[1][:, j, :], part[:], hidden[0][:, j, :].bitcast(F32), ALU.subtract).then_inc(f_lo, 1)
                per = 8 // tiles
                for m in range(KT):
                    if m % per == per - 1:
                        dve.wait_ge(w_used, 12 * c + s0 + 2 * tiles + m // per + 1)
                    else:
                        dve.wait_ge(first_half, down_before + m - m // per + 1)
                    tt(y[:, m, :], y[:, m, :], wide(m % 4), ALU.add).then_inc(f_added, 1)

            with dve.Fori(0, FF_TILES // CHUNK) as c:
                ffn_hidden(c, CHUNK, 4 * c + 8)
            ffn_hidden(FF_TILES // CHUNK, FF_TILES % CHUNK, 4 * (FF_TILES // CHUNK) + 8)
            for k in range(1, KT):
                add_square(2, k)
            residual(5, "ffn_post")
            lam = cols[:, COLS["lambda"][0]:COLS["lambda"][0] + 256].rearrange("p (v n) -> p v n", v=4)
            ts(col("diff_q"), col("diff_q"), 64 ** -0.5, None, ALU.mult)
            ts(col("diff_out"), col("diff_out"), 1.0 - LAM_INIT, None, ALU.mult)
            tt(lam[:, 0, :], lam[:, 0, :], lam[:, 1, :], ALU.mult)
            step(tt(lam[:, 2, :], lam[:, 2, :], lam[:, 3, :], ALU.mult))
            nc.vector.tensor_reduce(lam_ab[:, 0:1], lam[:, 0, :], AX.X, ALU.add)
            nc.vector.tensor_reduce(lam_ab[:, 1:2], lam[:, 2, :], AX.X, ALU.add).then_inc(lam_sum, 1)
            scaled(6, "attn_2", x, normed)
            dve.wait_ge(lam_exp, 1)
            step(tt(minus_lam, lam_ab[:, 1:2], lam_ab[:, 0:1], ALU.subtract))
            step(ts(minus_lam, minus_lam, -LAM_INIT, None, ALU.add))
            s0 = SLABS["in_2"][0]
            dve.wait_ge(tables_in, 48)
            dve.wait_ge(w_used, s0 + 4)
            tt(k_rope[:], wide(1), cos[:], ALU.mult).then_inc(d_free, 1)
            scaled(7, "q_a", c_q, cq)
            dve.wait_ge(w_used, s0 + 5)
            dve.wait_ge(n_lo, PRE["kv_a"][1])
            dve.wait_ge(n_sq, PRE["kv_a"][1] + 1)
            step(tt(tmp[1][:], wide(0), sin[:], ALU.mult))
            tt(k_rope[:], k_rope[:], tmp[1][:], ALU.add).then_inc(d_free, 1)
            scaled(8, "kv_a", c_kv, ckv)
            for part, gain in enumerate(("diff_q", "diff_k")):
                with dve.Fori(2 * part, 2 * part + 2) as it:
                    for e in range(2):
                        dve.wait_ge(d_rs, 2 * it + e + 1)
                        stt(d_out[e][:], wide(1 - e), col(gain), d_rms[e][:], ALU.mult, ALU.mult).then_inc(d_free, 1)
                    for e in range(2):
                        dve.wait_ge(d_stored[e], 16 * it + 16)
            dve.wait_ge(w_used, SLABS["diff_value"][0] + 4)
            for j in range(1, NT, 2):
                nc.vector.tensor_copy(d_value[:, j, :], ps[:, j, :]).then_inc(dv_dve, 1)
            for p in range(2):
                dve.wait_ge(r_done, 2 * p + 1)
                tt(q_rope[:, p, :], wide(2 * p), cos[:], ALU.mult)
                dve.wait_ge(*((w_used, SLABS["uq_rope"][0] + 1) if p else (r_done, 2)))
                step(tt(turned[:], wide(2 * p + 1), sin[:], ALU.mult))
                tt(q_rope[:, p, :], q_rope[:, p, :], turned[:], ALU.add).then_inc(r_free, 1)
                dve.wait_ge(r_free, p + 1)
            for j in range(1, NT, 2):
                dve.wait_ge(v_done, j + 1)
                nc.vector.tensor_copy(v_value[:, j, :], ps[:, j, :]).then_inc(v_dve, 1)
            for e in range(2 * MLA_HEADS):
                hd, is_q = e % MLA_HEADS, e >= MLA_HEADS
                dve.wait_ge(g_rs, e + 1)
                if e >= 2:
                    dve.wait_ge(g_stored[e % 2], 32 * (e // 2))
                which = "mla_q" if is_q else "mla_k"
                stt(g_nope[e % 2][:], wide(e % 2), col(which + "_nope"), g_rms[e % 2][:], ALU.mult,
                    ALU.mult).then_inc(g_free, 1)
                r0 = ROPE * (hd % 2) if is_q else 0
                rope = q_rope[r0:r0 + ROPE, hd // 2, :] if is_q else k_rope[0:ROPE, :]
                stt(g_rope[e % 2][r0:r0 + ROPE, :], rope, col(which + "_rope")[r0:r0 + ROPE, :],
                    g_rms[e % 2][r0:r0 + ROPE, :], ALU.mult, ALU.mult).then_inc(g_roped, 1)
            def maxima(unit):
                g, q, d = unit // 4 % 2, unit % 4, unit - NT * MLA_HEADS
                if d < 0:
                    dve.wait_ge(a_qk, unit + 1)
                    step(nc.vector.tensor_reduce(mstat[:, g, 0, q:q + 1], wide(unit % 2), AX.X, ALU.max))
                    ts(mstat[:, g, 1, q:q + 1], mstat[:, g, 0, q:q + 1], -(P + ROPE) ** -0.5, None, ALU.mult).then_inc(a_max, 1)
                    return
                i, bias = unit % NT, e_bias[:, d // NT % 2, :]
                if i == 0:
                    dve.wait_ge(bias_2_in[d // NT % 2], 16 * (d // NT // 2) + 16)
                near0, near1 = max(0, i - 1) * P, min(NT, i + 2) * P
                b0 = P if i == 0 else 0
                stats = e_stat[:, unit % 8]
                dve.wait_ge(a_tr, 2 * (unit - unit % 4) - 8)
                if d >= 2:
                    dve.wait_ge(a_probs, d - 1)
                for m, row in enumerate((prob_rows[g][q], second[unit % 2])):
                    dve.wait_ge(a_qk, NT * MLA_HEADS + 2 * d + m + 1)
                    for kind, lo, hi, b in ((0, 0, near0, bias[:, 0:1].broadcast_to([P, near0])),
                                            (2, near1, S, bias[:, 3 * P - 1:3 * P].broadcast_to([P, S - near1])),
                                            (1, near0, near1, bias[:, b0:b0 + near1 - near0])):
                        if lo < hi:
                            ins = nc.vector.tensor_tensor_reduce(row[:, lo:hi], wide(m)[:, lo:hi], b, 1.0, TAKEN,
                                                                 ALU.add, ALU.max, stats[:, kind, m:m + 1])
                    ins.then_inc(e_red, 1)
                dve.wait_ge(e_red, 2 * d + 2)
                for kind, there in ((0, near0 > 0), (2, near1 < S)):
                    if there:
                        step(tt(stats[:, 1, :], stats[:, 1, :], stats[:, kind, :], ALU.max))
                ts(stats[:, 3, :], stats[:, 1, :], -1.0, None, ALU.mult).then_inc(a_max, 1)

            def difference(unit):
                g, q, d = unit // 4 % 2, unit % 4, unit - NT * MLA_HEADS
                row, other = prob_rows[g][q], second[unit % 2]
                sums, factor = e_stat[:, unit % 8, 4, :], e_stat[:, unit % 8, 5, :]
                dve.wait_ge(a_exp, NT * MLA_HEADS + 2 * d + 2)
                step(nc.vector.reciprocal(factor[:, 0:1], sums[:, 1:2]))
                step(stt(factor[:, 1:2], factor[:, 0:1], minus_lam, sums[:, 0:1], ALU.mult, ALU.mult))
                stt(row[:], other[:], factor[:, 1:2], row[:], ALU.mult, ALU.add).then_inc(a_probs, 1)

            def inverse_sums(group):
                g, first = group % 2, 4 * group
                if group < 2 * MLA_HEADS:
                    dve.wait_ge(a_exp, first + 4)
                    sums = mstat[:, g, 2, :]
                else:
                    sums = e_stat[:, 4 * g:4 * g + 4, 4, 0]
                step(nc.vector.reciprocal(mstat[:, g, 3, :], sums))
                for q in range(4):
                    ins = ts(diagonal[:, q, :], ident[:], mstat[:, g, 3, q:q + 1], None, ALU.mult)
                ins.then_inc(a_diag, 1)

            def head_out(group):
                dve.wait_ge(a_spread, group + 1)
                dve.wait_ge(a_copied, group + 1)
                tt(o_stage[:], o_stage[:], ps[:, 7 - group % 2, :], ALU.mult).then_inc(a_out, 1)

            def rest_probs(group, j):
                dve.wait_ge(a_pthi, 8 * group + j + 1)
                tt(pt[j % 2][1][:], ps[:, 4 + j % 2, :], pt[j % 2][0][:].bitcast(F32), ALU.subtract).then_inc(a_ptlo, 1)

            first_diff = NT * MLA_HEADS
            for e in range(2):
                dve.wait_ge(g_stored[e], 32 * MLA_HEADS)
            for q in range(4):
                maxima(q)
            for group in range(GROUPS):
                for n in range(4):
                    unit = 4 * (group + 1) + n
                    late = first_diff < unit <= 4 * GROUPS
                    if group + 1 < GROUPS:
                        maxima(unit)
                    if late and n == 0:
                        difference(unit - 1)
                    if n == 0 and group:
                        head_out(group - 1)
                    rest_probs(group, 2 * n)
                    rest_probs(group, 2 * n + 1)
                    if late and n:
                        difference(unit - 1)
                    if n == 1:
                        inverse_sums(group)
            head_out(GROUPS - 1)
            def out_scaled(n):
                k = MLA_HEADS + n
                dve.wait_ge(s_rs, n + 1)
                stt(o_in[:, k, :], o_in[:, k, :], col("diff_out"), o_rms[n % 2][:], ALU.mult, ALU.mult).then_inc(s_scaled, 1)

            def out_lo(k):
                dve.wait_ge(s_hi, k + 1)
                tt(o_all[1][:, k, :], o_in[:, k, :], o_all[0][:, k, :].bitcast(F32), ALU.subtract).then_inc(s_lo, 1)

            for k in range(MLA_HEADS):
                out_lo(k)
            out_scaled(0)
            for n in range(1, DIFF_HEADS):
                out_scaled(n)
                out_lo(MLA_HEADS + n - 1)
            out_lo(KT - 1)
            for k in range(KT):
                dve.wait_ge(w_used, SLABS["out_2"][0] + k + 1)
                tt(x[:, k, :], x[:, k, :], wide(k % 2), ALU.add).then_inc(x_added, 1)
            scaled(9, "mlp_2", x, normed)
            dve.sem_inc(u_lo, 2)
            dve.sem_inc(u_added, 8)
            s0 = SLABS["mlp_2"][0]
            down0 = 4 + 4 + 4 * (FF_TILES // CHUNK) + 6
            with dve.Fori(0, FF2_TILES // CHUNK) as c:
                for j in range(CHUNK):
                    part = tmp[j % 2]
                    dve.wait_ge(u_relu, 4 * c + j + 1)
                    tt(part[:], part[:], part[:], ALU.mult).then_inc(u_sq, 1)
                    dve.wait_ge(u_hi, 4 * c + j + 1)
                    tt(hidden[1][:, j, :], part[:], hidden[0][:, j, :].bitcast(F32), ALU.subtract).then_inc(u_lo, 1)
                for m in range(KT):
                    if m % 2:
                        dve.wait_ge(w_used, 8 * c + s0 + 4 + m // 2 + 1)
                    else:
                        dve.wait_ge(first_half, 4 * c + down0 + m // 2 + 1)
                    tt(x[:, m, :], x[:, m, :], wide(m % 4), ALU.add).then_inc(u_added, 1)


def slabs_of(w, kt):
    n = w.shape[1] // P
    w = w.reshape(kt, P, n, P).transpose(2, 0, 1, 3).reshape(n * kt // 8, 8, P, P)
    return w.transpose(0, 2, 1, 3).reshape(-1, P, 1024)


def moving_slabs(w):
    return w.reshape(4, 2, P, 512).transpose(0, 2, 1, 3).reshape(4, P, 1024)


def pack_weights(a):
    out = np.zeros((N_SLABS, P, 1024), np.float32)

    def put(name, slabs):
        first, n = SLABS[name]
        assert slabs.shape[0] == n, (name, slabs.shape)
        out[first:first + n] = slabs

    w = a["w_in"]
    pool_w, q_w, k_w, v_w, qi_w, ki_w, wi_w, gp_w, ga_w = np.split(
        w, np.cumsum((512, 1024, 128, 128, 256, 64, 4, 1024)), axis=1)
    put("mix_in", slabs_of(np.concatenate([pool_w, ki_w, ki_w, qi_w, k_w], axis=1), KT))
    vw = np.concatenate([v_w, wi_w], axis=1).reshape(2, 4, P, VW).transpose(0, 2, 1, 3).reshape(2, P, 4 * VW)
    first = SLABS["value_pool"][0]
    out[first:first + 2, :, 0:4 * VW] = vw
    for g in range(POOL_GROUPS):
        b = 4 * VW + g % 3 * P
        out[first + g // 3, :, b:b + P] = a["pool_w"][g]
    put("proj_pool", slabs_of(a["w_proj_pool"], 4))
    put("gate_pool", slabs_of(gp_w, KT))
    put("gate_attn", slabs_of(ga_w, KT))
    put("query", slabs_of(q_w, KT))
    put("proj_attn", slabs_of(a["w_proj_attn"], KT))
    put("mix_out", slabs_of(a["w_out"], KT))
    w = a["w_kv_mem"]
    put("mem_key", slabs_of(w[:, :MEM_HEADS * P], KT))
    put("mem_value", moving_slabs(w[:, MEM_HEADS * P:]))
    put("mem_query", slabs_of(a["w_q_mem"], KT))
    put("mem_out", slabs_of(a["w_o_mem"], 4))
    gate, up = slabs_of(a["w_gate_up"][:, :FF], KT), slabs_of(a["w_gate_up"][:, FF:], KT)
    parts = []
    for c in range(0, FF_TILES, CHUNK):
        n = min(CHUNK, FF_TILES - c)
        parts.append(np.stack([gate[c:c + n], up[c:c + n]], axis=1).reshape(2 * n, P, 1024))
        parts.append(slabs_of(a["w_down"][c * P:(c + n) * P], n))
    put("ffn", np.concatenate(parts))
    w = a["w_in_2"][0]
    cq, ckv, kr, dq, dk, dv = np.split(w, np.cumsum((256, 128, 64, 512, 512)), axis=1)
    kr2 = np.roll(kr, 32, axis=1)
    put("in_2", slabs_of(np.concatenate([cq, ckv, kr, kr, kr2, kr2, dq, dk], axis=1), KT))
    put("diff_value", moving_slabs(dv))
    w = a["w_ukv_2"][0].reshape(P, MLA_HEADS, 2, P)
    put("ukv", np.concatenate([w[:, :, 0].reshape(P, 512), w[:, :, 1].reshape(P, 512)], axis=1)[None])
    w = a["w_uq_2"][0].reshape(2 * P, MLA_HEADS, P + ROPE)
    rope = w[:, :, P:]
    turned = np.roll(rope, 32, axis=2)
    order = [v[:, 2 * p:2 * p + 2].reshape(2 * P, P) for p in range(2) for v in (rope, turned)]
    put("uq_rope", slabs_of(np.concatenate(order, axis=1), 2))
    put("uq_nope", slabs_of(w[:, :, :P].reshape(2 * P, 512), 2))
    put("out_2", slabs_of(a["w_out_2"][0], KT))
    up = slabs_of(a["w_up_2"][0], KT)
    parts = []
    for c in range(0, FF2_TILES, CHUNK):
        parts += [up[c:c + CHUNK], slabs_of(a["w_down_2"][0][c * P:(c + CHUNK) * P], CHUNK)]
    put("mlp_2", np.concatenate(parts))
    return out


def pack_cols(a):
    out = np.zeros((P, N_COLS), np.float32)

    def put(name, v):
        first, n = COLS[name]
        out[:, first:first + n] = v.reshape(n, P).T

    for name, key in (("mix_pre", "norm_mix_pre"), ("mix_post", "norm_mix_post"), ("pool_scale", "pool_scale"),
                      ("mem_pre", "norm_mem_pre"), ("mem_kv", "norm_mem_kv"), ("mem_post", "norm_mem_post"),
                      ("ffn_pre", "norm_ffn_pre"), ("ffn_post", "norm_ffn_post"), ("attn_2", "attn_norm_w_2"),
                      ("q_a", "q_a_norm_w_2"), ("kv_a", "kv_a_norm_w_2"), ("diff_out", "diff_out_norm_w_2"),
                      ("mlp_2", "mlp_norm_w_2")):
        put(name, a[key])
    for name, key in (("mla_q", "mla_q_norm_w_2"), ("mla_k", "mla_k_norm_w_2")):
        put(name + "_nope", a[key][0, :P])
        put(name + "_rope", np.tile(a[key][0, P:], 2))
    put("diff_q", np.tile(a["diff_q_norm_w_2"][0], 2))
    put("diff_k", np.tile(a["diff_k_norm_w_2"][0], 2))
    first = COLS["lambda"][0]
    for n, key in enumerate(("lambda_q1_2", "lambda_k1_2", "lambda_q2_2", "lambda_k2_2")):
        out[:, first + 64 * n:first + 64 * n + 64] = a[key]
    return out


def features_first(v):
    return np.ascontiguousarray(v.T.reshape(-1, P, v.shape[0]).transpose(1, 0, 2))


def bucket_causal(dist):
    n = np.maximum(dist, 0)
    large = 16 + (np.log(np.maximum(n, 1).astype(np.float32) / np.float32(16)) / np.float32(np.log(8.0))
                  * np.float32(16)).astype(np.int32)
    return np.where(n < 16, n, np.minimum(large, 31))


def bucket_both_ways(rel):
    n = np.abs(rel)
    large = 8 + (np.log(np.maximum(n, 1).astype(np.float32) / np.float32(8)) / np.float32(np.log(16.0))
                 * np.float32(8)).astype(np.int32)
    return np.where(rel > 0, 16, 0) + np.where(n < 8, n, np.minimum(large, 15))


def constants():
    c = {"c_ident": np.eye(P, dtype=np.float32)}
    c["c_flip"] = c["c_ident"][::-1].copy()
    c["c_tri"] = np.where(np.arange(P)[None, :] > np.arange(P)[:, None], np.float32(NEG), np.float32(0))
    fix = np.ones((POOL_GROUPS, 16), np.float32)
    for g in range(POOL_GROUPS):
        n = np.arange(1, 17)
        fix[g] = (2 << g) / np.minimum(n, 2 << g)
    c["c_pool_fix"] = np.broadcast_to(fix, (P, POOL_GROUPS, 16)).copy()
    dist = 255 - np.arange(384)
    c["c_onehot"] = (bucket_causal(dist)[None, :] == np.arange(BUCKETS)[:, None]).astype(np.float32)
    rel = np.arange(512) - 255
    c["c_onehot_2"] = (bucket_both_ways(rel)[None, :] == np.arange(BUCKETS)[:, None]).astype(np.float32)
    inv = (10000.0 ** (-np.arange(0, ROPE, 2) / ROPE)).astype(np.float32)
    ang = (np.arange(S, dtype=np.float32)[None, :] * inv[:, None]).astype(np.float64)
    c["c_cos"] = np.tile(np.cos(ang), (4, 1)).astype(np.float32)
    c["c_sin"] = np.concatenate([-np.sin(ang), np.sin(ang)] * 2).astype(np.float32)
    halves = np.zeros((P, 3, P), np.float32)
    halves[:64, 0, :64] = halves[64:, 0, 64:] = 1
    halves[:64, 1] = halves[64:, 2] = 1
    c["c_halves"] = halves
    return c


N_CONSTS = 8
SCRATCH = {"bias_rows": (HEADS, 384), "gates": (3 * KT, P, S), "bias_rows_2": (DIFF_HEADS, 512),
           "bias_tiles_2": (DIFF_HEADS, P, 3 * P),
           "diff_qk": (2 * DIFF_HEADS, P, S), "diff_v": (DIFF_HEADS, P, NT, P),
           "mla_nope": (2 * MLA_HEADS, P, S), "mla_rope": (2 * MLA_HEADS, ROPE, S), "mla_v": (MLA_HEADS, P, NT, P),
           "heads_out": (KT, P, S)}


def arrays_of(inputs):
    a = {k: np.asarray(v) for k, v in inputs.items()}
    out = {"weights": pack_weights(a), "cols": pack_cols(a), "x": features_first(a["x"][0]),
           "mem": features_first(a["mem"][0]), "rel_bias_table": a["rel_bias_table"],
           "rel_bias_2": a["rel_bias_2"]}
    return {**out, **constants()}


def kernel(**inputs):
    from concourse import bacc
    from concourse.bass_utils import run_bass_kernel_spmd

    nc = bacc.Bacc("TRN2", target_bir_lowering=False, num_devices=1)
    arrays = arrays_of(inputs)
    t = {name: nc.dram_tensor(f"{name}_dram", a.shape, mybir.dt.from_np(a.dtype), kind="ExternalInput").ap()
         for name, a in arrays.items()}
    t["out"] = nc.dram_tensor("out_dram", (P, KT, S), F32, kind="ExternalOutput").ap()
    for name, shape in SCRATCH.items():
        t[name] = nc.dram_tensor(f"{name}_scratch", shape, F32, kind="Internal").ap()
    program(nc, t)
    r = run_bass_kernel_spmd(nc, [{f"{name}_dram": a for name, a in arrays.items()}], core_ids=[0])
    got = r.results[0]["out_dram"]
    return np.ascontiguousarray(got.transpose(2, 1, 0).reshape(1, S, D))
```

```python
from contextlib import ExitStack

import numpy as np

import concourse.bass as bass
from concourse import mybir

F32 = mybir.dt.float32
F32R = mybir.dt.float32r
BF16 = mybir.dt.bfloat16
ACT = mybir.ActivationFunctionType
ALU = mybir.AluOpType
AX = mybir.AxisListType

P = 128
D = 1024
KT = D // P
S = 1024
NT = S // P
HALF = 512
EPS = 1e-6

POOL_GROUPS = 4
HEADS = 8
IDX_HEADS, IDX_DIM = 4, 64
TOPK = 256
ROUNDS = TOPK // 8
BY_POOL = 3
BUCKETS = 32
MAX_DISTANCE = 128
M = 256
MT = M // P
MEM_HEADS = 4
FF = 2816
FF_TILES = FF // P
FF2 = 4096
FF2_TILES = FF2 // P
CHUNK = 4
MLA_HEADS = 4
DIFF_HEADS = 4
ROPE = 64
LAM_INIT = 0.2
NEG = -1e30
TAKEN = -3e38

SPLITS = 5 + 5, 5 + 4

GROUPS = (MLA_HEADS + DIFF_HEADS) * NT // 4

COLS = {}
for _name, _n in (
    ("mix_pre", 8), ("mix_post", 8), ("pool_scale", 4), ("mem_pre", 8), ("mem_kv", 8), ("mem_post", 8),
    ("ffn_pre", 8), ("ffn_post", 8), ("attn_2", 8), ("q_a", 2), ("kv_a", 1), ("mla_q_nope", 1),
    ("mla_q_rope", 1), ("mla_k_nope", 1), ("mla_k_rope", 1), ("diff_q", 1), ("diff_k", 1),
    ("diff_out", 1), ("mlp_2", 8), ("lambda", 256),
):
    COLS[_name] = (sum(n for _, n in COLS.values()), _n)
N_COLS = sum(n for _, n in COLS.values())

PRE_ORDER = ("mix_pre", "mem_pre", "ffn_pre", "attn_2", "q_a", "kv_a", "mlp_2")
PRE = {}
for _name in PRE_ORDER:
    PRE[_name] = (COLS[_name][1], sum(n for n, _ in PRE.values()))

SLABS = {}
for _name, _n in (
    ("mix_in", 9),
    ("gates", 14), ("pool_mix", 1), ("last_gates", 2), ("proj_pool", 4), ("query", 8), ("proj_attn", 8), ("mix_out", 8),
    ("mem_key", 4), ("mem_value", 4), ("mem_query", 4), ("mem_out", 4),
    ("ffn", 2 * FF_TILES + FF_TILES),
    ("in_2", 13), ("diff_value", 4), ("uq_rope", 1), ("ukv", 1), ("uq_nope", 1), ("out_2", 8), ("mlp_2", 64),
):
    SLABS[_name] = (sum(n for _, n in SLABS.values()), _n)
N_SLABS = sum(n for _, n in SLABS.values())
SPLIT_BY_TWO = (8, 26)

POOL_ORDER = (3, 0, 1, 2)
WINDOW_STEPS = [(g, e) for g in range(POOL_GROUPS) for e in range(g + 4)]


class Chain:

    def __init__(self, engine, sem):
        self.engine, self.sem, self.n = engine, sem, 0

    def __call__(self, instruction):
        self.n += 1
        instruction.then_inc(self.sem, 1)
        self.engine.wait_ge(self.sem, self.n)


def program(nc, t):
    out = t["out"]
    with ExitStack() as ctx:
        def sem(name):
            return ctx.enter_context(nc.semaphore(name))

        KB = 1024
        base = -(-nc.sbuf_base // 64) * 64
        RAW, SPLIT = base, base + 8 * KB
        XR = SPLIT + 16 * KB
        AR = XR + 32 * KB
        BR = AR + 64 * KB
        ER = BR + 64 * KB
        place = [ER]

        def at(name, offset, shape, dt=F32):
            return nc.alloc_sbuf_tensor_at(name, shape, dt, offset=offset)

        def small(name, shape, dt=F32):
            size = int(np.prod(shape[1:])) * (2 if dt == BF16 else 4)
            here = place[0]
            place[0] += -(-size // 32) * 32
            return at(name, here, shape, dt)

        raw = [at(f"w_raw{i}", RAW + 4 * KB * i, [P, 1024]) for i in range(2)]
        w_hi = [at(f"w_hi{i}", SPLIT + 8 * KB * i, [P, 1024], F32R) for i in range(2)]
        w_lo = [at(f"w_lo{i}", SPLIT + 8 * KB * i + 4 * KB, [P, 1024], F32R) for i in range(2)]

        acc_at = place[0]
        acc = small("acc", [P, S])
        tmp_at = place[0]
        tmp = [small(f"tmp{i}", [P, S]) for i in range(2)]
        cols = small("cols", [P, N_COLS])
        ident = small("ident", [P, P])
        ident16 = small("ident16", [P, P], BF16)
        tri = small("tri", [P, P])
        ones = small("ones", [P, P])
        zero = small("zero", [P, 1])
        eps = small("eps", [P, 1])
        pool_fix = small("pool_fix", [P, POOL_GROUPS, 16])
        stat = small("stat", [P, 64])
        top8 = small("top8", [P, 2, 8])
        mstat = small("mstat", [P, 2, 4, 4])
        late_at = place[0]
        place[0] += 8 * KB
        lam_ab, minus_lam = stat[:, 0:2], stat[:, 2:3]
        assert place[0] <= nc.sbuf_usable_end, place[0] - nc.sbuf_usable_end

        def col(name, k=0):
            return cols[:, COLS[name][0] + k:COLS[name][0] + k + 1]

        def pair(name, offset, shape):
            size = int(np.prod(shape[1:])) * 4
            return at(name + "_hi", offset, shape, F32R), at(name + "_lo", offset + size, shape, F32R)

        x_in = at("x_in", XR, [P, KT, S])
        h1 = pair("h1", AR, [P, KT, S])
        u = at("u", XR + 16 * KB, [P, POOL_GROUPS, S])
        win = [at(f"win{i}", XR + 8 * KB + 4 * KB * i, [P, S]) for i in range(2)]
        pooled = [pair(f"pooled{g}", o, [P, S]) for g, o in enumerate((XR, BR + 40 * KB, BR + 48 * KB, XR + 16 * KB))]
        u_plain = [at(f"u_plain{g}", o, [P, S]) for g, o in enumerate((XR, BR + 40 * KB, BR + 48 * KB, acc_at))]
        kidx_t = at("kidx_t", acc_at, [P, S])
        value_t = at("value_t", late_at, [P, S])
        wi_t = at("wi_t", late_at + 4 * KB, [P, S])
        wi = stat[:, 0:NT * IDX_HEADS].rearrange("p (j h) -> p j h", j=NT)
        mixed = pair("mixed", XR, [P, POOL_GROUPS, S])
        mixed_sum = at("mixed_sum", XR + 16 * KB, [P, POOL_GROUPS, S])
        qidx = pair("qidx", BR + 32 * KB, [P, 2, S])
        kidx = pair("kidx", BR + 48 * KB, [P, S])
        key = pair("key", BR + 56 * KB, [P, S])
        score_at = {i: sum(j + 1 for j in range(2, i)) * P for i in range(2, NT)}
        score = at("score", BR, [P, sum(j + 1 for j in range(2, NT)) * P])
        mask_at = {i: sum(j + 1 for j in range(i)) * P for i in range(NT)}
        mask = at("mask", BR + 16896, [P, sum(range(1, NT + 1)) * P], BF16)
        query = at("query", XR, [P, HEADS, S])
        value = at("value", BR + 32 * KB, [P, NT, P])
        mix_rows = [[at(f"mix_rows0_{q}", BR + 4 * KB * q, [P, S]) for q in range(4)],
                    [at(f"mix_rows1_{q}", o, [P, S]) for q, o in enumerate((late_at, late_at + 4 * KB, BR + 26 * KB, acc_at))]]
        probs_t = [at(f"probs_t{i}", BR + 40 * KB + 2 * KB * i, [P, HALF]) for i in range(2)]
        q_tile = [pair(f"q_tile{i}", tmp_at + 4 * KB * i, [P, 4, P]) for i in range(2)]
        bias = at("bias", BR + 48 * KB, [P, HEADS, 2 * P])
        bias_2 = at("bias_2", BR + 40 * KB, [P, DIFF_HEADS, 3 * P])
        flip = at("flip", BR + 46 * KB, [P, P])
        frow = at("frow", BR + 56 * KB, [HEADS, 384])
        onehot = at("onehot", BR + 58 * KB, [BUCKETS, 384])
        table = at("table", BR + 60 * KB, [BUCKETS, HEADS])
        table_2 = at("table_2", BR + 60 * KB + 512, [BUCKETS, DIFF_HEADS])
        onehot_2 = at("onehot_2", BR + 61 * KB, [BUCKETS, HALF])
        frow_2 = at("frow_2", late_at + 6 * KB, [DIFF_HEADS, HALF])
        att = pair("att", AR, [P, HEADS, S])
        gated = [at(f"gated{i}", XR + 12 * KB * i, [P, 3, S]) for i in range(2)]
        merged = pair("merged", BR, [P, KT, S])
        y = at("y", AR, [P, KT, S])
        x = at("x", XR, [P, KT, S])

        mem_in = at("mem_in", AR + 32 * KB, [P, KT, M])
        memn = pair("memn", AR + 40 * KB, [P, KT, M])
        mem_sq = at("mem_sq", AR + 48 * KB, [P, KT, M])
        mem_rms = at("mem_rms", AR + 56 * KB, [P, M])
        kmem = pair("kmem", AR + 32 * KB, [P, MEM_HEADS, M])
        vmem = at("vmem", late_at, [P, MT, HALF])
        normed = pair("normed", BR, [P, KT, S])
        qm = pair("qm", AR, [P, MEM_HEADS, S])
        om = pair("om", BR, [P, MEM_HEADS, S])
        mprobs = at("mprobs", BR + 32 * KB, [P, 2, 4, M])
        mpt = [at(f"mpt{j}", BR + 40 * KB + 4 * KB * j, [P, HALF]) for j in range(MT)]
        hidden = pair("hidden", AR + 32 * KB, [P, CHUNK, S])
        c_q = at("c_q", AR, [P, 2, S])
        cq = pair("cq", AR + 8 * KB, [P, 2, S])
        c_kv = at("c_kv", AR + 24 * KB, [P, 1, S])
        ckv = pair("ckv", AR + 28 * KB, [P, 1, S])
        k_rope = at("k_rope", AR + 36 * KB, [P, S])
        q_rope = at("q_rope", AR + 40 * KB, [P, 2, S])
        q_rope_sq = at("q_rope_sq", AR + 48 * KB, [P, 2, S])
        k_rope_sq = at("k_rope_sq", AR + 56 * KB, [P, S])
        halves = at("halves", AR + 60 * KB, [P, 3, P])
        cos, sin = at("cos", late_at, [P, S]), at("sin", late_at + 4 * KB, [P, S])
        d_rms = [at(f"d_rms{i}", AR + 48 * KB + 4 * KB * i, [P, S]) for i in range(2)]
        d_out = [at(f"d_out{i}", AR + 4 * KB * i, [P, S]) for i in range(2)]
        d_value = at("d_value", BR, [P, NT, HALF])
        v_value = at("v_value", BR + 16 * KB, [P, NT, HALF])
        g_rms = [at(f"g_rms{i}", AR + 4 * KB * i, [P, S]) for i in range(2)]
        g_nope = [at(f"g_nope{i}", BR + 56 * KB + 4 * KB * i, [P, S]) for i in range(2)]
        g_rope = [at(f"g_rope{i}", late_at + 4 * KB * i, [P, S]) for i in range(2)]
        turned = at("turned", acc_at, [P, S])
        head_raw = [at(f"head_raw{i}", BR + 36 * KB + 4 * KB * i, [P, S]) for i in range(5)]
        head_parts = [[at(f"head_part{e}_{i}", (BR, AR)[e] + 4 * KB * i, [P, S], F32R) for i in range(9)]
                      for e in range(2)]
        v_plain = [at(f"v_plain{e}", (BR, AR)[e] + 16 * KB, [P, S]) for e in range(2)]
        pt_plain = [at(f"pt_plain{i}", AR + 36 * KB + 4 * KB * i, [P, HALF]) for i in range(2)]
        pt = [pair(f"pt{i}", AR + 36 * KB + 4 * KB * i, [P, HALF]) for i in range(2)]
        rows_at = [AR + 44 * KB + 4 * KB * i for i in range(5)] + [BR + 56 * KB, BR + 60 * KB, acc_at]
        prob_rows = [[at(f"rows{g}_{q}", rows_at[4 * g + q], [P, S]) for q in range(4)] for g in range(2)]
        second = [at(f"second{i}", tmp_at + 4 * KB * i, [P, S]) for i in range(2)]
        o_stage = at("o_stage", late_at, [P, HALF])
        diagonal = at("diagonal", late_at + 2 * KB, [P, 4, P])
        e_bias = at("e_bias", late_at + 4 * KB, [P, 2, 3 * P])
        e_stat = at("e_stat", late_at + 7 * KB, [P, 8, 6, 2])
        o_in = at("o_in", BR, [P, KT, S])
        o_rms = [at(f"o_rms{i}", BR + 40 * KB + 4 * KB * i, [P, S]) for i in range(2)]
        o_all = pair("o_all", AR, [P, KT, S])
        ps = ctx.enter_context(nc.psum_tensor("ps", [P, 8, HALF], F32))

        def wide(slot):
            return ps[:, 2 * slot:2 * slot + 2, :].rearrange("p b n -> p (b n)")

        def mix_stat(unit, kind):
            c = 6 * (unit % 8) + kind
            return stat[:, c:c + 1]

        def tiles_before(group):
            return sum(g // 2 + 1 for g in range(group))

        def tiles_of(group, n):
            tiles = group // 2 + 1
            return range(-(-n * tiles // 4), -(-(n + 1) * tiles // 4))

        def splits_before(hd):
            return SPLITS[0] * min(hd, MLA_HEADS) + SPLITS[1] * max(0, hd - MLA_HEADS)

        raw_landed = [sem(f"raw_landed{i}") for i in range(2)]
        w_rounded = sem("w_rounded")
        w_split = sem("w_split")
        w_used = sem("w_used")
        first_half = sem("first_half")
        consts_in = sem("consts_in")
        x_in_landed = [sem(f"x_in_landed{i}") for i in range(4)]
        dve_consts = sem("dve_consts")
        dve_step = sem("dve_step")
        n_sq, n_added = sem("norm_squared"), sem("norm_added")
        n_post_sq, n_acc = sem("norm_post_squared"), sem("norm_post_added")
        n_sum, n_rs = sem("norm_total"), sem("norm_inverse")
        act_step = sem("act_step")
        n_tmp, n_hi, n_lo = (sem("norm_" + n) for n in ("scaled", "hi", "lo"))
        in_hi, in_free = sem("in_hi"), sem("in_free")
        turn_ready, turn_done = sem("turn_ready"), sem("turn_done")
        last_ready = sem("last_ready")
        kidx_doubled, mix_hi, pool_step = sem("kidx_doubled"), sem("mix_hi"), sem("pool_step")
        pooled_ready = sem("pooled_ready")
        pool_done, mix_free = sem("pool_done"), sem("mix_free")
        idx_done, idx_relu, idx_added = sem("idx_done"), sem("idx_relu"), sem("idx_added")
        gate_free = sem("gate_free")
        staged = [sem(f"staged{i}") for i in range(2)]
        frow_done, frow_out = sem("frow_done"), sem("frow_out")
        shifted_in, flipped, bias_done = sem("shifted_in"), sem("flipped"), sem("bias_done")
        value_out = sem("value_out")
        masks_ready = sem("masks_ready")
        qt_hi, qt_lo, inv_ready = sem("qt_hi"), sem("qt_lo"), sem("inv_ready")
        qk_done, logits_ready, nmax_ready, exp_done, probs_ready = (
            sem(n) for n in ("qk_done", "logits_ready", "nmax_ready", "exp_done", "probs_ready"))
        tr_done, pt_out, pv_done, o_hi, o_lo = (
            sem(n) for n in ("tr_done", "pt_out", "pv_done", "o_hi", "o_lo"))
        gates_in = [sem(f"gates_in{i}") for i in range(2)]
        merge_free = sem("merge_free")
        x_landed = sem("x_landed")
        y_free, x_added = sem("y_free"), sem("x_added")
        mem_landed = sem("mem_landed")
        mem_squared, mem_total, mem_rs, mem_scaled, mem_hi, mem_lo = (
            sem("mem_" + n) for n in ("squared", "total", "inverse", "scaled", "hi", "lo"))
        mkv_hi, mkv_lo, mq_hi, mq_lo = (sem(n) for n in ("mem_kv_hi", "mem_kv_lo", "mem_q_hi", "mem_q_lo"))
        m_qk, m_max, m_exp, m_probs, m_tr, m_copied, m_pv, m_ohi, m_olo = (
            sem("mem_" + n) for n in ("logits", "max", "exp", "probs", "transposed", "probs_copied",
                                      "weighed", "out_hi", "out_lo"))
        f_silu, f_mul, f_hi, f_lo, f_added, y_zero = (
            sem("ffn_" + n) for n in ("silu", "hidden", "hidden_hi", "hidden_lo", "added", "y_zeroed"))
        tables_in, bias_2_out = sem("tables_in"), sem("bias_2_out")
        c_free, d_free = sem("c_free"), sem("d_free")
        d_sq, d_tot, d_ln, d_rs = (sem("diff_norm_" + n) for n in ("squared", "total", "log", "inverse"))
        d_stored = [sem(f"diff_stored{i}") for i in range(2)]
        dv_act, dv_dve, v_done, v_act, v_dve = (
            sem(n) for n in ("dv_out_act", "dv_out_dve", "v_done", "v_out_act", "v_out_dve"))
        dv_stored, v_stored = sem("dv_stored"), sem("v_stored")
        rope_sq = sem("rope_squared")
        g_done, g_sq, g_tot, g_rs, g_free, g_roped = (
            sem("mla_" + n) for n in ("tile", "squared", "total", "inverse", "nope_out", "rope_out"))
        r_done, r_free = sem("rope_done"), sem("rope_free")
        g_stored = [sem(f"mla_stored{i}") for i in range(2)]
        lam_sum, lam_exp = sem("lam_sum"), sem("lam_exp")
        heads_in, bias_2_in, head_split = sem("heads_in"), [sem(f"bias_2_in{i}") for i in range(2)], sem("head_split")
        a_qk, a_max, a_exp, a_probs, a_tr, a_pthi, a_ptlo, a_pv, a_out, e_red, a_inv, a_diag, a_spread, a_copied = (
            sem("attn_" + n) for n in ("logits", "max", "exp", "probs", "transposed", "probs_t_hi", "probs_t_lo",
                                       "weighed", "out", "biased", "inverse", "diagonal", "spread", "copied"))
        o_stored, o_landed, o_last = sem("o_stored"), sem("o_landed"), sem("o_last")
        s_sq, s_tot, s_rs, s_scaled, s_hi, s_lo = (
            sem("heads_" + n) for n in ("squared", "total", "inverse", "scaled", "hi", "lo"))
        u_relu, u_sq, u_hi, u_lo, u_added = (sem("mlp_" + n) for n in ("relu", "squared", "hi", "lo", "added"))
        stored = sem("stored")

        block = ctx.enter_context(nc.Block())

        @block.sync
        def _(sp):
            for s in range(2):
                sp.dma_start(raw[s][:], t["weights"][s]).then_inc(raw_landed[s], 16)
            def load_slabs(first, end):
                with sp.Fori(first // 2, end // 2) as pr:
                    for s in range(2):
                        sp.wait_ge(w_split, 2 * pr + s - 1)
                        sp.dma_start(raw[s][:], t["weights"][2 * pr + s]).then_inc(raw_landed[s], 16)

            load_slabs(2, SLABS["out_2"][0] + 2)
            sp.wait_ge(v_stored, 16 * MLA_HEADS)
            sp.wait_ge(dv_stored, 16 * DIFF_HEADS)
            for hd in range(2 * MLA_HEADS):
                if hd < MLA_HEADS:
                    for e in range(2):
                        sp.wait_ge(g_stored[e], 32 * hd + 32)
                if hd == MLA_HEADS:
                    sp.wait_ge(bias_2_out, 16)
                    for e in range(2):
                        sp.wait_ge(d_stored[e], 16 * DIFF_HEADS)
                d = hd - MLA_HEADS
                if d < 0:
                    srcs = ((t["mla_nope"][hd],), (t["mla_nope"][hd + MLA_HEADS],), (t["mla_v"][hd].rearrange("p j n -> p (j n)"),),
                            (t["mla_rope"][hd],) * 2, (t["mla_rope"][hd + MLA_HEADS],) * 2)
                else:
                    q, k = t["diff_qk"][d], t["diff_qk"][d + DIFF_HEADS]
                    srcs = ((q[0:64],) * 2, (q[64:P],) * 2, (t["diff_v"][d].rearrange("p j n -> p (j n)"),),
                            (k[0:64],) * 2, (k[64:P],) * 2)
                for i, n in enumerate((0, 1, 3, 4, 2)):
                    src = srcs[n]
                    if hd:
                        sp.wait_ge(head_split, splits_before(hd - 1) + 5 + i if n != 2 else splits_before(hd))
                    for e, part in enumerate(src):
                        rows_of = slice(0, P) if len(src) == 1 else slice(64 * e, 64 * e + 64)
                        sp.dma_start(head_raw[n][rows_of, :], part).then_inc(heads_in, 16)
                if d >= 2:
                    sp.wait_ge(e_red, 16 * (d - 1))
                if d >= 0:
                    sp.dma_start(e_bias[:, d % 2, :], t["bias_tiles_2"][d]).then_inc(bias_2_in[d % 2], 16)
            load_slabs(SLABS["out_2"][0] + 2, N_SLABS)

        @block.gpsimd
        def _(pool):
            step = Chain(pool, pool_step)
            step(nc.gpsimd.memset(zero[:], 0.0))

            def split(s, n):
                nc.gpsimd.tensor_tensor(w_hi[s][:], raw[s][:], zero[:, 0:1].broadcast_to([P, 1024]),
                                        ALU.add).then_inc(w_rounded, 1)
                pool.wait_ge(w_rounded, n)
                nc.gpsimd.tensor_tensor(w_lo[s][:], raw[s][:], w_hi[s][:].bitcast(F32),
                                        ALU.subtract).then_inc(w_split, 1)

            for s in range(2):
                pool.wait_ge(raw_landed[s], 16)
                split(s, s + 1)
            def split_slabs(first, end):
                with pool.Fori(first // 2, end // 2) as pr:
                    for s in range(2):
                        pool.wait_ge(w_used, 2 * pr + s - 1)
                        pool.wait_ge(raw_landed[s], 16 * pr + 16)
                        split(s, 2 * pr + s + 1)

            split_slabs(2, SPLIT_BY_TWO[0])
            tt = nc.gpsimd.tensor_tensor

            def window_step(g, e):
                summed, less = win[g % 2], win[(g + 1) % 2]
                if e <= g:
                    cur, nxt, n = win[(e + 1) % 2][:] if e else u_plain[g][:], win[e % 2], 1 << e
                    if e == 0:
                        pool.wait_ge(gate_free, g + 1)
                        if g:
                            pool.wait_ge(pooled_ready, g)
                    step(tt(nxt[:, 0:n], cur[:, 0:n], zero[:, 0:1].broadcast_to([P, n]), ALU.add))
                    step(tt(nxt[:, n:S], cur[:, n:S], cur[:, 0:S - n], ALU.add))
                    if e == g:
                        step(tt(nxt[:, 0:16], nxt[:, 0:16], pool_fix[:, g, :], ALU.mult))
                elif e == g + 1:
                    step(tt(less[:], summed[:], u[:, g, :], ALU.subtract))
                elif e == g + 2:
                    step(tt(pooled[g][0][:], less[:], zero[:, 0:1].broadcast_to([P, S]), ALU.add))
                else:
                    tt(pooled[g][1][:], less[:], pooled[g][0][:].bitcast(F32), ALU.subtract).then_inc(pooled_ready, 1)

            done = 0
            for n in range(*SPLIT_BY_TWO):
                pool.wait_ge(w_rounded, n + 1)
                tt(w_lo[n % 2][:], raw[n % 2][:], w_hi[n % 2][:].bitcast(F32), ALU.subtract).then_inc(w_split, 1)
                more = 2 - n % 2
                for g, e in WINDOW_STEPS[done:done + more]:
                    window_step(g, e)
                done += more
            split_slabs(SPLIT_BY_TWO[1], SLABS["proj_attn"][0] + 2)
            for unit in range(HEADS * NT):
                group, q = unit // 4, unit % 4
                if q >= BY_POOL:
                    continue
                n = (group // 2 + 1) * P
                row = mix_rows[group % 2][q][:, 0:n]
                pool.wait_ge(inv_ready, unit + 1)
                nc.gpsimd.tensor_tensor(row, row, mix_stat(unit, 5).broadcast_to([P, n]), ALU.mult).then_inc(probs_ready, 1)
            split_slabs(SLABS["proj_attn"][0] + 2, SLABS["out_2"][0])
            landed = 0
            for hd in range(2 * MLA_HEADS):
                p = head_parts[hd % 2]
                top, bottom, both = slice(0, 64), slice(64, P), slice(0, P)
                if hd < MLA_HEADS:
                    landed += 16 * 7
                    hi = (p[0], p[2], p[4], p[6], p[7])
                    lo = ((0, p[1], both), (1, p[3], both), (3, p[6], bottom), (4, p[8], top))
                else:
                    landed += 16 * 9
                    hi = (p[0], p[1], v_plain[hd % 2], p[2], p[3])
                    lo = ((0, p[0], bottom), (1, p[1], top), (3, p[8], top), (4, p[8], bottom))
                pool.wait_ge(heads_in, landed)
                if hd == 1:
                    pool.wait_ge(g_roped, 2 * MLA_HEADS)
                if hd >= 2:
                    pool.wait_ge(a_qk, NT * (hd - 1) + NT * max(0, hd - 1 - MLA_HEADS))
                if hd:
                    pool.wait_ge(head_split, splits_before(hd))

                def whole(n):
                    nc.gpsimd.tensor_tensor(hi[n][:], head_raw[n][:], zero[:, 0:1].broadcast_to([P, S]),
                                            ALU.add).then_inc(head_split, 1)

                def rest(n, dst, lanes):
                    nc.gpsimd.tensor_tensor(dst[lanes, :], head_raw[n][lanes, :], hi[n][lanes, :].bitcast(F32),
                                            ALU.subtract).then_inc(head_split, 1)

                for n in (0, 1, 3, 4):
                    whole(n)
                for done, part in enumerate(lo):
                    pool.wait_ge(head_split, splits_before(hd) + 4 + done)
                    rest(*part)
                if hd >= 2:
                    pool.wait_ge(a_pv, 16 * (hd - 1))
                pool.wait_ge(head_split, splits_before(hd) + 8)
                whole(2)
                if hd < MLA_HEADS:
                    pool.wait_ge(head_split, splits_before(hd) + 9)
                    rest(2, p[5], both)
            pool.wait_ge(head_split, splits_before(MLA_HEADS + DIFF_HEADS))
            split_slabs(SLABS["out_2"][0], N_SLABS)

        @block.tensor
        def _(pe):
            def product(out, stationary, moving, start, stop):
                (sh, sl), (mh, ml) = stationary, moving
                nc.tensor.matmul(out, sh, mh, start=start, stop=False)
                nc.tensor.matmul(out, sh, ml, start=False, stop=False)
                return nc.tensor.matmul(out, sl, mh, start=False, stop=stop)

            def weight(s, b, width=P):
                return w_hi[s][:, b:b + width], w_lo[s][:, b:b + width]

            def tile(s, first, src, kt, slot, between=None, late=(None,)):
                out = wide(slot)
                for k in range(kt):
                    if k == late[0]:
                        pe.wait_ge(*late[1:])
                    for n in range(0, S, HALF):
                        last = product(out[:, n:n + HALF], weight(s, first + k * P),
                                       (src[0][:, k, n:n + HALF], src[1][:, k, n:n + HALF]), k == 0, k == kt - 1)
                    if between and k == 1:
                        between()
                return last

            def first_tiles(slabs, name, src):
                tiles, before = PRE[name]
                for s in range(2):
                    pe.wait_ge(w_split, SLABS[slabs][0] + s + 1)
                for k in range(tiles):
                    pe.wait_ge(n_lo, before + k + 1)
                    for s in range(2):
                        for n in range(0, S, HALF):
                            last = product(wide(s)[:, n:n + HALF], weight(s, k * P),
                                           (src[0][:, k, n:n + HALF], src[1][:, k, n:n + HALF]), k == 0, k == tiles - 1)
                        if k == tiles - 1:
                            last.then_inc(w_used, 1)

            def over_features(out, src, lhs, start=True, stop=True):
                for n in range(0, S, HALF):
                    last = nc.tensor.matmul(out[:, n:n + HALF], lhs, src[:, n:n + HALF], start=start, stop=stop)
                return last

            def total_added(post):
                pe.wait_ge(n_acc, 7 * (post + 1))
                over_features(wide(2), acc, ones[:]).then_inc(n_sum, 1)

            def total_tile(name, k):
                tiles, before = PRE[name]
                pe.wait_ge(n_sq, before + k + 1)
                over_features(wide(2), tmp[k % 2], ones[:], k == 0, k == tiles - 1).then_inc(
                    n_sum if k == tiles - 1 else n_added, 1)

            def total(name):
                for k in range(PRE[name][0]):
                    total_tile(name, k)

            pe.wait_ge(dve_consts, 1)
            total("mix_pre")
            pe.wait_ge(consts_in, 16 * N_CONSTS)
            pe.wait_ge(dve_consts, 2)
            nc.tensor.matmul(ps[0:HEADS, 6, 0:384], table[:, :], onehot[:, :], start=True, stop=True)
            nc.tensor.matmul(ps[0:DIFF_HEADS, 7, :], table_2[:, :], onehot_2[:, :], start=True, stop=True).then_inc(frow_done, 1)
            first_tiles("mix_in", "mix_pre", h1)

            def mix_in_tile(n):
                pe.wait_ge(w_split, n + 1)
                tile(n % 2, 0, h1, KT, n % 2).then_inc(w_used, 1)

            pe.wait_ge(turn_ready, 1)
            mix_in_tile(2)
            for j in range(NT):
                last = nc.tensor.transpose(ps[:, 4, 64 * j:64 * j + 64], wi_t[64:P, j * P:(j + 1) * P], ident[64:P, 64:P])
            last.then_inc(turn_done, 1)
            pe.wait_ge(in_free, 1)
            mix_in_tile(3)
            pe.wait_ge(in_free, 3)
            unit = 0
            for i in reversed(range(2, NT)):
                for hd in range(IDX_HEADS):
                    if unit >= 2:
                        pe.wait_ge(idx_relu, unit - 1)
                    lo, hi = IDX_DIM * (hd % 2), IDX_DIM * (hd % 2 + 1)
                    for n in range(0, (i + 1) * P, HALF):
                        m = min(HALF, (i + 1) * P - n)
                        last = product(wide(2 + unit % 2)[:, n:n + m],
                                       tuple(q[lo:hi, hd // 2, i * P:(i + 1) * P] for q in qidx),
                                       tuple(k[lo:hi, n:n + m] for k in kidx), True, True)
                    last.then_inc(idx_done, 1)
                    unit += 1
            mix_in_tile(4)
            pe.wait_ge(turn_ready, 2)
            pe.wait_ge(idx_relu, unit)
            for j in range(NT):
                last = nc.tensor.transpose(wide(2)[:, j * P:(j + 1) * P], value_t[:, j * P:(j + 1) * P], ident[:])
            last.then_inc(turn_done, 1)
            mix_in_tile(5)
            pe.wait_ge(in_free, 4)
            mix_in_tile(6)
            for n in (7, 8):
                pe.wait_ge(gate_free, n - 6)
                mix_in_tile(n)
            s0 = SLABS["gates"][0]
            with pe.Fori(0, 7) as it:
                for half in range(2):
                    s = (s0 + half) % 2
                    pe.wait_ge(w_split, 2 * it + s0 + half + 1)
                    pe.wait_ge(gate_free, 2 * it + s0 + half - 6)
                    tile(s, 0, h1, KT, s).then_inc(w_used, 1)
            s0 = SLABS["pool_mix"][0]
            pe.wait_ge(w_split, s0 + 1)
            pe.wait_ge(pooled_ready, POOL_GROUPS)
            pe.wait_ge(value_out, 1)
            for i, g in enumerate(POOL_ORDER):
                if i >= 2:
                    pe.wait_ge(mix_hi, i - 1)
                for n in range(0, S, HALF):
                    last = product(wide(2 + i % 2)[:, n:n + HALF], weight(s0 % 2, g * P),
                                   tuple(part[:, n:n + HALF] for part in pooled[g]), True, True)
                last.then_inc(w_used if i == POOL_GROUPS - 1 else pool_done, 1)
            for n in range(2):
                s = SLABS["last_gates"][0] + n
                pe.wait_ge(w_split, s + 1)
                pe.wait_ge(gate_free, s - 7)
                tile(s % 2, 0, h1, KT, 1 - s % 2).then_inc(w_used, 1)
            pe.wait_ge(mix_free, POOL_GROUPS)
            s0 = SLABS["proj_pool"][0]
            with pe.Fori(0, 2) as it:
                for s in range(2):
                    pe.wait_ge(w_split, 2 * it + s0 + s + 1)
                    for half in range(2):
                        pe.wait_ge(gate_free, 4 * it + s0 + 2 * s + half - 7)
                        tile(s, half * POOL_GROUPS * P, mixed, POOL_GROUPS, 1 - half).then_inc((first_half, w_used)[half], 1)
            pe.wait_ge(shifted_in, 48)
            for n in range(4):
                last = nc.tensor.matmul(ps[:, 4 + n, :], flip[:], bias[:, 2 * n:2 * n + 2, :].rearrange("p h u -> p (h u)"),
                                        start=True, stop=True)
            last.then_inc(flipped, 1)
            pe.wait_ge(bias_done, 1)
            for n in range(3):
                last = nc.tensor.matmul(ps[:, 4 + n, :], flip[:],
                                        bias_2[:].rearrange("p h u -> p (h u)")[:, n * HALF:(n + 1) * HALF],
                                        start=True, stop=True)
            last.then_inc(flipped, 1)
            s0 = SLABS["query"][0]
            with pe.Fori(0, 4) as it:
                for s in range(2):
                    pe.wait_ge(w_split, 2 * it + s0 + s + 1)
                    pe.wait_ge(gate_free, 2 * it + s0 + s - 3)
                    tile(s, 0, h1, KT, 1 - s).then_inc(w_used, 1)
            pe.wait_ge(masks_ready, 1)
            pe.wait_ge(value_out, 1)
            pe.wait_ge(bias_done, 2)
            pe.wait_ge(gate_free, POOL_GROUPS + 4 * KT)
            def mix_logits(unit):
                group, q = unit // 4, unit % 4
                i = group // 2
                if q == 0:
                    pe.wait_ge(qt_lo, group + 1)
                if unit >= 2:
                    pe.wait_ge(logits_ready, unit - 1)
                for n in range(0, (i + 1) * P, HALF):
                    m = min(HALF, (i + 1) * P - n)
                    out = wide(unit % 2)[:, n:n + m]
                    product(out, tuple(e[:, q, :] for e in q_tile[group % 2]), tuple(e[:, n:n + m] for e in key), True, False)
                    last = nc.tensor.matmul(out, ident16[:], mask[:, mask_at[i] + n:mask_at[i] + n + m],
                                            start=False, stop=True)
                last.then_inc(qk_done, 1)

            def mix_transposes(group, j):
                n_tr = tiles_before(group) + j
                if j == 0:
                    pe.wait_ge(probs_ready, BY_POOL * (group + 1))
                    pe.wait_ge(last_ready, (4 - BY_POOL) * (group + 1))
                if n_tr >= 2:
                    pe.wait_ge(pt_out, n_tr - 1)
                for q in range(4):
                    last = nc.tensor.transpose(ps[:, 4 + n_tr % 2, q * P:(q + 1) * P],
                                               mix_rows[group % 2][q][:, j * P:(j + 1) * P], ident[:])
                last.then_inc(tr_done, 1)

            def mix_values(group, j):
                n_tr = tiles_before(group) + j
                if j == 0 and group >= 2:
                    pe.wait_ge(o_lo, group - 1)
                pe.wait_ge(pt_out, n_tr + 1)
                nc.tensor.matmul(ps[:, 6 + group % 2, :], value[:, j, :], probs_t[n_tr % 2][:], start=j == 0,
                                 stop=j == group // 2).then_inc(pv_done, 1)

            for q in range(4):
                mix_logits(q)
            pending = ()
            for group in range(2 * NT):
                for n in range(4):
                    if group + 1 < 2 * NT:
                        mix_logits(4 * (group + 1) + n)
                    for g, j in pending:
                        mix_values(g, j)
                    pending = [(group, j) for j in tiles_of(group, n)]
                    for g, j in pending:
                        mix_transposes(g, j)
            for g, j in pending:
                mix_values(g, j)
            s0 = SLABS["proj_attn"][0]

            def proj_tile(n, s, late=(None,)):
                pe.wait_ge(w_split, n + s0 + 1)
                pe.wait_ge(merge_free, n + 1)
                tile(s, 0, att, KT, s, late=late).then_inc(w_used, 1)

            pe.wait_ge(o_lo, 2 * NT - 1)
            proj_tile(0, 0, (KT // 2, o_lo, 2 * NT))
            proj_tile(1, 1)
            with pe.Fori(1, 4) as it:
                for s in range(2):
                    proj_tile(2 * it + s, s)
            s0 = SLABS["mix_out"][0]

            def out_tile(n, s, late=(None,)):
                pe.wait_ge(w_split, n + s0 + 1)
                pe.wait_ge(y_free, n + 1)
                tile(s, 0, merged, KT, s, late=late).then_inc(w_used, 1)

            def out_tiles(first, end):
                with pe.Fori(first, end) as it:
                    for s in range(2):
                        out_tile(2 * it + s, s)

            pe.wait_ge(merge_free, 2 + KT - 1)
            out_tile(0, 0, (KT - 1, merge_free, 2 + KT))
            out_tile(1, 1)
            out_tiles(1, 2)
            pe.wait_ge(mem_squared, 1)
            for k in range(KT):
                last = nc.tensor.matmul(ps[:, 6, 0:M], ones[:], mem_sq[:, k, :], start=k == 0, stop=k == KT - 1)
            last.then_inc(mem_total, 1)
            out_tiles(2, 4)
            pe.wait_ge(mem_lo, 1)
            pe.wait_ge(y_free, 2 + KT)
            s0 = SLABS["mem_key"][0]
            for n in range(MEM_HEADS):
                pe.wait_ge(w_split, s0 + n + 1)
                for k in range(KT):
                    last = product(wide(0)[:, n * M:(n + 1) * M], weight(n % 2, k * P),
                                   (memn[0][:, k, :], memn[1][:, k, :]), k == 0, k == KT - 1)
                last.then_inc(w_used, 1)
                if n == 0:
                    total_added(0)
                if n == MEM_HEADS - 1:
                    total_tile("mem_pre", 0)
            s0 = SLABS["mem_value"][0]
            for n in range(4):
                pe.wait_ge(w_split, s0 + n + 1)
                for j in range(MT):
                    for k in (2 * n, 2 * n + 1):
                        last = product(wide(1)[:, j * HALF:(j + 1) * HALF],
                                       tuple(v[:, k, j * P:(j + 1) * P] for v in memn),
                                       weight(n % 2, k % 2 * HALF, HALF), k == 0, k == KT - 1)
                last.then_inc(w_used, 1)
                total_tile("mem_pre", n + 1)
            for k in range(5, KT):
                total_tile("mem_pre", k)
            pe.wait_ge(mkv_hi, 2)
            pe.wait_ge(mkv_lo, 1)
            first_tiles("mem_query", "mem_pre", normed)
            for n in range(2, MEM_HEADS):
                pe.wait_ge(w_split, SLABS["mem_query"][0] + n + 1)
                pe.wait_ge(mq_lo, n + 1)
                tile(n % 2, 0, normed, KT, n % 2).then_inc(w_used, 1)
            pe.wait_ge(mq_lo, 2 + MEM_HEADS)

            def mem_logits(n):
                if n >= 2:
                    pe.wait_ge(m_exp, 4 * (n - 1))
                for q in range(4):
                    t0 = (4 * (n % 2) + q) * P
                    last = product(wide(n % 2)[:, q * M:(q + 1) * M], tuple(v[:, n // 2, t0:t0 + P] for v in qm),
                                   tuple(v[:, n // 2, :] for v in kmem), True, True)
                last.then_inc(m_qk, 1)

            def mem_values(n):
                if n >= 2:
                    pe.wait_ge(m_olo, n - 1)
                for j in range(MT):
                    pe.wait_ge(m_copied, MT * n + j + 1)
                    d0 = n // 2 * P
                    nc.tensor.matmul(ps[:, 6 + n % 2, :], vmem[:, j, d0:d0 + P], mpt[j][:], start=j == 0,
                                     stop=j == MT - 1).then_inc(m_pv, 1)

            mem_logits(0)
            for n in range(2 * MEM_HEADS):
                if n + 1 < 2 * MEM_HEADS:
                    mem_logits(n + 1)
                if n:
                    mem_values(n - 1)
                pe.wait_ge(m_probs, n + 1)
                for j in range(MT):
                    if n:
                        pe.wait_ge(m_copied, MT * (n - 1) + j + 1)
                    for q in range(4):
                        last = nc.tensor.transpose(ps[:, 4 + j, q * P:(q + 1) * P],
                                                   mprobs[:, n % 2, q, j * P:(j + 1) * P], ident[:])
                    last.then_inc(m_tr, 1)
            mem_values(2 * MEM_HEADS - 1)
            pe.wait_ge(m_olo, 2 * MEM_HEADS)
            s0 = SLABS["mem_out"][0]
            with pe.Fori(0, 2) as it:
                for s in range(2):
                    pe.wait_ge(w_split, 2 * it + s0 + s + 1)
                    for half in range(2):
                        pe.wait_ge(y_free, 4 * it + 2 * s + half + KT + 1)
                        tile(s, half * 4 * P, om, 4, half).then_inc((first_half, w_used)[half], 1)
            total_added(1)
            total("ffn_pre")
            s0 = SLABS["ffn"][0]

            def ffn_chunk(c, tiles, first=0):
                for j in range(first, tiles):
                    pe.wait_ge(w_split, 12 * c + s0 + 2 * j + 1)
                    if j < 2:
                        pe.wait_ge(f_added, 8 * c + 2 * j + 6)
                    else:
                        pe.wait_ge(f_mul, 4 * c + j - 1)
                    tile(0, 0, normed, KT, 2 * (j % 2)).then_inc(w_used, 1)
                    pe.wait_ge(w_split, 12 * c + s0 + 2 * j + 2)
                    tile(1, 0, normed, KT, 2 * (j % 2) + 1).then_inc(w_used, 1)
                per = 8 // tiles
                for m in range(KT):
                    if m % per == 0:
                        pe.wait_ge(w_split, 12 * c + s0 + 2 * tiles + m // per + 1)
                    if m < 4:
                        pe.wait_ge(f_mul, 4 * c + (m // 2 + tiles - 1 if tiles == 4 else m // 2 + 1))
                    else:
                        pe.wait_ge(f_added, 8 * c + 8 + m - 3)
                    for k in range(tiles):
                        if m == 0:
                            pe.wait_ge(f_lo, 4 * c + 2 + k + 1)
                        for n in range(0, S, HALF):
                            last = product(wide(m % 4)[:, n:n + HALF], weight(m // per % 2, (m % per * tiles + k) * P),
                                           tuple(v[:, k, n:n + HALF] for v in hidden), k == 0, k == tiles - 1)
                    last.then_inc(w_used if m % per == per - 1 else first_half, 1)

            pe.wait_ge(y_free, 2 + 2 * KT)
            first_tiles("ffn", "ffn_pre", normed)
            ffn_chunk(0, CHUNK, 1)
            with pe.Fori(1, FF_TILES // CHUNK) as c:
                ffn_chunk(c, CHUNK)
            ffn_chunk(FF_TILES // CHUNK, FF_TILES % CHUNK)
            total_added(2)
            total("attn_2")
            first_tiles("in_2", "attn_2", normed)
            s0 = SLABS["in_2"][0]
            for n in range(2, 5):
                pe.wait_ge(w_split, s0 + n + 1)
                pe.wait_ge(c_free, n - 1)
                tile(n % 2, 0, normed, KT, n % 2).then_inc(w_used, 1)
                if n >= 3:
                    total(("q_a", "kv_a")[n - 3])
            pe.wait_ge(tables_in, 48)

            def diff_total(q, e):
                pe.wait_ge(d_sq, q + 1)
                over_features(wide(2 + e), tmp[e], halves[:, 0, :]).then_inc(d_tot, 1)

            with pe.Fori(0, DIFF_HEADS) as it:
                for e in range(2):
                    pe.wait_ge(w_split, 2 * it + s0 + 5 + e + 1)
                    pe.wait_ge(d_free, 2 * it + e + 1)
                    tile(1 - e, 0, normed, KT, 1 - e,
                         between=(lambda: diff_total(2 * it, 0)) if e else None).then_inc(w_used, 1)
                diff_total(2 * it + 1, 1)
            pe.wait_ge(d_free, 2 + 2 * DIFF_HEADS)
            s0 = SLABS["diff_value"][0]
            for n in range(4):
                pe.wait_ge(w_split, s0 + n + 1)
                for j in range(NT):
                    for k in (2 * n, 2 * n + 1):
                        last = product(ps[:, j, :], tuple(v[:, k, j * P:(j + 1) * P] for v in normed),
                                       weight((s0 + n) % 2, k % 2 * HALF, HALF), k == 0, k == KT - 1)
                last.then_inc(w_used, 1)
            s0 = SLABS["uq_rope"][0]
            pe.wait_ge(w_split, s0 + 1)
            for p in range(2):
                pe.wait_ge(dv_act, 2 * p + 2)
                pe.wait_ge(dv_dve, 2 * p + 2)
                for n in range(2):
                    tile(s0 % 2, (2 * p + n) * 2 * P, cq, 2, 2 * p + n).then_inc(w_used if p and n else r_done, 1)
            s0 = SLABS["ukv"][0]
            pe.wait_ge(w_split, s0 + 1)
            for j in range(NT):
                pe.wait_ge(r_free, j // 4 + 1)
                product(ps[:, j, :], tuple(v[:, 0, j * P:(j + 1) * P] for v in ckv),
                        weight(s0 % 2, HALF, HALF), True, True).then_inc(v_done, 1)
            pe.wait_ge(v_act, 4)
            pe.wait_ge(v_dve, 4)

            def expand(e):
                hd, is_q = e // 2, e % 2
                if e >= 2:
                    pe.wait_ge(g_free, e - 1)
                s = SLABS["uq_nope" if is_q else "ukv"][0]
                if e == 1:
                    pe.wait_ge(w_split, s + 1)
                parts, kt = (cq, 2) if is_q else (ckv, 1)
                tile(s % 2, hd * kt * P, parts, kt, e % 2).then_inc(w_used if hd == MLA_HEADS - 1 else g_done, 1)

            def head_total(e):
                pe.wait_ge(g_sq, e + 1)
                if e == 0:
                    pe.wait_ge(rope_sq, 3)
                hd, is_q = e // 2, e % 2
                over_features(wide(2 + e % 2), tmp[e % 2], ones[:], True, False)
                rope = q_rope_sq[:, hd // 2, :] if is_q else k_rope_sq[:]
                over_features(wide(2 + e % 2), rope, halves[:, 1 + (hd % 2 if is_q else 0), :],
                              False, True).then_inc(g_tot, 1)

            expand(0)
            for e in range(2 * MLA_HEADS):
                head_total(e)
                if e + 1 < 2 * MLA_HEADS:
                    expand(e + 1)
            def logits(unit):
                hd, t0 = unit // NT, unit % NT * P
                p, d = head_parts[hd % 2], unit - NT * MLA_HEADS
                if unit % NT == 0:
                    pe.wait_ge(head_split, splits_before(hd + 1))
                if d < 0:
                    if unit >= 2:
                        pe.wait_ge(a_exp, unit - 1)
                    for n in range(0, S, HALF):
                        out, keys = wide(unit % 2)[:, n:n + HALF], slice(n, n + HALF)
                        product(out, (p[0][:, t0:t0 + P], p[1][:, t0:t0 + P]), (p[2][:, keys], p[3][:, keys]), True, False)
                        nc.tensor.matmul(out, p[6][:, t0:t0 + P], p[7][:, keys], start=False, stop=False)
                        last = nc.tensor.matmul(out, p[6][0:64, t0:t0 + P], p[8][0:64, keys], start=False, stop=True)
                    last.then_inc(a_qk, 1)
                    return
                for m in range(2):
                    if d:
                        pe.wait_ge(e_red, 2 * d + m - 1)
                    else:
                        pe.wait_ge(a_exp, NT * MLA_HEADS - 1 + m)
                    lanes = slice(64 * m, 64 * m + 64)
                    for n in range(0, S, HALF):
                        out, keys = wide(m)[:, n:n + HALF], slice(n, n + HALF)
                        nc.tensor.matmul(out, p[m][:, t0:t0 + P], p[2 + m][:, keys], start=True, stop=False)
                        last = nc.tensor.matmul(out, p[m][lanes, t0:t0 + P], p[8][lanes, keys], start=False, stop=True)
                    last.then_inc(a_qk, 1)

            def probs_out(n):
                return (a_ptlo if n < 16 * MLA_HEADS else a_pthi), n + 1

            def transposes(group, j):
                if j == 0:
                    pe.wait_ge(*((a_exp, 4 * group + 4) if group < 2 * MLA_HEADS else (a_probs, 4 * (group - 2 * MLA_HEADS) + 4)))
                if 8 * group + j >= 2:
                    pe.wait_ge(*probs_out(8 * group + j - 2))
                for q in range(4):
                    last = nc.tensor.transpose(ps[:, 4 + j % 2, q * P:(q + 1) * P],
                                               prob_rows[group % 2][q][:, j * P:(j + 1) * P], ident[:])
                last.then_inc(a_tr, 1)

            def add_values(group, j):
                e, diff = group // 2 % 2, group >= 2 * MLA_HEADS
                if j == 0 and group:
                    pe.wait_ge(a_out, group)
                pe.wait_ge(*probs_out(8 * group + j))
                out, cols_of = ps[:, 6 + group % 2, :], slice(j * P, (j + 1) * P)
                if diff:
                    last = nc.tensor.matmul(out, v_plain[e][:, cols_of], pt_plain[j % 2][:], start=j == 0, stop=j == NT - 1)
                else:
                    last = product(out, tuple(v[:, cols_of] for v in head_parts[e][4:6]), tuple(v[:] for v in pt[j % 2]),
                                   j == 0, j == NT - 1)
                last.then_inc(a_pv, 1)

            def finish(group):
                add_values(group, NT - 2)
                add_values(group, NT - 1)
                pe.wait_ge(a_diag, group + 1)
                nc.tensor.matmul(ps[:, 7 - group % 2, :], ones[:], diagonal[:].rearrange("p q n -> p (q n)"),
                                 start=True, stop=True).then_inc(a_spread, 1)

            pe.wait_ge(g_free, 2 * MLA_HEADS)
            for q in range(4):
                logits(q)
            for group in range(GROUPS):
                for n in range(4):
                    if group + 1 < GROUPS:
                        logits(4 * (group + 1) + n)
                    if n:
                        add_values(group, 2 * n - 2)
                        add_values(group, 2 * n - 1)
                    elif group:
                        finish(group - 1)
                    transposes(group, 2 * n)
                    transposes(group, 2 * n + 1)
            finish(GROUPS - 1)
            def head_square_total(n):
                pe.wait_ge(s_sq, n + 1)
                if n >= 2:
                    pe.wait_ge(s_rs, n - 1)
                over_features(wide(2 + n % 2), tmp[n % 2], ones[:]).then_inc(s_tot, 1)

            s0 = SLABS["out_2"][0]
            pe.wait_ge(a_out, GROUPS)
            for s in range(2):
                pe.wait_ge(w_split, s0 + s + 1)
            for k in range(KT):
                pe.wait_ge(s_lo, k + 1)
                for s in range(2):
                    for n in range(0, S, HALF):
                        last = product(wide(s)[:, n:n + HALF], weight(s, k * P),
                                       tuple(e[:, k, n:n + HALF] for e in o_all), k == 0, k == KT - 1)
                    if k == KT - 1:
                        last.then_inc(w_used, 1)
                if k in (0, 1, 2, 4):
                    head_square_total((0, 1, 2, 4).index(k))
            with pe.Fori(1, 4) as it:
                for s in range(2):
                    pe.wait_ge(w_split, 2 * it + s0 + s + 1)
                    pe.wait_ge(x_added, 2 * it + 3 * KT + s - 1)
                    tile(s, 0, o_all, KT, s).then_inc(w_used, 1)
            total("mlp_2")
            first_tiles("mlp_2", "mlp_2", normed)
            s0 = SLABS["mlp_2"][0]

            def mlp_chunk(c, first=0):
                for j in range(first, CHUNK):
                    pe.wait_ge(w_split, 8 * c + s0 + j + 1)
                    pe.wait_ge(u_added, 8 * c + 5 + j)
                    tile(j % 2, 0, normed, KT, j).then_inc(w_used, 1)
                for m in range(KT):
                    if m % 2 == 0:
                        pe.wait_ge(w_split, 8 * c + s0 + 4 + m // 2 + 1)
                    if m < 4:
                        pe.wait_ge(u_relu, 4 * c + m + 1)
                    else:
                        pe.wait_ge(u_added, 8 * c + 8 + m - 3)
                    for k in range(CHUNK):
                        if m == 0:
                            pe.wait_ge(u_lo, 4 * c + 2 + k + 1)
                        for n in range(0, S, HALF):
                            last = product(wide(m % 4)[:, n:n + HALF], weight(m // 2 % 2, (m % 2 * CHUNK + k) * P),
                                           tuple(v[:, k, n:n + HALF] for v in hidden), k == 0, k == CHUNK - 1)
                    last.then_inc(w_used if m % 2 else first_half, 1)

            mlp_chunk(0, 2)
            with pe.Fori(1, FF2_TILES // CHUNK) as c:
                mlp_chunk(c)

        @block.scalar
        def _(act):
            step = Chain(act, act_step)

            def squares(name, src, ready):
                tiles, before = PRE[name]
                for k in range(tiles):
                    act.wait_ge(*ready(k))
                    if k >= 2:
                        act.wait_ge(n_added, before - PRE_ORDER.index(name) + k - 1)
                    nc.scalar.activation(tmp[k % 2][:], src(k), ACT.Square).then_inc(n_sq, 1)

            def post_square(post, k, src):
                if k >= 3:
                    act.wait_ge(n_acc, 7 * post + k - 2)
                nc.scalar.activation(tmp[k % 2][:] if k else acc[:], src, ACT.Square).then_inc(n_post_sq, 1)

            def inverse(r, width=D):
                act.wait_ge(n_sum, r + 1)
                step(nc.scalar.activation(acc[:], wide(2), ACT.Ln, bias=eps[:], scale=1.0 / width))
                nc.scalar.activation(acc[:], acc[:], ACT.Exp, scale=-0.5).then_inc(n_rs, 1)

            def round_hi(name, dst):
                tiles, before = PRE[name]
                for k in range(tiles):
                    act.wait_ge(n_tmp, before + k + 1)
                    nc.scalar.activation(dst[:, k, :], tmp[k % 2][:], ACT.Copy).then_inc(n_hi, 1)

            for k in range(4):
                act.dma_start(x_in[:, 2 * k:2 * k + 2, :], t["x"][:, 2 * k:2 * k + 2, :]).then_inc(x_in_landed[k], 16)
            for dst, name in ((cols, "cols"), (ident, "c_ident"), (tri, "c_tri"), (pool_fix, "c_pool_fix"),
                              (table, "rel_bias_table"), (onehot, "c_onehot"),
                              (table_2, "rel_bias_2"), (onehot_2, "c_onehot_2")):
                act.dma_start(dst[:], t[name]).then_inc(consts_in, 16)
            act.wait_ge(dve_consts, 1)
            squares("mix_pre", lambda k: x_in[:, k, :], lambda k: (x_in_landed[k // 2], 16))
            inverse(0)
            act.wait_ge(frow_done, 1)
            step(nc.scalar.activation(frow[:], ps[0:HEADS, 6, 0:384], ACT.Copy))
            step(nc.scalar.activation(frow_2[:], ps[0:DIFF_HEADS, 7, :], ACT.Copy))
            act.dma_start(t["bias_rows"], frow[:]).then_inc(frow_out, 16)
            act.dma_start(t["bias_rows_2"], frow_2[:]).then_inc(frow_out, 16)
            round_hi("mix_pre", h1[0])
            def in_tile(n, dst):
                act.wait_ge(w_used, n + 1)
                nc.scalar.activation(dst, wide(n % 2), ACT.Copy).then_inc(in_hi, 1)

            act.wait_ge(w_used, 1)
            step(nc.scalar.activation(kidx_t[0:IDX_DIM, :], wide(0)[0:IDX_DIM, :], ACT.Copy))
            act.dma_start(kidx_t[64:P, :], kidx_t[0:64, :]).then_inc(kidx_doubled, 16)
            act.wait_ge(frow_out, 32)
            nc.scalar.activation(wi_t[64:P, :], wide(0)[64:P, :], ACT.Copy).then_inc(turn_ready, 1)
            in_tile(1, qidx[0][:, 0, :])
            act.wait_ge(kidx_doubled, 16)
            nc.scalar.activation(kidx[0][:], kidx_t[:], ACT.Copy).then_inc(in_hi, 1)
            in_tile(2, qidx[0][:, 1, :])
            act.wait_ge(w_used, 4)
            nc.scalar.activation(value_t[:], wide(1), ACT.Copy).then_inc(turn_ready, 1)
            unit = 0
            for i in reversed(range(2, NT)):
                for hd in range(IDX_HEADS):
                    act.wait_ge(idx_done, unit + 1)
                    if unit >= 2:
                        act.wait_ge(idx_added, unit - 1)
                    n = (i + 1) * P
                    nc.scalar.activation(tmp[unit % 2][:, 0:n], wide(2 + unit % 2)[:, 0:n], ACT.Relu,
                                         scale=IDX_DIM ** -0.5 * IDX_HEADS ** -0.5).then_inc(idx_relu, 1)
                    unit += 1
            in_tile(4, key[0][:])
            act.wait_ge(turn_done, 2)
            nc.scalar.activation(value[:], wide(2).rearrange("p (j n) -> p j n", j=NT), ACT.Copy).then_inc(value_out, 1)

            def round_slab(s, nth):
                act.wait_ge(raw_landed[s], 16 * nth + 16)
                nc.scalar.activation(w_hi[s][:], raw[s][:], ACT.Copy).then_inc(w_rounded, 1)

            for g in range(POOL_GROUPS):
                n = SLABS["mix_in"][0] + 5 + g
                act.wait_ge(w_used, n + 1)
                if n + 2 == SPLIT_BY_TWO[0]:
                    act.wait_ge(w_split, n + 2)
                if n + 2 >= SPLIT_BY_TWO[0]:
                    round_slab(n % 2, n // 2 + 1)
                step(nc.scalar.activation(u[:, g, :], wide(n % 2), ACT.Copy, scale=float(2 << g)))
                nc.scalar.activation(u_plain[g][:], wide(n % 2), ACT.Copy).then_inc(gate_free, 1)
            act.wait_ge(idx_added, unit)

            def stage(i, n, func, half, first):
                if not first:
                    act.wait_ge(staged[half], 8 * (i - (1 - half)))
                nc.scalar.activation(tmp[half][:], wide(half), func).then_inc(gate_free, 1)
                act.wait_ge(gate_free, i + POOL_GROUPS + 1)
                act.dma_start(t["gates"][n], tmp[half][:]).then_inc(staged[half], 16)

            def gate_pair(it, first):
                for half in range(2):
                    s = (SLABS["gates"][0] + half) % 2
                    act.wait_ge(w_used, 2 * it + SLABS["gates"][0] + half + 1)
                    round_slab(s, it + (SLABS["gates"][0] + half) // 2 + 1)
                    stage(2 * it + half, 2 * it + half + KT, ACT.Sigmoid, s, first)

            gate_pair(0, True)
            with act.Fori(1, 7) as it:
                gate_pair(it, False)
            for i, g in enumerate(POOL_ORDER):
                if i == POOL_GROUPS - 1:
                    act.wait_ge(w_used, SLABS["pool_mix"][0] + 1)
                    round_slab((SLABS["pool_mix"][0] + 2) % 2, (SLABS["pool_mix"][0] + 2) // 2)
                else:
                    act.wait_ge(pool_done, i + 1)
                step(nc.scalar.activation(mixed_sum[:, g, :], wide(2 + i % 2), ACT.Copy, scale=col("pool_scale", g)))
                nc.scalar.activation(mixed[0][:, g, :], wide(2 + i % 2), ACT.Copy, scale=col("pool_scale", g)).then_inc(mix_hi, 1)
            for dst, name, heads, width in ((bias, "bias_rows", HEADS, 384), (bias_2, "bias_rows_2", DIFF_HEADS, HALF)):
                rows = t[name]
                act.dma_start(dst[:], bass.AP(tensor=rows.tensor, offset=rows.offset,
                                              ap=[[1, P], [width, heads], [1, dst.shape[2]]])).then_inc(shifted_in, 16)
            act.dma_start(flip[:], t["c_flip"]).then_inc(shifted_in, 16)
            for n in range(2):
                act.wait_ge(w_used, SLABS["last_gates"][0] + n + 1)
                stage(14 + n, KT + 14 + n, ACT.Sigmoid, 1 - n, False)
            s0 = SLABS["proj_pool"][0]
            with act.Fori(0, 4) as it:
                for half in range(2):
                    act.wait_ge((first_half, w_used)[half], it + (1, s0 + 1)[half])
                    stage(2 * it + 16 + half, 2 * it + half, ACT.Copy, 1 - half, False)
            act.wait_ge(flipped, 1)
            nc.scalar.activation(bias[:].rearrange("p h u -> p (h u)"), ps[:, 4:8, :].rearrange("p b n -> p (b n)"),
                                 ACT.Copy).then_inc(bias_done, 1)
            act.wait_ge(flipped, 2)
            nc.scalar.activation(bias_2[:].rearrange("p h u -> p (h u)"), ps[:, 4:7, :].rearrange("p b n -> p (b n)"),
                                 ACT.Copy).then_inc(bias_done, 1)
            act.wait_ge(bias_done, 2)
            act.dma_start(t["bias_tiles_2"].rearrange("h p u -> p h u"), bias_2[:]).then_inc(bias_2_out, 16)
            act.wait_ge(bias_2_out, 16)
            for k in range(KT):
                act.wait_ge(w_used, SLABS["query"][0] + k + 1)
                nc.scalar.activation(query[:, k, :], wide(1 - k % 2), ACT.Copy, scale=P ** -0.5).then_inc(gate_free, 1)
            for half in range(2):
                act.wait_ge(staged[half], 16 * 12)
            def round_query(group):
                if group >= 2:
                    act.wait_ge(qk_done, 4 * (group - 1))
                i, g = group // 2, group % 2
                nc.scalar.activation(q_tile[g][0][:], query[:, 4 * g:4 * g + 4, i * P:(i + 1) * P], ACT.Copy).then_inc(qt_hi, 1)

            def mix_exps(unit):
                group, q = unit // 4, unit % 4
                row = mix_rows[group % 2][q][:, 0:(group // 2 + 1) * P]
                act.wait_ge(nmax_ready, unit + 1)
                nc.scalar.activation(row, row, ACT.Exp, bias=mix_stat(unit, 3),
                                     accum_out=mix_stat(unit, 4)).then_inc(exp_done, 1)

            def mix_out_hi(group):
                i, g = group // 2, group % 2
                act.wait_ge(pv_done, tiles_before(group + 1))
                nc.scalar.activation(att[0][:, 4 * g:4 * g + 4, i * P:(i + 1) * P],
                                     ps[:, 6 + g, :].rearrange("p (h q) -> p h q", h=4), ACT.Copy).then_inc(o_hi, 1)

            act.wait_ge(masks_ready, 1)
            act.wait_ge(gate_free, POOL_GROUPS + 4 * KT)
            for group in range(2):
                round_query(group)
            for q in range(4):
                mix_exps(q)
            for group in range(2 * NT):
                for n in range(4):
                    if n == 0 and group:
                        mix_out_hi(group - 1)
                    for j in tiles_of(group, n):
                        n_tr = tiles_before(group) + j
                        act.wait_ge(tr_done, n_tr + 1)
                        if n_tr >= 2:
                            act.wait_ge(pv_done, n_tr - 1)
                        nc.scalar.activation(probs_t[n_tr % 2][:], ps[:, 4 + n_tr % 2, :], ACT.Copy).then_inc(pt_out, 1)
                    if group + 1 < 2 * NT:
                        mix_exps(4 * (group + 1) + n)
                    if n == 1 and group + 2 < 2 * NT:
                        round_query(group + 2)
            mix_out_hi(2 * NT - 1)
            act.wait_ge(qk_done, HEADS * NT)
            for k in range(KT):
                if k >= 2:
                    act.wait_ge(merge_free, 2 + k - 1)
                for n in range(3):
                    act.dma_start(gated[k % 2][:, n, :], t["gates"][KT * n + k]).then_inc(gates_in[k % 2], 16)
            act.sem_inc(y_free, 2)
            act.wait_ge(merge_free, 2 + KT)
            act.dma_start(x[:], t["x"]).then_inc(x_landed, 16)
            act.dma_start(mem_in[:], t["mem"]).then_inc(mem_landed, 16)
            for k in range(KT):
                act.wait_ge(w_used, SLABS["mix_out"][0] + k + 1)
                post_square(0, k, wide(k % 2))
                nc.scalar.activation(y[:, k, :], wide(k % 2), ACT.Copy).then_inc(y_free, 1)
                if k == 1:
                    act.wait_ge(mem_landed, 16)
                    nc.scalar.activation(mem_sq[:], mem_in[:], ACT.Square).then_inc(mem_squared, 1)
                if k == 4:
                    act.wait_ge(mem_total, 1)
                    step(nc.scalar.activation(mem_rms[:], ps[:, 6, 0:M], ACT.Ln, bias=eps[:], scale=1.0 / D))
                    nc.scalar.activation(mem_rms[:], mem_rms[:], ACT.Exp, scale=-0.5).then_inc(mem_rs, 1)
                if k == 6:
                    act.wait_ge(mem_scaled, KT)
                    nc.scalar.activation(memn[0][:], mem_in[:], ACT.Copy).then_inc(mem_hi, 1)
            inverse(1)
            squares("mem_pre", lambda k: x[:, k, :], lambda k: (x_added, k + 1))
            act.wait_ge(w_used, SLABS["mem_value"][0] + 4)
            nc.scalar.activation(kmem[0][:], wide(0).rearrange("p (h m) -> p h m", h=MEM_HEADS), ACT.Copy).then_inc(mkv_hi, 1)
            nc.scalar.activation(vmem[:], wide(1).rearrange("p (j n) -> p j n", j=MT), ACT.Copy).then_inc(mkv_hi, 1)
            inverse(2)
            round_hi("mem_pre", normed[0])
            for n in range(MEM_HEADS):
                act.wait_ge(w_used, SLABS["mem_query"][0] + n + 1)
                nc.scalar.activation(qm[0][:, n, :], wide(n % 2), ACT.Copy, scale=P ** -0.5).then_inc(mq_hi, 1)
            def mem_exps(n):
                act.wait_ge(m_max, n + 1)
                if n >= 2:
                    act.wait_ge(m_tr, MT * (n - 1))
                for q in range(4):
                    nc.scalar.activation(mprobs[:, n % 2, q, :], wide(n % 2)[:, q * M:(q + 1) * M], ACT.Exp,
                                         bias=mstat[:, n % 2, 1, q:q + 1],
                                         accum_out=mstat[:, n % 2, 2, q:q + 1]).then_inc(m_exp, 1)

            def mem_out_hi(n):
                act.wait_ge(m_pv, MT * (n + 1))
                t0 = n % 2 * HALF
                nc.scalar.activation(om[0][:, n // 2, t0:t0 + HALF], ps[:, 6 + n % 2, :], ACT.Copy).then_inc(m_ohi, 1)

            mem_exps(0)
            for n in range(2 * MEM_HEADS):
                if n:
                    mem_out_hi(n - 1)
                for j in range(MT):
                    act.wait_ge(m_tr, MT * n + j + 1)
                    if n:
                        act.wait_ge(m_pv, MT * (n - 1) + j + 1)
                    nc.scalar.activation(mpt[j][:], ps[:, 4 + j, :], ACT.Copy).then_inc(m_copied, 1)
                if n + 1 < 2 * MEM_HEADS:
                    mem_exps(n + 1)
            mem_out_hi(2 * MEM_HEADS - 1)
            act.wait_ge(m_olo, 2 * MEM_HEADS)
            for k in range(KT):
                act.wait_ge(*((w_used, SLABS["mem_out"][0] + k // 2 + 1) if k % 2 else (first_half, 4 + k // 2 + 1)))
                post_square(1, k, wide(k % 2))
                nc.scalar.activation(y[:, k, :], wide(k % 2), ACT.Copy).then_inc(y_free, 1)
            inverse(3)
            squares("ffn_pre", lambda k: x[:, k, :], lambda k: (x_added, KT + k + 1))
            inverse(4)
            round_hi("ffn_pre", normed[0])
            s0 = SLABS["ffn"][0]

            def ffn_hidden(c, tiles):
                for j in range(tiles):
                    act.wait_ge(w_used, 12 * c + s0 + 2 * j + 1)
                    act.wait_ge(f_lo, 4 * c + j + 1)
                    nc.scalar.activation(tmp[j % 2][:], wide(2 * (j % 2)), ACT.Silu).then_inc(f_silu, 1)
                    act.wait_ge(f_mul, 4 * c + j + 1)
                    nc.scalar.activation(hidden[0][:, j, :], tmp[j % 2][:], ACT.Copy).then_inc(f_hi, 1)

            with act.Fori(0, FF_TILES // CHUNK) as c:
                ffn_hidden(c, CHUNK)
            ffn_hidden(FF_TILES // CHUNK, FF_TILES % CHUNK)
            for k in range(KT):
                act.wait_ge(f_added, 8 + 8 * (FF_TILES // CHUNK) + k + 1)
                post_square(2, k, y[:, k, :])
            inverse(5)
            squares("attn_2", lambda k: x[:, k, :], lambda k: (x_added, 2 * KT + k + 1))
            for dst, name in ((cos, "c_cos"), (sin, "c_sin"), (halves, "c_halves")):
                act.dma_start(dst[:], t[name]).then_inc(tables_in, 16)
            inverse(6)
            round_hi("attn_2", normed[0])
            act.wait_ge(lam_sum, 1)
            nc.scalar.activation(lam_ab, lam_ab, ACT.Exp).then_inc(lam_exp, 1)
            s0 = SLABS["in_2"][0]
            for n, dst in enumerate((c_q[:, 0, :], c_q[:, 1, :], c_kv[:, 0, :])):
                act.wait_ge(w_used, s0 + n + 1)
                nc.scalar.activation(dst, wide(n % 2), ACT.Copy).then_inc(c_free, 1)
            squares("q_a", lambda k: c_q[:, k, :], lambda k: (c_free, k + 1))
            inverse(7, 2 * P)
            round_hi("q_a", cq[0])
            act.wait_ge(n_lo, PRE["kv_a"][1])
            squares("kv_a", lambda k: c_kv[:, k, :], lambda k: (c_free, 3))
            inverse(8, P)
            round_hi("kv_a", ckv[0])
            act.wait_ge(d_free, 2)
            nc.scalar.activation(k_rope_sq[:], k_rope[:], ACT.Square).then_inc(rope_sq, 1)
            act.wait_ge(n_lo, PRE["kv_a"][1] + 1)
            with act.Fori(0, DIFF_HEADS) as it:
                for e in range(2):
                    act.wait_ge(w_used, 2 * it + s0 + 5 + e + 1)
                    nc.scalar.activation(tmp[e][:], wide(1 - e), ACT.Square).then_inc(d_sq, 1)
                    act.wait_ge(d_tot, 2 * it + e + 1)
                    act.wait_ge(d_free, 2 * it + e + 1)
                    nc.scalar.activation(d_rms[e][:], wide(2 + e), ACT.Ln, bias=eps[:], scale=1.0 / 64).then_inc(d_ln, 1)
                    act.wait_ge(d_ln, 2 * it + e + 1)
                    nc.scalar.activation(d_rms[e][:], d_rms[e][:], ACT.Exp, scale=-0.5).then_inc(d_rs, 1)
                    act.wait_ge(d_free, 2 * it + e + 3)
                    act.dma_start(t["diff_qk"][2 * it + e], d_out[e][:]).then_inc(d_stored[e], 16)
            act.wait_ge(w_used, SLABS["diff_value"][0] + 4)
            for j in range(0, NT, 2):
                nc.scalar.activation(d_value[:, j, :], ps[:, j, :], ACT.Copy).then_inc(dv_act, 1)
            act.wait_ge(dv_act, 4)
            act.wait_ge(dv_dve, 4)
            for hd in range(DIFF_HEADS):
                act.dma_start(t["diff_v"][hd], d_value[:, :, hd * P:(hd + 1) * P]).then_inc(dv_stored, 16)
            for j in range(0, NT, 2):
                act.wait_ge(v_done, j + 1)
                nc.scalar.activation(v_value[:, j, :], ps[:, j, :], ACT.Copy).then_inc(v_act, 1)
            act.wait_ge(v_act, 4)
            act.wait_ge(v_dve, 4)
            for hd in range(MLA_HEADS):
                act.dma_start(t["mla_v"][hd], v_value[:, :, hd * P:(hd + 1) * P]).then_inc(v_stored, 16)
            for p in range(2):
                act.wait_ge(r_free, p + 1)
                nc.scalar.activation(q_rope_sq[:, p, :], q_rope[:, p, :], ACT.Square).then_inc(rope_sq, 1)
            for e in range(2):
                act.wait_ge(d_stored[e], 16 * DIFF_HEADS)

            def head_square(e):
                act.wait_ge(*((w_used, SLABS["uq_nope" if e % 2 else "ukv"][0] + 1) if e // 2 == MLA_HEADS - 1
                              else (g_done, e + 1)))
                nc.scalar.activation(tmp[e % 2][:], wide(e % 2), ACT.Square).then_inc(g_sq, 1)

            def store_parts(e):
                hd, is_q = e // 2, e % 2
                n, r0 = MLA_HEADS * (1 - is_q) + hd, ROPE * (hd % 2) if is_q else 0
                act.wait_ge(g_roped, e + 1)
                act.dma_start(t["mla_nope"][n], g_nope[e % 2][:]).then_inc(g_stored[e % 2], 16)
                act.dma_start(t["mla_rope"][n], g_rope[e % 2][r0:r0 + ROPE, :]).then_inc(g_stored[e % 2], 16)

            head_square(0)
            for e in range(2 * MLA_HEADS):
                act.wait_ge(g_tot, e + 1)
                if e >= 2:
                    act.wait_ge(g_roped, e - 1)
                step(nc.scalar.activation(g_rms[e % 2][:], wide(2 + e % 2), ACT.Ln, bias=eps[:],
                                          scale=1.0 / (P + ROPE)))
                if e:
                    store_parts(e - 1)
                if e + 1 < 2 * MLA_HEADS:
                    head_square(e + 1)
                nc.scalar.activation(g_rms[e % 2][:], g_rms[e % 2][:], ACT.Exp, scale=-0.5).then_inc(g_rs, 1)
            store_parts(2 * MLA_HEADS - 1)
            def exps(unit):
                g, q, d = unit // 4 % 2, unit % 4, unit - NT * MLA_HEADS
                act.wait_ge(a_max, unit + 1)
                if d < 0:
                    if unit >= 8:
                        act.wait_ge(a_tr, 2 * (unit - unit % 4) - 8)
                    nc.scalar.activation(prob_rows[g][q][:], wide(unit % 2), ACT.Exp, bias=mstat[:, g, 1, q:q + 1],
                                         scale=(P + ROPE) ** -0.5, accum_out=mstat[:, g, 2, q:q + 1]).then_inc(a_exp, 1)
                    return
                for m, row in enumerate((prob_rows[g][q], second[unit % 2])):
                    nc.scalar.activation(row[:], row[:], ACT.Exp, bias=e_stat[:, unit % 8, 3, m:m + 1],
                                         accum_out=e_stat[:, unit % 8, 4, m:m + 1]).then_inc(a_exp, 1)

            def round_probs(group, j):
                act.wait_ge(a_tr, 8 * group + j + 1)
                if 8 * group + j >= 2:
                    act.wait_ge(a_pv, 8 * group + j - 1)
                dst = pt[j % 2][0] if group < 2 * MLA_HEADS else pt_plain[j % 2]
                nc.scalar.activation(dst[:], ps[:, 4 + j % 2, :], ACT.Copy).then_inc(a_pthi, 1)

            def diagonal_inverses(group):
                act.wait_ge(a_inv, group + 1)
                if group:
                    act.wait_ge(a_spread, group)
                for q in range(4):
                    ins = nc.scalar.activation(diagonal[:, q, :], ident[:], ACT.Copy, scale=mstat[:, group % 2, 3, q:q + 1])
                ins.then_inc(a_diag, 1)

            def copy_head(group):
                act.wait_ge(a_pv, 8 * group + 8)
                if group:
                    act.wait_ge(o_stored, 16 * group)
                nc.scalar.activation(o_stage[:], ps[:, 6 + group % 2, :], ACT.Copy).then_inc(a_copied, 1)

            def store_head(group):
                g = group % 2
                act.wait_ge(a_out, group + 1)
                act.dma_start(t["heads_out"][group // 2][:, g * HALF:(g + 1) * HALF], o_stage[:]).then_inc(o_stored, 16)

            for q in range(4):
                exps(q)
            for e in range(2):
                act.wait_ge(g_stored[e], 32 * MLA_HEADS)
            for group in range(GROUPS):
                for n in range(4):
                    if n == 0 and group:
                        copy_head(group - 1)
                    round_probs(group, 2 * n)
                    round_probs(group, 2 * n + 1)
                    if group + 1 < GROUPS:
                        exps(4 * (group + 1) + n)
                    if n == 1:
                        diagonal_inverses(group)
                    if n == 1 and group:
                        store_head(group - 1)
                    if n == 3 and group == GROUPS - 2:
                        act.wait_ge(a_pv, 8 * (GROUPS - 2))
                        act.wait_ge(o_stored, 16 * (GROUPS - 2))
                        for k in range(KT - 1):
                            act.dma_start(o_in[:, k, :], t["heads_out"][k]).then_inc(o_landed, 16)
            copy_head(GROUPS - 1)
            store_head(GROUPS - 1)

            def out_hi(k):
                if k >= MLA_HEADS:
                    act.wait_ge(s_scaled, k - MLA_HEADS + 1)
                nc.scalar.activation(o_all[0][:, k, :], o_in[:, k, :], ACT.Copy).then_inc(s_hi, 1)

            def out_square(n):
                if n >= 2:
                    act.wait_ge(s_tot, n - 1)
                if n == DIFF_HEADS - 1:
                    act.wait_ge(o_last, 16)
                nc.scalar.activation(tmp[n % 2][:], o_in[:, MLA_HEADS + n, :], ACT.Square).then_inc(s_sq, 1)

            def out_inverse(n):
                act.wait_ge(s_tot, n + 1)
                if n >= 2:
                    act.wait_ge(s_scaled, n - 1)
                step(nc.scalar.activation(o_rms[n % 2][:], wide(2 + n % 2), ACT.Ln, bias=eps[:], scale=1.0 / P))
                nc.scalar.activation(o_rms[n % 2][:], o_rms[n % 2][:], ACT.Exp, scale=-0.5).then_inc(s_rs, 1)

            act.wait_ge(o_landed, 16 * (KT - 1))
            act.wait_ge(a_probs, 4 * NT)
            act.wait_ge(a_pv, 8 * GROUPS)
            out_hi(0)
            out_square(0)
            out_hi(1)
            out_square(1)
            act.wait_ge(o_stored, 16 * GROUPS)
            act.dma_start(o_in[:, KT - 1, :], t["heads_out"][KT - 1]).then_inc(o_last, 16)
            out_hi(2)
            out_inverse(0)
            out_hi(3)
            out_square(2)
            out_inverse(1)
            out_hi(4)
            out_square(3)
            out_inverse(2)
            out_hi(5)
            out_inverse(3)
            out_hi(6)
            out_hi(7)
            squares("mlp_2", lambda k: x[:, k, :], lambda k: (x_added, 3 * KT + k + 1))
            inverse(9)
            round_hi("mlp_2", normed[0])
            s0 = SLABS["mlp_2"][0]
            with act.Fori(0, FF2_TILES // CHUNK) as c:
                for j in range(CHUNK):
                    act.wait_ge(w_used, 8 * c + s0 + j + 1)
                    act.wait_ge(u_lo, 4 * c + j + 1)
                    nc.scalar.activation(tmp[j % 2][:], wide(j), ACT.Relu).then_inc(u_relu, 1)
                    act.wait_ge(u_sq, 4 * c + j + 1)
                    nc.scalar.activation(hidden[0][:, j, :], tmp[j % 2][:], ACT.Copy).then_inc(u_hi, 1)
            for m in range(KT):
                act.wait_ge(u_added, 8 * (FF2_TILES // CHUNK) + m + 1)
                act.dma_start(out[:, m, :], x[:, m, :]).then_inc(stored, 16)
            act.wait_ge(stored, 16 * KT)
        @block.vector
        def _(dve):
            step = Chain(dve, dve_step)
            tt, ts, stt = nc.vector.tensor_tensor, nc.vector.tensor_scalar, nc.vector.scalar_tensor_tensor

            def add_square(post, k):
                dve.wait_ge(n_post_sq, KT * post + k + 1)
                if k >= 2:
                    dve.wait_ge(n_acc, 7 * post + k - 1)
                tt(acc[:], acc[:], tmp[k % 2][:], ALU.add).then_inc(n_acc, 1)

            def scaled(r, name, src, dst):
                tiles, before = PRE[name]

                def rest(k):
                    dve.wait_ge(n_hi, before + k + 1)
                    tt(dst[1][:, k, :], tmp[k % 2][:], dst[0][:, k, :].bitcast(F32), ALU.subtract).then_inc(n_lo, 1)

                dve.wait_ge(n_rs, r + 1)
                for k in range(tiles):
                    if k >= 2:
                        dve.wait_ge(n_lo, before + k - 1)
                    stt(tmp[k % 2][:], src[:, k, :], col(name, k), acc[:], ALU.mult, ALU.mult).then_inc(n_tmp, 1)
                    if k:
                        rest(k - 1)
                rest(tiles - 1)

            def residual(r, gain):
                dve.wait_ge(n_rs, r + 1)
                for k in range(KT):
                    step(stt(y[:, k, :], y[:, k, :], col(gain, k), acc[:], ALU.mult, ALU.mult))
                    tt(x[:, k, :], x[:, k, :], y[:, k, :], ALU.add).then_inc(x_added, 1)

            nc.vector.memset(eps[:], EPS)
            nc.vector.memset(ones[:], 1.0).then_inc(dve_consts, 1)
            dve.wait_ge(consts_in, 16 * N_CONSTS)
            nc.vector.tensor_copy(ident16[:], ident[:]).then_inc(dve_consts, 1)
            dve.wait_ge(dve_consts, 2)
            scaled(0, "mix_pre", x_in, h1)
            for g in range(POOL_GROUPS):
                step(ts(col("pool_scale", g), col("pool_scale", g), 1.0 / (2 << g), None, ALU.mult))
            def in_lo(n, pair_of, src):
                dve.wait_ge(in_hi, n + 1)
                tt(pair_of[1], src, pair_of[0].bitcast(F32), ALU.subtract).then_inc(in_free, 1)

            in_lo(0, [part[:, 0, :] for part in qidx], wide(1))
            in_lo(1, [part[:] for part in kidx], kidx_t[:])
            dve.wait_ge(turn_done, 1)
            step(nc.vector.tensor_copy(wi, ps[:, 4, :].rearrange("p (j h) -> p j h", j=NT)[:, :, 0:IDX_HEADS]))
            in_lo(2, [part[:, 1, :] for part in qidx], wide(0))
            unit = 0
            for i in reversed(range(2, NT)):
                sc = score[:, score_at[i]:score_at[i] + (i + 1) * P]
                for hd in range(IDX_HEADS):
                    dve.wait_ge(idx_relu, unit + 1)
                    part, w = tmp[unit % 2][:, 0:(i + 1) * P], wi[:, i, hd:hd + 1]
                    if hd == 0:
                        ins = ts(sc, part, w, None, ALU.mult)
                    else:
                        dve.wait_ge(idx_added, unit)
                        ins = stt(sc, part, w, sc, ALU.mult, ALU.add)
                    ins.then_inc(idx_added, 1)
                    unit += 1
                dve.wait_ge(idx_added, unit)
                step(tt(sc[:, i * P:(i + 1) * P], sc[:, i * P:(i + 1) * P], tri[:], ALU.add))
            in_lo(3, [part[:] for part in key], wide(0))
            for both in ((7, 2), (6, 3), (5, 4)):
                if both == (5, 4):
                    for i, g in enumerate(POOL_ORDER):
                        dve.wait_ge(mix_hi, i + 1)
                        tt(mixed[1][:, g, :], mixed_sum[:, g, :], mixed[0][:, g, :].bitcast(F32),
                           ALU.subtract).then_inc(mix_free, 1)
                scs = [score[:, score_at[i]:score_at[i] + (i + 1) * P] for i in both]
                for _ in range(ROUNDS):
                    found = step.n
                    for e, sc in enumerate(scs):
                        if step.n > 2:
                            dve.wait_ge(dve_step, step.n - 1)
                        step.n += 1
                        nc.vector.max(top8[:, e, :], sc).then_inc(dve_step, 1)
                    for e, sc in enumerate(scs):
                        dve.wait_ge(dve_step, found + e + 1)
                        step.n += 1
                        nc.vector.match_replace(sc, top8[:, e, :], sc, TAKEN).then_inc(dve_step, 1)
            dve.wait_ge(dve_step, step.n)
            for i in range(2, NT):
                ts(mask[:, mask_at[i]:mask_at[i] + (i + 1) * P], score[:, score_at[i]:score_at[i] + (i + 1) * P],
                   TAKEN, NEG, ALU.not_equal, ALU.mult)
            nc.vector.memset(mask[:, mask_at[1]:mask_at[1] + P], 0.0)
            nc.vector.tensor_copy(mask[:, mask_at[1] + P:mask_at[1] + 2 * P], tri[:])
            nc.vector.tensor_copy(mask[:, 0:P], tri[:]).then_inc(masks_ready, 1)
            dve.wait_ge(bias_done, 1)
            dve.wait_ge(masks_ready, 1)
            def rest_query(group):
                i, g = group // 2, group % 2
                dve.wait_ge(qt_hi, group + 1)
                tt(q_tile[g][1][:], query[:, 4 * g:4 * g + 4, i * P:(i + 1) * P], q_tile[g][0][:].bitcast(F32),
                   ALU.subtract).then_inc(qt_lo, 1)

            def mix_maxima(unit):
                group, q = unit // 4, unit % 4
                i, hd = group // 2, 4 * (group % 2) + q
                row, n = mix_rows[group % 2][q], (i + 1) * P
                late = max(0, i - 1) * P
                if q == 0 and group >= 2:
                    dve.wait_ge(tr_done, tiles_before(group - 1))
                dve.wait_ge(qk_done, unit + 1)
                if late:
                    nc.vector.tensor_tensor_reduce(row[:, 0:late], wide(unit % 2)[:, 0:late],
                                                   bias[:, hd, 0:1].broadcast_to([P, late]), 1.0, TAKEN, ALU.add,
                                                   ALU.max, mix_stat(unit, 1))
                nc.vector.tensor_tensor_reduce(row[:, late:n], wide(unit % 2)[:, late:n],
                                               bias[:, hd, 2 * P - (n - late):2 * P], 1.0, TAKEN, ALU.add, ALU.max,
                                               mix_stat(unit, 0)).then_inc(logits_ready, 1)
                dve.wait_ge(logits_ready, unit + 1)
                if late:
                    step(tt(mix_stat(unit, 0), mix_stat(unit, 0), mix_stat(unit, 1), ALU.max))
                ts(mix_stat(unit, 3), mix_stat(unit, 0), -1.0, None, ALU.mult).then_inc(nmax_ready, 1)

            def mix_inverse(unit):
                dve.wait_ge(exp_done, unit + 1)
                nc.vector.reciprocal(mix_stat(unit, 5), mix_stat(unit, 4)).then_inc(inv_ready, 1)
                group, q = unit // 4, unit % 4
                if q >= BY_POOL:
                    row = mix_rows[group % 2][q][:, 0:(group // 2 + 1) * P]
                    dve.wait_ge(inv_ready, unit + 1)
                    ts(row, row, mix_stat(unit, 5), None, ALU.mult).then_inc(last_ready, 1)

            def mix_out_lo(group):
                i, g = group // 2, group % 2
                dve.wait_ge(o_hi, group + 1)
                tt(att[1][:, 4 * g:4 * g + 4, i * P:(i + 1) * P], ps[:, 6 + g, :].rearrange("p (h q) -> p h q", h=4),
                   att[0][:, 4 * g:4 * g + 4, i * P:(i + 1) * P].bitcast(F32), ALU.subtract).then_inc(o_lo, 1)

            for group in range(2):
                rest_query(group)
            for q in range(4):
                mix_maxima(q)
                mix_inverse(q)
            for group in range(2 * NT):
                for n in range(4):
                    unit = 4 * (group + 1) + n
                    more = group + 1 < 2 * NT
                    if more:
                        mix_maxima(unit)
                    if n == 0 and group:
                        mix_out_lo(group - 1)
                    if more and n:
                        mix_inverse(unit - 1)
                    if more and n == 3:
                        mix_inverse(unit)
                    if n == 1 and group + 2 < 2 * NT:
                        rest_query(group + 2)
            mix_out_lo(2 * NT - 1)
            dve.sem_inc(merge_free, 2)
            for k in range(KT):
                pool_part, pool_gate, attn_gate = (gated[k % 2][:, n, :] for n in range(3))
                dve.wait_ge(gates_in[k % 2], 48 * (k // 2 + 1))
                tt(pool_part, pool_part, pool_gate, ALU.mult)
                dve.wait_ge(w_used, SLABS["proj_attn"][0] + k + 1)
                step(tt(attn_gate, wide(k % 2), attn_gate, ALU.mult))
                step(tt(pool_part, pool_part, attn_gate, ALU.add))
                step(nc.vector.tensor_copy(merged[0][:, k, :], pool_part))
                tt(merged[1][:, k, :], pool_part, merged[0][:, k, :].bitcast(F32), ALU.subtract).then_inc(merge_free, 1)
            for k in range(1, KT):
                add_square(0, k)
                if k == 4:
                    dve.wait_ge(mem_rs, 1)
                    for e in range(KT):
                        stt(mem_in[:, e, :], mem_in[:, e, :], col("mem_kv", e), mem_rms[:], ALU.mult,
                            ALU.mult).then_inc(mem_scaled, 1)
            dve.wait_ge(mem_hi, 1)
            tt(memn[1][:], mem_in[:], memn[0][:].bitcast(F32), ALU.subtract).then_inc(mem_lo, 1)
            dve.wait_ge(x_landed, 16)
            dve.wait_ge(y_free, 2 + KT)
            residual(1, "mix_post")
            dve.wait_ge(mkv_hi, 1)
            tt(kmem[1][:], wide(0).rearrange("p (h m) -> p h m", h=MEM_HEADS), kmem[0][:].bitcast(F32),
               ALU.subtract).then_inc(mkv_lo, 1)
            scaled(2, "mem_pre", x, normed)
            dve.sem_inc(mq_lo, 2)
            for n in range(MEM_HEADS):
                dve.wait_ge(mq_hi, n + 1)
                stt(qm[1][:, n, :], wide(n % 2), P ** -0.5, qm[0][:, n, :].bitcast(F32), ALU.mult,
                    ALU.subtract).then_inc(mq_lo, 1)
            def mem_maxima(n):
                biggest, minus = (mstat[:, n % 2, e, :] for e in range(2))
                dve.wait_ge(m_qk, n + 1)
                step(nc.vector.tensor_reduce(biggest, wide(n % 2).rearrange("p (q m) -> p q m", q=4), AX.X, ALU.max))
                ts(minus, biggest, -1.0, None, ALU.mult).then_inc(m_max, 1)

            def mem_normalise(n):
                total, inv = (mstat[:, n % 2, e, :] for e in range(2, 4))
                dve.wait_ge(m_exp, 4 * (n + 1))
                step(nc.vector.reciprocal(inv, total))
                tt(mprobs[:, n % 2], mprobs[:, n % 2], inv.unsqueeze(2).broadcast_to([P, 4, M]),
                   ALU.mult).then_inc(m_probs, 1)

            def mem_out_lo(n):
                dve.wait_ge(m_ohi, n + 1)
                t0 = n % 2 * HALF
                tt(om[1][:, n // 2, t0:t0 + HALF], ps[:, 6 + n % 2, :], om[0][:, n // 2, t0:t0 + HALF].bitcast(F32),
                   ALU.subtract).then_inc(m_olo, 1)

            mem_maxima(0)
            mem_normalise(0)
            for n in range(2 * MEM_HEADS):
                if n + 1 < 2 * MEM_HEADS:
                    mem_maxima(n + 1)
                if n:
                    mem_out_lo(n - 1)
                if n + 1 < 2 * MEM_HEADS:
                    mem_normalise(n + 1)
            mem_out_lo(2 * MEM_HEADS - 1)
            for k in range(1, KT):
                add_square(1, k)
            dve.wait_ge(y_free, 2 + 2 * KT)
            residual(3, "mem_post")
            scaled(4, "ffn_pre", x, normed)
            dve.sem_inc(f_lo, 2)
            nc.vector.memset(y[:], 0.0).then_inc(y_zero, 1)
            dve.wait_ge(y_zero, 1)
            dve.sem_inc(f_added, 8)
            s0 = SLABS["ffn"][0]

            def ffn_hidden(c, tiles, down_before, last=False):
                for j in range(tiles):
                    part = tmp[j % 2]
                    dve.wait_ge(w_used, 12 * c + s0 + 2 * j + 2)
                    dve.wait_ge(f_silu, 4 * c + j + 1)
                    tt(part[:], part[:], wide(2 * (j % 2) + 1), ALU.mult).then_inc(f_mul, 1)
                    dve.wait_ge(f_hi, 4 * c + j + 1)
                    tt(hidden[1][:, j, :], part[:], hidden[0][:, j, :].bitcast(F32), ALU.subtract).then_inc(f_lo, 1)
                per = 8 // tiles
                for m in range(KT):
                    if m % per == per - 1:
                        dve.wait_ge(w_used, 12 * c + s0 + 2 * tiles + m // per + 1)
                    else:
                        dve.wait_ge(first_half, down_before + m - m // per + 1)
                    tt(y[:, m, :], y[:, m, :], wide(m % 4), ALU.add).then_inc(f_added, 1)
                    if last and m >= 2:
                        add_square(2, m - 1)

            with dve.Fori(0, FF_TILES // CHUNK) as c:
                ffn_hidden(c, CHUNK, 4 * c + 8)
            ffn_hidden(FF_TILES // CHUNK, FF_TILES % CHUNK, 4 * (FF_TILES // CHUNK) + 8, True)
            add_square(2, KT - 1)
            residual(5, "ffn_post")
            lam = cols[:, COLS["lambda"][0]:COLS["lambda"][0] + 256].rearrange("p (v n) -> p v n", v=4)
            ts(col("diff_q"), col("diff_q"), 64 ** -0.5, None, ALU.mult)
            ts(col("diff_out"), col("diff_out"), 1.0 - LAM_INIT, None, ALU.mult)
            tt(lam[:, 0, :], lam[:, 0, :], lam[:, 1, :], ALU.mult)
            step(tt(lam[:, 2, :], lam[:, 2, :], lam[:, 3, :], ALU.mult))
            nc.vector.tensor_reduce(lam_ab[:, 0:1], lam[:, 0, :], AX.X, ALU.add)
            nc.vector.tensor_reduce(lam_ab[:, 1:2], lam[:, 2, :], AX.X, ALU.add).then_inc(lam_sum, 1)
            scaled(6, "attn_2", x, normed)
            dve.wait_ge(lam_exp, 1)
            step(tt(minus_lam, lam_ab[:, 1:2], lam_ab[:, 0:1], ALU.subtract))
            step(ts(minus_lam, minus_lam, -LAM_INIT, None, ALU.add))
            s0 = SLABS["in_2"][0]
            dve.wait_ge(tables_in, 48)
            dve.wait_ge(w_used, s0 + 4)
            tt(k_rope[:], wide(1), cos[:], ALU.mult).then_inc(d_free, 1)
            scaled(7, "q_a", c_q, cq)
            dve.wait_ge(w_used, s0 + 5)
            dve.wait_ge(n_lo, PRE["kv_a"][1])
            dve.wait_ge(n_sq, PRE["kv_a"][1] + 1)
            step(tt(tmp[1][:], wide(0), sin[:], ALU.mult))
            tt(k_rope[:], k_rope[:], tmp[1][:], ALU.add).then_inc(d_free, 1)
            scaled(8, "kv_a", c_kv, ckv)
            for part, gain in enumerate(("diff_q", "diff_k")):
                with dve.Fori(2 * part, 2 * part + 2) as it:
                    for e in range(2):
                        dve.wait_ge(d_rs, 2 * it + e + 1)
                        stt(d_out[e][:], wide(1 - e), col(gain), d_rms[e][:], ALU.mult, ALU.mult).then_inc(d_free, 1)
                    for e in range(2):
                        dve.wait_ge(d_stored[e], 16 * it + 16)
            dve.wait_ge(w_used, SLABS["diff_value"][0] + 4)
            for j in range(1, NT, 2):
                nc.vector.tensor_copy(d_value[:, j, :], ps[:, j, :]).then_inc(dv_dve, 1)
            for p in range(2):
                dve.wait_ge(r_done, 2 * p + 1)
                tt(q_rope[:, p, :], wide(2 * p), cos[:], ALU.mult)
                dve.wait_ge(*((w_used, SLABS["uq_rope"][0] + 1) if p else (r_done, 2)))
                step(tt(turned[:], wide(2 * p + 1), sin[:], ALU.mult))
                tt(q_rope[:, p, :], q_rope[:, p, :], turned[:], ALU.add).then_inc(r_free, 1)
                dve.wait_ge(r_free, p + 1)
            for j in range(1, NT, 2):
                dve.wait_ge(v_done, j + 1)
                nc.vector.tensor_copy(v_value[:, j, :], ps[:, j, :]).then_inc(v_dve, 1)
            for e in range(2 * MLA_HEADS):
                hd, is_q = e // 2, e % 2
                dve.wait_ge(g_rs, e + 1)
                if e >= 2:
                    dve.wait_ge(g_stored[e % 2], 32 * (e // 2))
                which = "mla_q" if is_q else "mla_k"
                stt(g_nope[e % 2][:], wide(e % 2), col(which + "_nope"), g_rms[e % 2][:], ALU.mult,
                    ALU.mult).then_inc(g_free, 1)
                r0 = ROPE * (hd % 2) if is_q else 0
                rope = q_rope[r0:r0 + ROPE, hd // 2, :] if is_q else k_rope[0:ROPE, :]
                stt(g_rope[e % 2][r0:r0 + ROPE, :], rope, col(which + "_rope")[r0:r0 + ROPE, :],
                    g_rms[e % 2][r0:r0 + ROPE, :], ALU.mult, ALU.mult).then_inc(g_roped, 1)
            def maxima(unit):
                g, q, d = unit // 4 % 2, unit % 4, unit - NT * MLA_HEADS
                if d < 0:
                    dve.wait_ge(a_qk, unit + 1)
                    step(nc.vector.tensor_reduce(mstat[:, g, 0, q:q + 1], wide(unit % 2), AX.X, ALU.max))
                    ts(mstat[:, g, 1, q:q + 1], mstat[:, g, 0, q:q + 1], -(P + ROPE) ** -0.5, None, ALU.mult).then_inc(a_max, 1)
                    return
                i, bias = unit % NT, e_bias[:, d // NT % 2, :]
                if i == 0:
                    dve.wait_ge(bias_2_in[d // NT % 2], 16 * (d // NT // 2) + 16)
                near0, near1 = max(0, i - 1) * P, min(NT, i + 2) * P
                b0 = P if i == 0 else 0
                stats = e_stat[:, unit % 8]
                dve.wait_ge(a_tr, 2 * (unit - unit % 4) - 8)
                if d >= 2:
                    dve.wait_ge(a_probs, d - 1)
                for m, row in enumerate((prob_rows[g][q], second[unit % 2])):
                    dve.wait_ge(a_qk, NT * MLA_HEADS + 2 * d + m + 1)
                    for kind, lo, hi, b in ((0, 0, near0, bias[:, 0:1].broadcast_to([P, near0])),
                                            (2, near1, S, bias[:, 3 * P - 1:3 * P].broadcast_to([P, S - near1])),
                                            (1, near0, near1, bias[:, b0:b0 + near1 - near0])):
                        if lo < hi:
                            ins = nc.vector.tensor_tensor_reduce(row[:, lo:hi], wide(m)[:, lo:hi], b, 1.0, TAKEN,
                                                                 ALU.add, ALU.max, stats[:, kind, m:m + 1])
                    ins.then_inc(e_red, 1)
                dve.wait_ge(e_red, 2 * d + 2)
                for kind, there in ((0, near0 > 0), (2, near1 < S)):
                    if there:
                        step(tt(stats[:, 1, :], stats[:, 1, :], stats[:, kind, :], ALU.max))
                ts(stats[:, 3, :], stats[:, 1, :], -1.0, None, ALU.mult).then_inc(a_max, 1)

            def difference(unit):
                g, q, d = unit // 4 % 2, unit % 4, unit - NT * MLA_HEADS
                row, other = prob_rows[g][q], second[unit % 2]
                sums, factor = e_stat[:, unit % 8, 4, :], e_stat[:, unit % 8, 5, :]
                dve.wait_ge(a_exp, NT * MLA_HEADS + 2 * d + 2)
                step(nc.vector.reciprocal(factor[:, 0:1], sums[:, 1:2]))
                step(stt(factor[:, 1:2], factor[:, 0:1], minus_lam, sums[:, 0:1], ALU.mult, ALU.mult))
                stt(row[:], other[:], factor[:, 1:2], row[:], ALU.mult, ALU.add).then_inc(a_probs, 1)

            def inverse_sums(group):
                g, first = group % 2, 4 * group
                if group < 2 * MLA_HEADS:
                    dve.wait_ge(a_exp, first + 4)
                    sums = mstat[:, g, 2, :]
                else:
                    sums = e_stat[:, 4 * g:4 * g + 4, 4, 0]
                nc.vector.reciprocal(mstat[:, g, 3, :], sums).then_inc(a_inv, 1)

            def head_out(group):
                dve.wait_ge(a_spread, group + 1)
                dve.wait_ge(a_copied, group + 1)
                tt(o_stage[:], o_stage[:], ps[:, 7 - group % 2, :], ALU.mult).then_inc(a_out, 1)

            def rest_probs(group, j):
                dve.wait_ge(a_pthi, 8 * group + j + 1)
                tt(pt[j % 2][1][:], ps[:, 4 + j % 2, :], pt[j % 2][0][:].bitcast(F32), ALU.subtract).then_inc(a_ptlo, 1)

            first_diff = NT * MLA_HEADS
            for e in range(2):
                dve.wait_ge(g_stored[e], 32 * MLA_HEADS)
            for q in range(4):
                maxima(q)
            for group in range(GROUPS):
                for n in range(4):
                    unit = 4 * (group + 1) + n
                    late = first_diff < unit <= 4 * GROUPS
                    if late and n == 0:
                        difference(unit - 1)
                    if group + 1 < GROUPS:
                        maxima(unit)
                    if n == 0 and group:
                        head_out(group - 1)
                    if group < 2 * MLA_HEADS:
                        rest_probs(group, 2 * n)
                        rest_probs(group, 2 * n + 1)
                    if n == 0:
                        inverse_sums(group)
                    if late and n:
                        difference(unit - 1)
            head_out(GROUPS - 1)
            def out_scaled(n):
                k = MLA_HEADS + n
                dve.wait_ge(s_rs, n + 1)
                stt(o_in[:, k, :], o_in[:, k, :], col("diff_out"), o_rms[n % 2][:], ALU.mult, ALU.mult).then_inc(s_scaled, 1)

            def out_lo(k):
                dve.wait_ge(s_hi, k + 1)
                tt(o_all[1][:, k, :], o_in[:, k, :], o_all[0][:, k, :].bitcast(F32), ALU.subtract).then_inc(s_lo, 1)

            for k in range(MLA_HEADS):
                out_lo(k)
            out_scaled(0)
            for n in range(1, DIFF_HEADS):
                out_scaled(n)
                out_lo(MLA_HEADS + n - 1)
            out_lo(KT - 1)
            for k in range(KT):
                dve.wait_ge(w_used, SLABS["out_2"][0] + k + 1)
                tt(x[:, k, :], x[:, k, :], wide(k % 2), ALU.add).then_inc(x_added, 1)
            scaled(9, "mlp_2", x, normed)
            dve.sem_inc(u_lo, 2)
            dve.sem_inc(u_added, 8)
            s0 = SLABS["mlp_2"][0]
            down0 = 4 + 4 + 4 * (FF_TILES // CHUNK) + 6
            with dve.Fori(0, FF2_TILES // CHUNK) as c:
                for j in range(CHUNK):
                    part = tmp[j % 2]
                    dve.wait_ge(u_relu, 4 * c + j + 1)
                    tt(part[:], part[:], part[:], ALU.mult).then_inc(u_sq, 1)
                    dve.wait_ge(u_hi, 4 * c + j + 1)
                    tt(hidden[1][:, j, :], part[:], hidden[0][:, j, :].bitcast(F32), ALU.subtract).then_inc(u_lo, 1)
                for m in range(KT):
                    if m % 2:
                        dve.wait_ge(w_used, 8 * c + s0 + 4 + m // 2 + 1)
                    else:
                        dve.wait_ge(first_half, 4 * c + down0 + m // 2 + 1)
                    tt(x[:, m, :], x[:, m, :], wide(m % 4), ALU.add).then_inc(u_added, 1)


def slabs_of(w, kt):
    n = w.shape[1] // P
    w = w.reshape(kt, P, n, P).transpose(2, 0, 1, 3).reshape(n * kt // 8, 8, P, P)
    return w.transpose(0, 2, 1, 3).reshape(-1, P, 1024)


def moving_slabs(w):
    return w.reshape(4, 2, P, 512).transpose(0, 2, 1, 3).reshape(4, P, 1024)


def pack_weights(a):
    out = np.zeros((N_SLABS, P, 1024), np.float32)

    def put(name, slabs):
        first, n = SLABS[name]
        assert slabs.shape[0] == n, (name, slabs.shape)
        out[first:first + n] = slabs

    w = a["w_in"]
    pool_w, q_w, k_w, v_w, qi_w, ki_w, wi_w, gp_w, ga_w = np.split(
        w, np.cumsum((512, 1024, 128, 128, 256, 64, 4, 1024)), axis=1)
    pad = np.zeros((D, P - IDX_DIM - IDX_HEADS), np.float32)
    put("mix_in", slabs_of(np.concatenate([ki_w, wi_w, pad, qi_w, v_w, k_w, pool_w], axis=1), KT))
    gates = slabs_of(np.concatenate([gp_w, ga_w], axis=1), KT)
    put("gates", gates[:SLABS["gates"][1]])
    put("last_gates", gates[SLABS["gates"][1]:])
    first = SLABS["pool_mix"][0]
    for g in range(POOL_GROUPS):
        out[first, :, g * P:(g + 1) * P] = a["pool_w"][g]
    put("proj_pool", slabs_of(a["w_proj_pool"], 4))
    put("query", slabs_of(q_w, KT))
    put("proj_attn", slabs_of(a["w_proj_attn"], KT))
    put("mix_out", slabs_of(a["w_out"], KT))
    w = a["w_kv_mem"]
    put("mem_key", slabs_of(w[:, :MEM_HEADS * P], KT))
    put("mem_value", moving_slabs(w[:, MEM_HEADS * P:]))
    put("mem_query", slabs_of(a["w_q_mem"], KT))
    put("mem_out", slabs_of(a["w_o_mem"], 4))
    gate, up = slabs_of(a["w_gate_up"][:, :FF], KT), slabs_of(a["w_gate_up"][:, FF:], KT)
    parts = []
    for c in range(0, FF_TILES, CHUNK):
        n = min(CHUNK, FF_TILES - c)
        parts.append(np.stack([gate[c:c + n], up[c:c + n]], axis=1).reshape(2 * n, P, 1024))
        parts.append(slabs_of(a["w_down"][c * P:(c + n) * P], n))
    put("ffn", np.concatenate(parts))
    w = a["w_in_2"][0]
    cq, ckv, kr, dq, dk, dv = np.split(w, np.cumsum((256, 128, 64, 512, 512)), axis=1)
    kr2 = np.roll(kr, 32, axis=1)
    put("in_2", slabs_of(np.concatenate([cq, ckv, kr, kr, kr2, kr2, dq, dk], axis=1), KT))
    put("diff_value", moving_slabs(dv))
    w = a["w_ukv_2"][0].reshape(P, MLA_HEADS, 2, P)
    put("ukv", np.concatenate([w[:, :, 0].reshape(P, 512), w[:, :, 1].reshape(P, 512)], axis=1)[None])
    w = a["w_uq_2"][0].reshape(2 * P, MLA_HEADS, P + ROPE)
    rope = w[:, :, P:]
    turned = np.roll(rope, 32, axis=2)
    order = [v[:, 2 * p:2 * p + 2].reshape(2 * P, P) for p in range(2) for v in (rope, turned)]
    put("uq_rope", slabs_of(np.concatenate(order, axis=1), 2))
    put("uq_nope", slabs_of(w[:, :, :P].reshape(2 * P, 512), 2))
    put("out_2", slabs_of(a["w_out_2"][0], KT))
    up = slabs_of(a["w_up_2"][0], KT)
    parts = []
    for c in range(0, FF2_TILES, CHUNK):
        parts += [up[c:c + CHUNK], slabs_of(a["w_down_2"][0][c * P:(c + CHUNK) * P], CHUNK)]
    put("mlp_2", np.concatenate(parts))
    return out


def pack_cols(a):
    out = np.zeros((P, N_COLS), np.float32)

    def put(name, v):
        first, n = COLS[name]
        out[:, first:first + n] = v.reshape(n, P).T

    for name, key in (("mix_pre", "norm_mix_pre"), ("mix_post", "norm_mix_post"), ("pool_scale", "pool_scale"),
                      ("mem_pre", "norm_mem_pre"), ("mem_kv", "norm_mem_kv"), ("mem_post", "norm_mem_post"),
                      ("ffn_pre", "norm_ffn_pre"), ("ffn_post", "norm_ffn_post"), ("attn_2", "attn_norm_w_2"),
                      ("q_a", "q_a_norm_w_2"), ("kv_a", "kv_a_norm_w_2"), ("diff_out", "diff_out_norm_w_2"),
                      ("mlp_2", "mlp_norm_w_2")):
        put(name, a[key])
    for name, key in (("mla_q", "mla_q_norm_w_2"), ("mla_k", "mla_k_norm_w_2")):
        put(name + "_nope", a[key][0, :P])
        put(name + "_rope", np.tile(a[key][0, P:], 2))
    put("diff_q", np.tile(a["diff_q_norm_w_2"][0], 2))
    put("diff_k", np.tile(a["diff_k_norm_w_2"][0], 2))
    first = COLS["lambda"][0]
    for n, key in enumerate(("lambda_q1_2", "lambda_k1_2", "lambda_q2_2", "lambda_k2_2")):
        out[:, first + 64 * n:first + 64 * n + 64] = a[key]
    return out


def features_first(v):
    return np.ascontiguousarray(v.T.reshape(-1, P, v.shape[0]).transpose(1, 0, 2))


def bucket_causal(dist):
    n = np.maximum(dist, 0)
    large = 16 + (np.log(np.maximum(n, 1).astype(np.float32) / np.float32(16)) / np.float32(np.log(8.0))
                  * np.float32(16)).astype(np.int32)
    return np.where(n < 16, n, np.minimum(large, 31))


def bucket_both_ways(rel):
    n = np.abs(rel)
    large = 8 + (np.log(np.maximum(n, 1).astype(np.float32) / np.float32(8)) / np.float32(np.log(16.0))
                 * np.float32(8)).astype(np.int32)
    return np.where(rel > 0, 16, 0) + np.where(n < 8, n, np.minimum(large, 15))


def constants():
    c = {"c_ident": np.eye(P, dtype=np.float32)}
    c["c_flip"] = c["c_ident"][::-1].copy()
    c["c_tri"] = np.where(np.arange(P)[None, :] > np.arange(P)[:, None], np.float32(NEG), np.float32(0))
    fix = np.ones((POOL_GROUPS, 16), np.float32)
    for g in range(POOL_GROUPS):
        n = np.arange(1, 17)
        fix[g] = (2 << g) / np.minimum(n, 2 << g)
    c["c_pool_fix"] = np.broadcast_to(fix, (P, POOL_GROUPS, 16)).copy()
    dist = 255 - np.arange(384)
    c["c_onehot"] = (bucket_causal(dist)[None, :] == np.arange(BUCKETS)[:, None]).astype(np.float32)
    rel = np.arange(512) - 255
    c["c_onehot_2"] = (bucket_both_ways(rel)[None, :] == np.arange(BUCKETS)[:, None]).astype(np.float32)
    inv = (10000.0 ** (-np.arange(0, ROPE, 2) / ROPE)).astype(np.float32)
    ang = (np.arange(S, dtype=np.float32)[None, :] * inv[:, None]).astype(np.float64)
    c["c_cos"] = np.tile(np.cos(ang), (4, 1)).astype(np.float32)
    c["c_sin"] = np.concatenate([-np.sin(ang), np.sin(ang)] * 2).astype(np.float32)
    halves = np.zeros((P, 3, P), np.float32)
    halves[:64, 0, :64] = halves[64:, 0, 64:] = 1
    halves[:64, 1] = halves[64:, 2] = 1
    c["c_halves"] = halves
    return c


N_CONSTS = 8
SCRATCH = {"bias_rows": (HEADS, 384), "gates": (3 * KT, P, S), "bias_rows_2": (DIFF_HEADS, 512),
           "bias_tiles_2": (DIFF_HEADS, P, 3 * P),
           "diff_qk": (2 * DIFF_HEADS, P, S), "diff_v": (DIFF_HEADS, P, NT, P),
           "mla_nope": (2 * MLA_HEADS, P, S), "mla_rope": (2 * MLA_HEADS, ROPE, S), "mla_v": (MLA_HEADS, P, NT, P),
           "heads_out": (KT, P, S)}


def arrays_of(inputs):
    a = {k: np.asarray(v) for k, v in inputs.items()}
    out = {"weights": pack_weights(a), "cols": pack_cols(a), "x": features_first(a["x"][0]),
           "mem": features_first(a["mem"][0]), "rel_bias_table": a["rel_bias_table"],
           "rel_bias_2": a["rel_bias_2"]}
    return {**out, **constants()}


def kernel(**inputs):
    from concourse import bacc
    from concourse.bass_utils import run_bass_kernel_spmd

    nc = bacc.Bacc("TRN2", target_bir_lowering=False, num_devices=1)
    arrays = arrays_of(inputs)
    t = {name: nc.dram_tensor(f"{name}_dram", a.shape, mybir.dt.from_np(a.dtype), kind="ExternalInput").ap()
         for name, a in arrays.items()}
    t["out"] = nc.dram_tensor("out_dram", (P, KT, S), F32, kind="ExternalOutput").ap()
    for name, shape in SCRATCH.items():
        t[name] = nc.dram_tensor(f"{name}_scratch", shape, F32, kind="Internal").ap()
    program(nc, t)
    r = run_bass_kernel_spmd(nc, [{f"{name}_dram": a for name, a in arrays.items()}], core_ids=[0])
    got = r.results[0]["out_dram"]
    return np.ascontiguousarray(got.transpose(2, 1, 0).reshape(1, S, D))
```
